# Optimizing a Trainium2 kernel written in Bass

```python
import math
import jax, jax.numpy as jnp
from jax import lax
import numpy as np

D_MODEL = 1024
BATCH = 1
SEQ = 256
DEPTH = 2

CONV_WIDTH = D_MODEL // 2
CONV_K = 3
N_HEADS = 8
QK_NOPE_DIM = 64
QK_ROPE_DIM = 32
V_HEAD_DIM = 64
QK_HEAD_DIM = QK_NOPE_DIM + QK_ROPE_DIM
Q_LORA_RANK = 256
KV_LORA_RANK = 128
ROPE_THETA = 10000.0
Q_BLOCK = 128
N_BRANCHES = 2
IN_COLS = 3 * CONV_WIDTH + Q_LORA_RANK + KV_LORA_RANK + QK_ROPE_DIM + N_BRANCHES * D_MODEL
N_EXPERTS = 16
N_GROUPS = 4
EXPERTS_PER_GROUP = N_EXPERTS // N_GROUPS
TOP_K = 2
D_EXPERT = 256
D_SHARED = 256
EPS = 1e-6

kernel_name = "hybrid_conv_mla_grouped_moe_adaln_encoder"

def rmsnorm(x, g):
    xf = x.astype(jnp.float32)
    y = xf * lax.rsqrt(jnp.mean(xf * xf, axis=-1, keepdims=True) + EPS)
    return (y * g.astype(jnp.float32)).astype(x.dtype)

def rope(x, positions):
    half = QK_ROPE_DIM // 2
    inv_freq = ROPE_THETA ** (-jnp.arange(half, dtype=jnp.float32) / half)
    ang = positions.astype(jnp.float32)[..., None] * inv_freq
    cos = jnp.cos(ang)[:, :, None, :]
    sin = jnp.sin(ang)[:, :, None, :]
    xf = x.astype(jnp.float32)
    x1, x2 = xf[..., :half], xf[..., half:]
    out = jnp.concatenate([x1 * cos - x2 * sin, x2 * cos + x1 * sin], axis=-1)
    return out.astype(x.dtype)

def short_conv(u, w):
    pad = CONV_K // 2
    return lax.conv_general_dilated(
        u, w[:, None, :], window_strides=(1,), padding=[(pad, pad)],
        dimension_numbers=('NWC', 'WIO', 'NWC'), feature_group_count=u.shape[-1])

def block_attention(q, k, v):
    b, s, h, dq = q.shape
    nblk = s // Q_BLOCK
    scale = QK_HEAD_DIM ** -0.5
    qb = q.reshape(b, nblk, Q_BLOCK, h, dq).transpose(1, 0, 2, 3, 4)

    def one_block(qblk):
        sc = jnp.einsum('bqhd,bkhd->bhqk', qblk, k).astype(jnp.float32) * scale
        p = jax.nn.softmax(sc, axis=-1)
        return jnp.einsum('bhqk,bkhd->bqhd', p.astype(v.dtype), v)

    o = lax.map(one_block, qb)
    return o.transpose(1, 0, 2, 3, 4).reshape(b, s, h, v.shape[-1])

def mixer(h, positions, w_in, conv_w, g_q_a, w_uq, g_kv_a, w_ukv, g_qn, g_kn,
          w_conv_out, w_attn_out, w_o):
    b, s, _ = h.shape
    sizes = [CONV_WIDTH, CONV_WIDTH, CONV_WIDTH, Q_LORA_RANK, KV_LORA_RANK, QK_ROPE_DIM, D_MODEL]
    splits = [int(i) for i in np.cumsum(sizes)]
    proj = h @ w_in
    cb, cc, cx, cq, ckv, k_pe, ga, gb = jnp.split(proj, splits, axis=-1)

    ya = (cb * short_conv(cc * cx, conv_w)) @ w_conv_out

    q = (rmsnorm(cq, g_q_a) @ w_uq).reshape(b, s, N_HEADS, QK_HEAD_DIM)
    kv = (rmsnorm(ckv, g_kv_a) @ w_ukv).reshape(b, s, N_HEADS, QK_NOPE_DIM + V_HEAD_DIM)
    k_nope, v = kv[..., :QK_NOPE_DIM], kv[..., QK_NOPE_DIM:]
    k = jnp.concatenate(
        [k_nope, jnp.broadcast_to(k_pe[:, :, None, :], (b, s, N_HEADS, QK_ROPE_DIM))], axis=-1)
    q = rmsnorm(q, g_qn)
    k = rmsnorm(k, g_kn)
    q = jnp.concatenate([q[..., :QK_NOPE_DIM], rope(q[..., QK_NOPE_DIM:], positions)], axis=-1)
    k = jnp.concatenate([k[..., :QK_NOPE_DIM], rope(k[..., QK_NOPE_DIM:], positions)], axis=-1)
    o = block_attention(q, k, v).reshape(b, s, N_HEADS * V_HEAD_DIM)
    yb = o @ w_attn_out

    merged = jax.nn.sigmoid(ga) * ya + jax.nn.sigmoid(gb) * yb
    return merged @ w_o

def moe(h, w_router, b_router, w_e_gate, w_e_up, w_e_down, w_s_gate, w_s_up, w_s_down):
    scores = jax.nn.sigmoid(jnp.einsum('bsd,de->bse', h, w_router).astype(jnp.float32))
    biased = scores + b_router.astype(jnp.float32)
    grouped = biased.reshape(biased.shape[:-1] + (N_GROUPS, EXPERTS_PER_GROUP))
    group_score = lax.top_k(grouped, TOP_K)[0].sum(axis=-1)
    sel_group = jnp.argmax(group_score, axis=-1)
    expert_group = jnp.arange(N_EXPERTS) // EXPERTS_PER_GROUP
    masked = jnp.where(expert_group == sel_group[..., None], biased, -jnp.inf)
    _, idx = lax.top_k(masked, TOP_K)
    sel = jnp.take_along_axis(scores, idx, axis=-1)
    wts = sel / jnp.sum(sel, axis=-1, keepdims=True)
    combine = jnp.sum(jax.nn.one_hot(idx, N_EXPERTS, dtype=jnp.float32) * wts[..., None], axis=-2)

    a = jax.nn.silu(jnp.einsum('bsd,edf->bsef', h, w_e_gate)) * jnp.einsum('bsd,edf->bsef', h, w_e_up)
    a = a * combine.astype(h.dtype)[..., None]
    routed = jnp.einsum('bsef,efd->bsd', a, w_e_down)
    shared = (jax.nn.silu(h @ w_s_gate) * (h @ w_s_up)) @ w_s_down
    return routed + shared

def setup_inputs(seed: int = 0) -> dict:
    key = jax.random.key(seed)
    ks = jax.random.split(key, 32)
    f32 = jnp.float32

    def nrm(k, shape, fan_in, mult=1.0):
        return jax.random.normal(k, shape, f32) * (mult * fan_in ** -0.5)

    def gain(k, shape):
        return 1.0 + 0.02 * jax.random.normal(k, shape, f32)

    x = jax.random.normal(ks[0], (BATCH, SEQ, D_MODEL), f32)
    c = jax.random.normal(ks[1], (BATCH, D_MODEL), f32)
    offset = jax.random.randint(ks[2], (BATCH, 1), 0, SEQ, dtype=jnp.int32)
    positions = jnp.broadcast_to(jnp.arange(SEQ, dtype=jnp.int32)[None, :], (BATCH, SEQ)) + offset
    L = DEPTH
    return {
        'x': x,
        'c': c,
        'positions': positions,
        'w_ada': nrm(ks[3], (L, D_MODEL, 6 * D_MODEL), D_MODEL, 0.5),
        'b_ada': 0.01 * jax.random.normal(ks[4], (L, 6 * D_MODEL), f32),
        'g_mix': gain(ks[5], (L, D_MODEL)),
        'g_ffn': gain(ks[6], (L, D_MODEL)),
        'w_in': nrm(ks[7], (L, D_MODEL, IN_COLS), D_MODEL),
        'conv_w': nrm(ks[8], (L, CONV_K, CONV_WIDTH), CONV_K),
        'g_q_a': gain(ks[9], (L, Q_LORA_RANK)),
        'w_uq': nrm(ks[10], (L, Q_LORA_RANK, N_HEADS * QK_HEAD_DIM), Q_LORA_RANK),
        'g_kv_a': gain(ks[11], (L, KV_LORA_RANK)),
        'w_ukv': nrm(ks[12], (L, KV_LORA_RANK, N_HEADS * (QK_NOPE_DIM + V_HEAD_DIM)), KV_LORA_RANK),
        'g_qn': gain(ks[13], (L, QK_HEAD_DIM)),
        'g_kn': gain(ks[14], (L, QK_HEAD_DIM)),
        'w_conv_out': nrm(ks[15], (L, CONV_WIDTH, D_MODEL), CONV_WIDTH),
        'w_attn_out': nrm(ks[16], (L, N_HEADS * V_HEAD_DIM, D_MODEL), N_HEADS * V_HEAD_DIM),
        'w_o': nrm(ks[17], (L, D_MODEL, D_MODEL), D_MODEL),
        'w_router': nrm(ks[18], (D_MODEL, N_EXPERTS), D_MODEL),
        'b_router': 0.01 * jax.random.normal(ks[19], (N_EXPERTS,), f32),
        'w_e_gate': nrm(ks[20], (L, N_EXPERTS, D_MODEL, D_EXPERT), D_MODEL),
        'w_e_up': nrm(ks[21], (L, N_EXPERTS, D_MODEL, D_EXPERT), D_MODEL),
        'w_e_down': nrm(ks[22], (L, N_EXPERTS, D_EXPERT, D_MODEL), D_EXPERT),
        'w_s_gate': nrm(ks[23], (L, D_MODEL, D_SHARED), D_MODEL),
        'w_s_up': nrm(ks[24], (L, D_MODEL, D_SHARED), D_MODEL),
        'w_s_down': nrm(ks[25], (L, D_SHARED, D_MODEL), D_SHARED),
    }

def reference(x, c, positions, w_ada, b_ada, g_mix, g_ffn, w_in, conv_w, g_q_a, w_uq,
              g_kv_a, w_ukv, g_qn, g_kn, w_conv_out, w_attn_out, w_o, w_router, b_router,
              w_e_gate, w_e_up, w_e_down, w_s_gate, w_s_up, w_s_down):
    for l in range(DEPTH):
        mod = jax.nn.silu(c) @ w_ada[l] + b_ada[l]
        sh1, sc1, gt1, sh2, sc2, gt2 = jnp.split(mod[:, None, :], 6, axis=-1)
        h = rmsnorm(x, g_mix[l]) * (1 + sc1) + sh1
        x = x + gt1 * mixer(h, positions, w_in[l], conv_w[l], g_q_a[l], w_uq[l], g_kv_a[l],
                            w_ukv[l], g_qn[l], g_kn[l], w_conv_out[l], w_attn_out[l], w_o[l])
        h = rmsnorm(x, g_ffn[l]) * (1 + sc2) + sh2
        x = x + gt2 * moe(h, w_router, b_router, w_e_gate[l], w_e_up[l], w_e_down[l],
                          w_s_gate[l], w_s_up[l], w_s_down[l])
    return x


_drawn_inputs = setup_inputs


def setup_inputs(seed=0):
    import zlib

    import numpy as np

    out = dict(_drawn_inputs(seed))
    spreads = {}
    factors = {'g_q_a': 8.0, 'g_kv_a': 5.121, 'g_qn': 8.0, 'g_kn': 8.0}
    for name, (base, spread) in spreads.items():
        noise = np.random.default_rng([zlib.crc32(name.encode()), seed]).standard_normal(out[name].shape)
        drawn = base * np.exp(spread * noise) if base else spread * noise
        out[name] = __import__('jax').numpy.asarray(drawn.astype(out[name].dtype))
    for name, factor in factors.items():
        out[name] = (out[name] * factor).astype(out[name].dtype)
    return out
```

```python
from contextlib import ExitStack

import numpy as np

import concourse.bass as bass
from concourse import mybir
from concourse.alu_op_type import AluOpType as ALU

ACT = mybir.ActivationFunctionType
AX = mybir.AxisListType
F32 = mybir.dt.float32
BF16 = mybir.dt.bfloat16
I32 = mybir.dt.int32

P = 128
EPS = 1e-6
ROPE_THETA = 10000.0
BANK = 512
SLOTS = 64
CHUNK = 4096
RING = 5


class Signal:

    def __init__(self, sem, per_layer=1):
        self.sem, self.per_layer = sem, per_layer

    def __call__(self, layer, n=1):
        return self.sem, layer * self.per_layer + n


def trunk(nc, x, c, positions, w_ada, b_ada, g_mix, g_ffn, w_in, conv_w, g_q_a, w_uq, g_kv_a, w_ukv,
          g_qn, g_kn, w_conv_out, w_attn_out, w_o, w_router, b_router, w_e_gate, w_e_up, w_e_down,
          w_s_gate, w_s_up, w_s_down, out):
    _, S, D = x.shape
    L = w_in.shape[0]
    CW = w_conv_out.shape[1]
    QR, KR = w_uq.shape[1], w_ukv.shape[1]
    E, F = w_e_gate.shape[1], w_e_gate.shape[3]
    DH = g_qn.shape[1]
    NH = w_uq.shape[2] // DH
    VD = w_attn_out.shape[1] // NH
    ND = w_ukv.shape[2] // NH - VD
    RD = DH - ND
    HALF = RD // 2
    GRP = 4
    EPG = E // GRP
    T = S // P
    C = D // P
    NB = CW // P
    LAT = QR + KR + RD
    QB = QR // P
    PAIRS = E // 2
    GROUPS = S // SLOTS
    EXTRAS = 8
    assert 2 * S // SLOTS <= EXTRAS
    ITERS = EXTRAS // 2
    SCALE = DH ** -0.5
    FC = F // P
    UNITS = 22
    F_LOADED = 6 * 16
    assert (S, D, CW, QR, KR, F, E, NH, DH, VD) == (256, 1024, 512, 256, 128, 256, 16, 8, 96, 64)

    o_cb, o_cc, o_cx = 0, CW, 2 * CW
    o_lat = 3 * CW
    o_ga = o_lat + LAT
    o_gb = o_ga + D

    with ExitStack() as ctx:
        def sb(name, shape, dt=F32):
            return ctx.enter_context(nc.sbuf_tensor(name, shape, dt))

        def signal(name, per_layer=1):
            return Signal(ctx.enter_context(nc.semaphore(name)), per_layer)

        ring = sb("ring", [P, RING, CHUNK])
        w_lat = sb("w_lat", [P, QB * NH * DH + NH * (ND + VD)])
        uq_sb = w_lat[:, 0:QB * NH * DH].rearrange("p (k n) -> p k n", k=QB)
        ukv_sb = w_lat[:, QB * NH * DH:]
        sdown_sb = sb("sdown_sb", [P, FC, D])
        router_sb = sb("router_sb", [P, C, E])
        x_sb = sb("x_sb", [P, T, D])
        hT = sb("hT", [P, C, S])
        gate_rows = sb("gate_rows", [P, 2, D])
        ada_row = sb("ada_row", [P, BANK])
        ada_bias = sb("ada_bias", [P, 2, BANK])
        mod_cols = sb("mod_cols", [P, 2, 3, 2 * C])
        gain = sb("gain", [P, 2, 2, C])
        ident = sb("ident", [P, P])
        tri = sb("tri", [P, P], BF16)
        ones = sb("ones", [P, P], BF16)
        slot_id = sb("slot_id", [P, SLOTS])
        count_up = sb("count_up", [P, E + 1])
        lower = sb("lower", [P, GRP, EPG])
        b_router_sb = sb("b_router_sb", [P, E])
        head_gain = sb("head_gain", [P, L, 2, DH])
        NPRM = 2 * C + QB + 1 + 3 * NB
        cols = sb("cols", [P, L * NPRM + C])
        c_act = sb("c_act", [P, C, 32])
        c_tmp = sb("c_tmp", [P, 2, C])
        cos_sin = sb("cos_sin", [P, T, 2, HALF])
        freq = sb("freq", [P, HALF])
        pos_i = sb("pos_i", [P, T], I32)
        pos_f = sb("pos_f", [P, T])
        sumsq = sb("sumsq", [P, T, 2])
        mean_sq = sb("mean_sq", [P, 2 * NH])
        rstd = sb("rstd", [P, 2 * NH])
        minus_half = sb("minus_half", [P, 2 * NH])
        top = sb("top", [P, 2, T])
        bias_m = sb("bias_m", [P, 2, T])
        denom = sb("denom", [P, 2, T])
        r_small = sb("r_small", [P, 12, T * E])
        pairwise = sb("pairwise", [P, 3, T * GRP, EPG, EPG])
        sel_b = sb("sel_b", [P, T, E], BF16)
        slot_of = sb("slot_of", [P, T, E])
        combine = sb("combine", [P, T, E])
        lengths = sb("lengths", [P, E])
        slot_x = sb("slot_x", [P, T, EXTRAS])
        combine_x = sb("combine_x", [P, T, EXTRAS])
        extra_expert = sb("extra_expert", [P, EXTRAS], I32)
        n_extras = sb("n_extras", [P, 1], I32)
        passes_before = sb("passes_before", [P, 1], I32)
        passes_f = sb("passes_f", [P, 2 + ITERS])

        work = sb("work", [P, 17928])

        def part(a, *shape):
            n = int(np.prod(shape))
            names = "abcd"[:len(shape)]
            v = work[:, a:a + n]
            if len(shape) == 1:
                return v
            return v.rearrange(f"p ({' '.join(names)}) -> p {' '.join(names)}",
                               **{k: s for k, s in zip(names, shape)})

        xn = part(0, T, D)
        merged = part(0, C, S)
        cc_tmp = part(2048, 2, BANK)
        u = part(3072, NB, S + 2)
        yc = part(4104, NB, S)
        qk = part(5128, T, 2, NH, DH)
        sq = part(8200, 2 * NH, DH)
        lat_n = part(8200, T, QR + KR)
        v_sb = part(9736, T, NH, VD)
        qkT = part(10760, 2, 2, S)
        tanh_b = part(11784, C, S)
        oT = part(13832, NH // 2, S)
        probs = part(14856, 2, T, S)
        rot_tmp = part(14856, 4, 2 * NH, HALF)
        probsT = part(15880, 2, T, S)
        latT = part(15880, QB + 1, S)
        tanh_a = part(16904, 2, BANK)
        unused = part(16904, T, QR + KR)
        angle = part(11784, 3, T, 2, HALF)
        rows = part(13832, P)
        ids_i = part(14000, SLOTS).bitcast(I32)
        count_i = part(14100, E + 1).bitcast(I32)
        onehot = part(2048, T, E, SLOTS)
        y = part(2048, D)
        weighted = part(4096, T, E, SLOTS)
        combT = part(6144, PAIRS, S)
        hE = part(8192, C, E, SLOTS)
        e_tanh = part(16384, 2, F)
        e_act = part(16896, 2, F)
        s_tanh = part(16384, FC, S)
        s_act = part(16896, FC, S)
        aT = part(17408, FC, P)
        router_out = part(17664, S)
        hT_flat = hT[:, :, :].rearrange("p c s -> p (c s)")
        NF = E * (GROUPS - 1)
        LEAD = 32
        flags = hT_flat[:, 0:NF]
        run_sums = [hT_flat[:, 64 + k * 96:64 + k * 96 + LEAD + NF] for k in range(2)]
        match = hT_flat[:, 256:256 + EXTRAS * NF].rearrange("p (k e g) -> p k e g", k=EXTRAS, e=E)
        is_expert = hT_flat[:, 640:640 + EXTRAS * E].rearrange("p (k e) -> p k e", k=EXTRAS)
        scratch_e = hT_flat[:, 768:768 + EXTRAS * E].rearrange("p (k e) -> p k e", k=EXTRAS)
        is_group = hT_flat[:, 896:896 + EXTRAS * (GROUPS - 1)].rearrange("p (k g) -> p k g", k=EXTRAS)
        group_of = hT_flat[:, 928:928 + EXTRAS]
        expert_f = hT_flat[:, 936:936 + EXTRAS]
        onehot_x = hT_flat[:, 1024:1280].rearrange("p (t e s) -> p t e s", t=T, e=2)
        weighted_x = hT_flat[:, 1280:1536].rearrange("p (t e s) -> p t e s", t=T, e=2)

        psum = ctx.enter_context(nc.psum_tensor("psum", [P, 8, BANK], F32))

        slot_loaded = [signal(f"slot{i}_loaded") for i in range(RING)]
        x_loaded = signal("x_loaded")
        params_loaded = signal("params_loaded")
        bias_loaded = [signal(f"ada_bias{i}_loaded") for i in range(2)]
        latw_loaded = signal("latw_loaded")
        sdown_loaded = signal("sdown_loaded")
        out_stored = signal("out_stored")
        consts = signal("consts_ready")
        vconsts = signal("vector_consts_ready")
        cols_psum = signal("param_columns_in_psum")
        cols_ready = signal("param_columns_ready")
        c_tanh = signal("c_tanh_ready")
        c_ready = signal("c_act_ready")
        angles_ready = signal("angles_ready")
        rope_ready = signal("cos_sin_ready")
        dve = signal("vector_step_done")
        pool = signal("pool_step_done")
        ada_sums = signal("ada_sums")
        ada_row_ready = signal("ada_row_ready")
        ada_turned = signal("ada_turned")
        mod_ready = signal("mod_columns_ready")
        gate_ready = signal("gate_row_ready", 2)
        gain_ready = signal("gain_ready", 2)
        x_squares = signal("x_squares_ready", 2)
        ms_ready = signal("mean_squares_ready", 5)
        rstd_ready = signal("rstd_ready", 5)
        xn_ready = signal("x_normed", 2)
        xnT_ready = signal("x_turned", 8)
        hT_act = signal("hT_half_by_scalar", 2)
        hT_dve = signal("hT_half_by_vector", 2)
        lat_psum = signal("latents_in_psum", T)
        lat_squares = signal("latent_squares_ready", T)
        lat_ready = signal("latents_normed", T)
        latT_psum = signal("latents_turned", T)
        latT_ready = signal("latT_ready", T)
        up_psum = signal("up_projections_in_psum", 2 * T)
        qkv_copied = signal("qkv_copied", 2 * T)
        qk_squares = signal("qk_squares_ready", T)
        qk_ready = signal("qk_normed_rotated", T)
        unit_psum = signal("unit_in_psum", UNITS)
        cc_ready = signal("cc_copied", 2)
        u_ready = signal("u_ready", 2)
        conv_ready = signal("conv_gated", 2)
        ya_ready = signal("ya_copied", 4)
        ga_tanh = signal("gate_a_tanh", 4)
        ga_used = signal("gate_a_used", 4)
        gb_tanh = signal("gate_b_tanh", 4)
        qkT_psum = signal("qk_turned", NH)
        qkT_ready = signal("qkT_ready", NH)
        scores_psum = signal("scores_in_psum", NH)
        bias_ready = signal("score_bias_ready", NH)
        exp_done = signal("exp_done", NH)
        probs_ready = signal("probs_ready", NH)
        pT_psum = signal("probs_turned", NH)
        pT_ready = signal("probsT_ready", NH)
        pv_psum = signal("pv_in_psum", NH)
        oT_ready = signal("oT_pair_ready", NH // 2)
        yb_gated = signal("gated_yb_ready", 4)
        merged_ready = signal("merged_ready", 4)
        mix_psum = signal("mixer_out_in_psum", 2 * T)
        mix_added = signal("mixer_added", 1)
        router_psum = signal("router_in_psum")
        router_copied = signal("router_copied")
        routerT_psum = signal("router_turned")
        router_exp = signal("router_exp_ready")
        chosen = signal("experts_chosen")
        rank_psum = signal("ranks_in_psum")
        ranks_read = signal("ranks_read")
        onehot_ready = signal("onehot_ready")
        weighted_ready = signal("weighted_onehot_ready")
        s_gate_psum = signal("shared_gate_in_psum")
        s_tanh_ready = signal("shared_tanh_ready")
        s_up_psum = signal("shared_up_in_psum")
        s_act_ready = signal("shared_act_ready")
        s_down_psum = signal("shared_down_issued")
        gather_psum = signal("gathered_in_psum", 2 * C)
        hE_act = signal("gathered_by_scalar", C)
        hE_dve = signal("gathered_by_vector", C)
        combT_psum = signal("weighted_turned", 4)
        combT_act = signal("combT_by_scalar", 2)
        combT_dve = signal("combT_by_vector", 2)
        gu_psum = signal("gate_up_in_psum", PAIRS)
        tanh_ready = signal("expert_tanh_ready", PAIRS)
        act_ready = signal("expert_act_ready", PAIRS)
        aT_psum = signal("expert_act_turned", PAIRS)
        aT_ready = signal("aT_ready", PAIRS)
        down_psum = signal("down_in_psum", 2 * PAIRS)
        y_act = signal("y_by_scalar", PAIRS)
        y_dve = signal("y_by_vector", PAIRS)
        added_psum = signal("added_to_tokens", PAIRS)
        moe_psum = signal("moe_out_in_psum")
        moe_added = signal("moe_added", 1)
        extras_ready = signal("extras_listed")
        x_loaded_w = signal("extra_weights_loaded")
        x_onehot = signal("extra_onehot_ready")
        x_weighted = signal("extra_weighted_ready")
        x_gathered = signal("extra_gathered")
        x_turned = signal("extra_onehot_turned")
        x_tokens_act = signal("extra_tokens_by_scalar")
        x_tokens_dve = signal("extra_tokens_by_vector")
        x_gu = signal("extra_gate_up")
        x_tanh = signal("extra_tanh_ready")
        x_act1 = signal("extra_act_begun")
        x_act = signal("extra_act_ready")
        x_aT_psum = signal("extra_act_turned")
        x_aT = signal("extra_aT_ready")
        x_down = signal("extra_down")
        x_y_act = signal("extra_y_by_scalar")
        x_y_dve = signal("extra_y_by_vector")
        x_free = signal("extra_pass_done")

        chunks, number = [], {}

        def chunk(key, pieces, freed_by):
            number[key] = len(chunks)
            chunks.append((pieces, freed_by))

        def ada_chunks(s, parts=range(4)):
            w = w_ada[s // 3, :, (s % 3) * 4 * BANK:(s % 3 + 1) * 4 * BANK].rearrange("(c p) n -> p c n", p=P)
            for i in parts:
                chunk(("ada", s, i), [(0, 2, w[:, 2 * i:2 * i + 2, :])], ada_sums(0, 4 * s + i + 1))

        def in_chunk(l, key, a, n, freed_by):
            chunk((key, l), [(0, C, w_in[l, :, a:a + n].rearrange("(c p) n -> p c n", p=P))], freed_by)

        ada_chunks(0)
        for l in range(L):
            in_chunk(l, "lat", o_lat, LAT, lat_psum(l, T))
            in_chunk(l, "cc", o_cc, CW, unit_psum(l, 3))
            in_chunk(l, "cx", o_cx, CW, unit_psum(l, 4))
            in_chunk(l, "cb", o_cb, CW, unit_psum(l, 6))
            chunk(("conv", l), [(0, NB, w_conv_out[l].rearrange("(c p) n -> p c n", p=P))], unit_psum(l, 10))
            in_chunk(l, "ga0", o_ga, BANK, unit_psum(l, 12))
            ada_chunks(3 * l + 1, [0])
            in_chunk(l, "ga1", o_ga + BANK, BANK, unit_psum(l, 14))
            ada_chunks(3 * l + 1, [1, 2])
            in_chunk(l, "gb0", o_gb, BANK, unit_psum(l, 16))
            ada_chunks(3 * l + 1, [3])
            in_chunk(l, "gb1", o_gb + BANK, BANK, unit_psum(l, 18))
            ada_chunks(3 * l + 2)
            chunk(("attn", l), [(0, NB, w_attn_out[l].rearrange("(c p) n -> p c n", p=P))], unit_psum(l, UNITS))
            for i in range(2):
                chunk((f"wo{i}", l), [(0, C, w_o[l, :, i * BANK:(i + 1) * BANK].rearrange("(c p) n -> p c n", p=P))],
                      mix_psum(l, 2 + 2 * i))
            if l + 1 < L:
                ada_chunks(3 * l + 3)
            chunk(("shared", l), [(0, C, w_s_gate[l].rearrange("(c p) n -> p c n", p=P)),
                                  (F, C, w_s_up[l].rearrange("(c p) n -> p c n", p=P))], s_up_psum(l))
            for i in range(PAIRS + 1):
                for e in range(2 * i, min(2 * i + 2, E)):
                    chunk(("gu", l, e), [(0, C, w_e_gate[l, e].rearrange("(c p) n -> p c n", p=P)),
                                         (F, C, w_e_up[l, e].rearrange("(c p) n -> p c n", p=P))], gu_psum(l, i + 1))
                if i:
                    chunk(("down", l, i - 1),
                          [(0, 2 * FC, w_e_down[l, 2 * i - 2:2 * i].rearrange("e (c p) n -> p (e c) n", p=P))],
                          down_psum(l, 2 * i))
            for k in range(3):
                chunk(("extra", l, k), [], moe_psum(l))

        def slot(key, k):
            return ring[:, number[key] % RING, :].rearrange("p (k n) -> p k n", k=k)

        def loaded(key):
            n = number[key]
            return slot_loaded[n % RING].sem, 16 * len(pieces_before(n))

        def pieces_before(n):
            return [q for i in range(n % RING, n + 1, RING) for q in chunks[i][0]]

        PRM = {}
        at = 0
        for l in range(L):
            for name, n in (("g_mix", C), ("g_ffn", C), ("g_q_a", QB), ("g_kv_a", 1), ("conv", 3 * NB)):
                PRM[name, l] = at
                at += n
        PRM["c"] = at
        NROWS = at + C

        def col(name, l, i, n=1):
            return cols[:, PRM[name, l] + i:PRM[name, l] + i + n]

        sc_of = lambda l, which: mod_cols[:, l % 2, 0, C:2 * C] if which == 0 else mod_cols[:, l % 2, 2, 0:C]
        sh_of = lambda l, which: mod_cols[:, l % 2, 0, 0:C] if which == 0 else mod_cols[:, l % 2, 1, C:2 * C]

        block = ctx.enter_context(nc.Block())

        @block.sync
        def _(sp):
            sp.dma_start(x_sb[:, :, :], x[0].rearrange("(t p) d -> p t d", p=P)).then_inc(x_loaded.sem, 16)

            def load_pair(l, j):
                slots = [ring[:, number["extra", l, k] % RING, :] for k in range(3)]
                for k in range(2):
                    e = sp.value_load(extra_expert[0:1, bass.ds(2 * j + k, 1)], min_val=0, max_val=E - 1)
                    dst = slots[k].rearrange("p (c n) -> p c n", c=C)
                    for at, w in ((0, w_e_gate), (F, w_e_up)):
                        sp.dma_start(dst[:, :, at:at + F], w[l, bass.ds(e, 1)].rearrange("e (c p) n -> p (e c) n", p=P)) \
                            .then_inc(x_loaded_w.sem, 16)
                    dst = slots[2].rearrange("p (k n) -> p k n", k=2 * FC)
                    sp.dma_start(dst[:, k * FC:(k + 1) * FC, :],
                                 w_e_down[l, bass.ds(e, 1)].rearrange("e (c p) n -> p (e c) n", p=P)) \
                        .then_inc(x_loaded_w.sem, 16)

            def load_first_extras(l):
                for k in range(3):
                    sp.wait_ge(*chunks[number["extra", l, k] - RING][1])
                sp.wait_ge(*extras_ready(l))
                listed = sp.value_load(n_extras[0:1, 0:1], min_val=0, max_val=EXTRAS)
                with sp.If(listed > 0):
                    load_pair(l, 0)
                return listed

            def load_further_extras(l, listed):
                before = sp.value_load(passes_before[0:1, 0:1], min_val=0, max_val=L * ITERS)
                with sp.Fori(1, ITERS) as j:
                    with sp.If(listed > 2 * j):
                        sp.wait_ge(x_free.sem, j + before + 1)
                        load_pair(l, j)

            for n, (pieces, _) in enumerate(chunks):
                for l in range(L):
                    if n == number["extra", l, 0]:
                        listed = load_first_extras(l)
                    if n == number["extra", l, 2] + RING - 2:
                        load_further_extras(l, listed)
                if n >= RING and pieces:
                    sp.wait_ge(*chunks[n - RING][1])
                for a, k, src in pieces:
                    width = src.shape[2]
                    dst = ring[:, n % RING, :].rearrange("p (k n) -> p k n", k=k)[:, :, a:a + width]
                    sp.dma_start(dst, src).then_inc(slot_loaded[n % RING].sem, 16)
                for l in range(L):
                    if n == number["cc", l]:
                        if l:
                            sp.wait_ge(*up_psum(l - 1, 2 * T))
                        sp.dma_start(uq_sb, w_uq[l].rearrange("(c p) n -> p c n", p=P)).then_inc(latw_loaded.sem, 16)
                        sp.dma_start(ukv_sb, w_ukv[l]).then_inc(latw_loaded.sem, 16)
                    if n == number["shared", l]:
                        if l:
                            sp.wait_ge(*s_down_psum(l - 1))
                        sp.dma_start(sdown_sb[:, :, :], w_s_down[l].rearrange("(c p) n -> p c n", p=P)) \
                            .then_inc(sdown_loaded.sem, 16)
            load_further_extras(L - 1, listed)
            sp.wait_ge(*moe_added(L - 1))
            sp.dma_start(out[0].rearrange("(t p) d -> p t d", p=P), x_sb[:, :, :]).then_inc(out_stored.sem, 16)
            sp.wait_ge(out_stored.sem, 16)

        @block.gpsimd
        def _(gp):
            step = [0]

            def link(ins):
                step[0] += 1
                ins.then_inc(pool.sem, 1)
                gp.wait_ge(pool.sem, step[0])

            link(gp.memset(ident[:, :], 0.0))
            gp.affine_select(out=ident[:, :], in_=ident[:, :], compare_op=ALU.not_equal, fill=1.0, base=0,
                             pattern=[[-1, P]], channel_multiplier=1).then_inc(consts.sem, 1)
            link(gp.memset(tri[:, :], 1.0))
            gp.affine_select(out=tri[:, :], in_=tri[:, :], compare_op=ALU.is_gt, fill=0.0, base=0,
                             pattern=[[1, P]], channel_multiplier=-1).then_inc(consts.sem, 1)
            gp.memset(ones[:, :], 1.0).then_inc(consts.sem, 1)
            gp.iota(ids_i, pattern=[[1, SLOTS]], base=-2 * S, channel_multiplier=0).then_inc(consts.sem, 1)
            gp.iota(count_i, pattern=[[1, E + 1]], base=0, channel_multiplier=0).then_inc(consts.sem, 1)
            gp.memset(minus_half[:, :], -0.5).then_inc(consts.sem, 1)
            gp.wait_ge(*consts(0, 6))

            def power(l, n, width):
                gp.wait_ge(*ms_ready(l, n))
                gp.tensor_tensor(rstd[:, 0:width], mean_sq[:, 0:width], minus_half[:, 0:width], ALU.pow) \
                    .then_inc(rstd_ready.sem, 1)
                gp.wait_ge(*rstd_ready(l, n))

            def gates(l, which):
                gp.wait_ge(*ada_row_ready(0, 3 * l + 2 + which))
                if l:
                    gp.wait_ge(*(mix_added if which == 0 else moe_added)(l - 1))
                first = 0 if which == 0 else 2
                for j in range(2):
                    q = 32 * (first + j)
                    ins = gp.partition_broadcast(gate_rows[:, which, j * BANK:(j + 1) * BANK], ada_row[q:q + 1, :], P)
                    if j == 0:
                        link(ins)
                ins.then_inc(gate_ready.sem, 1)
                gp.wait_ge(*gate_ready(l, which + 1))

            for l in range(L):
                power(l, 1, T)
                power(l, 2, 2 * T)
                power(l, 3, 2 * NH)
                power(l, 4, 2 * NH)
                gates(l, 0)
                gates(l, 1)
                power(l, 5, T)

        @block.scalar
        def _(act):
            for l in range(L):
                for name, src in (("g_mix", g_mix[l]), ("g_ffn", g_ffn[l]), ("g_q_a", g_q_a[l]), ("g_kv_a", g_kv_a[l])):
                    a = PRM[name, l]
                    n = src.shape[0] // P
                    act.dma_start(rows[a:a + n, :], src.rearrange("(c p) -> c p", p=P)).then_inc(params_loaded.sem, 16)
                a = PRM["conv", l]
                act.dma_start(rows[a:a + 3 * NB, :], conv_w[l].rearrange("k (c p) -> (k c) p", p=P)) \
                    .then_inc(params_loaded.sem, 16)
                act.dma_start(head_gain[:, l, 0, :], g_qn[l].partition_broadcast(P)).then_inc(params_loaded.sem, 16)
                act.dma_start(head_gain[:, l, 1, :], g_kn[l].partition_broadcast(P)).then_inc(params_loaded.sem, 16)
            act.dma_start(rows[PRM["c"]:PRM["c"] + C, :], c[0].rearrange("(c p) -> c p", p=P)) \
                .then_inc(params_loaded.sem, 16)
            act.dma_start(b_router_sb[:, :], b_router.partition_broadcast(P)).then_inc(params_loaded.sem, 16)
            act.dma_start(router_sb[:, :, :], w_router.rearrange("(c p) e -> p c e", p=P)) \
                .then_inc(params_loaded.sem, 16)
            for t in range(T):
                act.dma_start(pos_i[:, t:t + 1], positions[0, t * P:(t + 1) * P].rearrange("(p o) -> p o", o=1)) \
                    .then_inc(params_loaded.sem, 16)

            def load_bias(s):
                if s >= 2:
                    act.wait_ge(*ada_row_ready(0, s - 1))
                for j in range(4):
                    a = ((s % 3) * 4 + j) * BANK
                    act.dma_start(ada_bias[32 * j:32 * j + 32, s % 2, :],
                                  b_ada[s // 3, a:a + BANK].partition_broadcast(32)) \
                        .then_inc(bias_loaded[s % 2].sem, 16)

            def mod_columns(s, bank):
                act.wait_ge(*ada_turned(0, s + 1))
                src = psum[:, bank, :].rearrange("p (b j r) -> p j b r", b=4, r=32)[:, :, :, 0]
                nc.scalar.activation(mod_cols[:, (s // 3) % 2, s % 3, :].rearrange("p (j b) -> p j b", b=4), src,
                                     ACT.Identity).then_inc(mod_ready.sem, 1)
                if s + 2 < 3 * L:
                    load_bias(s + 2)

            def square_x(l, which):
                if which:
                    act.wait_ge(*mix_added(l))
                elif l:
                    act.wait_ge(*moe_added(l - 1))
                else:
                    act.wait_ge(x_loaded.sem, 16)
                for t in range(T):
                    ins = nc.scalar.activation(xn[:, t, :], x_sb[:, t, :], ACT.Square, accum_out=sumsq[:, t, 0:1])
                ins.then_inc(x_squares.sem, 1)

            def modulate_half(l, which):
                act.wait_ge(*gain_ready(l, which + 1))
                for b in range(2):
                    act.wait_ge(*xnT_ready(l, 4 * which + b + 1))
                    for k in range(2):
                        q = 2 * b + k
                        ins = nc.scalar.activation(hT[:, q, :], psum[:, 3 + b, k * S:(k + 1) * S], ACT.Identity,
                                                   bias=sh_of(l, which)[:, q:q + 1],
                                                   scale=gain[:, l % 2, which, q:q + 1])
                ins.then_inc(hT_act.sem, 1)

            load_bias(0)
            load_bias(1)
            act.wait_ge(*cols_ready(0))
            nc.scalar.activation(c_tmp[:, 0, :], cols[:, PRM["c"]:PRM["c"] + C], ACT.Tanh, scale=0.5) \
                .then_inc(c_tanh.sem, 1)
            act.wait_ge(*angles_ready(0))
            nc.scalar.activation(cos_sin[:, :, :, :], angle[:, 0], ACT.Sin).then_inc(rope_ready.sem, 1)
            square_x(0, 0)
            mod_columns(0, 7)

            for l in range(L):
                if l:
                    square_x(l, 0)
                modulate_half(l, 0)

                for t in range(T):
                    act.wait_ge(*lat_psum(l, t + 1))
                    nc.scalar.activation(unused[:, t, 0:QR], psum[:, 2 + t, 0:QR], ACT.Square,
                                         accum_out=sumsq[:, t, 0:1])
                    nc.scalar.activation(unused[:, t, QR:], psum[:, 2 + t, QR:QR + KR], ACT.Square,
                                         accum_out=sumsq[:, t, 1:2]).then_inc(lat_squares.sem, 1)

                def copy_cc(j):
                    act.wait_ge(*unit_psum(l, 2 * j + 1))
                    nc.scalar.activation(cc_tmp[:, j, :], psum[:, 0, :], ACT.Identity).then_inc(cc_ready.sem, 1)

                copy_cc(0)
                for t in range(T):
                    act.wait_ge(*latT_psum(l, t + 1))
                    for b in range(QB + 1):
                        g = col("g_q_a", l, b) if b < QB else col("g_kv_a", l, 0)
                        ins = nc.scalar.activation(latT[:, b, t * P:(t + 1) * P], psum[:, 4 + t, b * P:(b + 1) * P],
                                                   ACT.Identity, scale=g)
                    ins.then_inc(latT_ready.sem, 1)
                copy_cc(1)

                for n, (t, what, bank) in enumerate(((0, "q", 2), (0, "kv", 4), (1, "q", 6), (1, "kv", 2))):
                    act.wait_ge(*up_psum(l, n + 1))
                    if what == "q":
                        flat = qk[:, t, 0].rearrange("p h d -> p (h d)")
                        nc.scalar.activation(flat[:, 0:BANK], psum[:, bank, :], ACT.Identity)
                        nc.scalar.activation(flat[:, BANK:], psum[:, bank + 1, 0:NH * DH - BANK], ACT.Identity) \
                            .then_inc(qkv_copied.sem, 1)
                    else:
                        src = psum[:, bank:bank + 2, :].rearrange("p b (h d) -> p (b h) d", d=ND + VD)
                        nc.scalar.activation(qk[:, t, 1, :, 0:ND], src[:, :, 0:ND], ACT.Identity)
                        nc.scalar.activation(v_sb[:, t, :, :], src[:, :, ND:], ACT.Identity) \
                            .then_inc(qkv_copied.sem, 1)

                def square_qk(t):
                    act.wait_ge(*qkv_copied(l, 2 * t + 2))
                    act.wait_ge(*lat_ready(l, t + 1))
                    if t:
                        act.wait_ge(*ms_ready(l, 3))
                    nc.scalar.activation(sq[:, :, :], qk[:, t].rearrange("p a h d -> p (a h) d"), ACT.Square) \
                        .then_inc(qk_squares.sem, 1)

                def copy_ya(j):
                    act.wait_ge(*unit_psum(l, 7 + j))
                    nc.scalar.activation(merged[:, 2 * j:2 * j + 2, :].rearrange("p c s -> p (c s)"),
                                         psum[:, j % 2, :], ACT.Identity, scale=0.5).then_inc(ya_ready.sem, 1)

                def tanh_unit(n):
                    act.wait_ge(*unit_psum(l, n + 1))
                    if n < 14:
                        j = n - 10
                        if j >= 2:
                            act.wait_ge(*ga_used(l, j - 1))
                        nc.scalar.activation(tanh_a[:, j % 2, :], psum[:, n % 2, :], ACT.Tanh, scale=0.5) \
                            .then_inc(ga_tanh.sem, 1)
                    else:
                        j = n - 14
                        nc.scalar.activation(tanh_b[:, 2 * j:2 * j + 2, :].rearrange("p c s -> p (c s)"),
                                             psum[:, n % 2, :], ACT.Tanh, scale=0.5).then_inc(gb_tanh.sem, 1)

                square_qk(0)
                copy_ya(0)
                copy_ya(1)
                square_qk(1)
                copy_ya(2)
                copy_ya(3)
                tanh_unit(10)

                def copy_qkT(h):
                    act.wait_ge(*qkT_psum(l, h + 1))
                    if h >= 2:
                        act.wait_ge(*scores_psum(l, h - 1))
                    nc.scalar.activation(qkT[0:DH, h % 2].rearrange("p a s -> p (a s)"), psum[0:DH, 2, :],
                                         ACT.Identity).then_inc(qkT_ready.sem, 1)

                copy_qkT(0)
                for h in range(NH):
                    if h + 1 < NH:
                        copy_qkT(h + 1)
                    act.wait_ge(*bias_ready(l, h + 1))
                    if h >= 2:
                        act.wait_ge(*pT_psum(l, h - 1))
                    for t in range(T):
                        ins = nc.scalar.activation(probs[:, h % 2, t, :], psum[:, 4 + h % 2, t * S:(t + 1) * S], ACT.Exp,
                                                   bias=bias_m[:, h % 2, t:t + 1], scale=SCALE,
                                                   accum_out=denom[:, h % 2, t:t + 1])
                    ins.then_inc(exp_done.sem, 1)
                    if h < 7:
                        tanh_unit(11 + h)
                    if h == 4:
                        mod_columns(3 * l + 1, 3)
                    act.wait_ge(*pT_psum(l, h + 1))
                    if h >= 2:
                        act.wait_ge(*pv_psum(l, h - 1))
                    nc.scalar.activation(probsT[:, h % 2].rearrange("p a s -> p (a s)"), psum[:, 6, :],
                                         ACT.Identity).then_inc(pT_ready.sem, 1)
                mod_columns(3 * l + 2, 3)

                square_x(l, 1)
                modulate_half(l, 1)
                if l + 1 < L:
                    mod_columns(3 * l + 3, 7)
                act.wait_ge(*router_psum(l))
                nc.scalar.activation(router_out[0:E, :], psum[0:E, 5, 0:S], ACT.Identity).then_inc(router_copied.sem, 1)
                act.wait_ge(*routerT_psum(l))
                nc.scalar.activation(r_small[:, 0, :], psum[:, 6, 0:T * E], ACT.Exp, scale=-1.0) \
                    .then_inc(router_exp.sem, 1)
                act.wait_ge(*s_gate_psum(l))
                nc.scalar.activation(s_tanh.rearrange("p c s -> p (c s)"), psum[:, 4, :], ACT.Tanh, scale=0.5) \
                    .then_inc(s_tanh_ready.sem, 1)
                for n in range(0, 2 * C, 2):
                    half, q = divmod(n, C)
                    act.wait_ge(*gather_psum(l, n + 1))
                    nc.scalar.activation(hE[:, q, half * 8:half * 8 + 8, :].rearrange("p e s -> p (e s)"),
                                         psum[:, 4 + n % 4, :], ACT.Identity, bias=sh_of(l, 1)[:, q:q + 1],
                                         scale=gain[:, l % 2, 1, q:q + 1]).then_inc(hE_act.sem, 1)
                for b in range(0, 4, 2):
                    act.wait_ge(*combT_psum(l, b + 1))
                    nc.scalar.activation(combT[:, 2 * b:2 * b + 2, :].rearrange("p j s -> p (j s)"),
                                         psum[:, 4 + b, :], ACT.Identity).then_inc(combT_act.sem, 1)

                def copy_y(i):
                    act.wait_ge(*down_psum(l, 2 * i + 1))
                    nc.scalar.activation(y[:, 0:BANK], psum[:, 7, :], ACT.Identity).then_inc(y_act.sem, 1)

                for i in range(PAIRS + 1):
                    if i < PAIRS:
                        act.wait_ge(*gu_psum(l, i + 1))
                        nc.scalar.activation(e_tanh[:, i % 2, :], psum[:, 4 + i % 2, 0:F], ACT.Tanh, scale=0.5) \
                            .then_inc(tanh_ready.sem, 1)
                    if i >= 1:
                        act.wait_ge(*aT_psum(l, i))
                        nc.scalar.activation(aT.rearrange("p c s -> p (c s)"), psum[:, 6, 0:FC * P], ACT.Identity) \
                            .then_inc(aT_ready.sem, 1)
                        copy_y(i - 1)

                act.wait_ge(*extras_ready(l))
                listed = act.value_load(n_extras[0:1, 0:1], min_val=0, max_val=EXTRAS)
                before = act.value_load(passes_before[0:1, 0:1], min_val=0, max_val=L * ITERS)
                with act.Fori(0, ITERS) as j:
                    with act.If(listed > 2 * j):
                        act.wait_ge(x_gathered.sem, j + before + 1)
                        for q in range(0, C, 2):
                            ins = nc.scalar.activation(hE[:, q, 0:2, :].rearrange("p e s -> p (e s)"),
                                                       psum[:, 4 + q % 2, (q // 2) * P:(q // 2 + 1) * P],
                                                       ACT.Identity, bias=sh_of(l, 1)[:, q:q + 1],
                                                       scale=gain[:, l % 2, 1, q:q + 1])
                        ins.then_inc(x_tokens_act.sem, 1)
                        act.wait_ge(x_turned.sem, j + before + 1)
                        nc.scalar.activation(combT[:, 0, :], psum[:, 6, 0:S], ACT.Identity)
                        act.wait_ge(x_gu.sem, j + before + 1)
                        nc.scalar.activation(e_tanh[:, 0, :], psum[:, 7, 0:F], ACT.Tanh, scale=0.5) \
                            .then_inc(x_tanh.sem, 1)
                        act.wait_ge(x_aT_psum.sem, j + before + 1)
                        nc.scalar.activation(aT.rearrange("p c s -> p (c s)"), psum[:, 6, 0:FC * P],
                                             ACT.Identity).then_inc(x_aT.sem, 1)
                        act.wait_ge(x_down.sem, j + before + 1)
                        nc.scalar.activation(y[:, 0:BANK], psum[:, 4, :], ACT.Identity).then_inc(x_y_act.sem, 1)

        @block.vector
        def _(ve):
            step = [0]

            def link(ins):
                step[0] += 1
                ins.then_inc(dve.sem, 1)
                ve.wait_ge(dve.sem, step[0])

            for i in range(HALF):
                nc.vector.memset(freq[:, i:i + 1], float(np.float32(ROPE_THETA ** (-i / HALF))))
            nc.vector.memset(passes_f[:, :], 0.0)
            link(nc.vector.memset(lower[:, :, :], 0.0))
            for i in range(1, GRP):
                ins = nc.vector.memset(lower[:, i, 0:i], 1.0)
            link(ins)
            ve.wait_ge(*consts(0, 6))
            nc.vector.tensor_copy(slot_id[:, :], ids_i)
            link(nc.vector.tensor_copy(count_up[:, :], count_i))

            ve.wait_ge(*cols_psum(0))
            nc.vector.tensor_copy(cols[:, 0:NROWS], psum[:, 6, 0:NROWS]).then_inc(cols_ready.sem, 1)
            ve.wait_ge(*cols_ready(0))
            ve.wait_ge(*c_tanh(0))
            link(nc.vector.scalar_tensor_tensor(out=c_tmp[:, 1, :], in0=c_tmp[:, 0, :], scalar=1.0,
                                                in1=cols[:, PRM["c"]:PRM["c"] + C], op0=ALU.add, op1=ALU.mult))
            nc.vector.tensor_scalar(c_act[:, :, :], c_tmp[:, 1, :].unsqueeze(2).broadcast_to([P, C, 32]), 0.5, None,
                                    ALU.mult).then_inc(c_ready.sem, 1)

            link(nc.vector.tensor_copy(pos_f[:, :], pos_i[:, :]))
            two_pi = 2 * np.pi
            part1 = 6.28125
            part2 = float(round((two_pi - part1) * 2 ** 20)) / 2 ** 20
            part3 = float(np.float32(two_pi - part1 - part2))
            turn = 1.5 * 2.0 ** 23
            for t in range(T):
                for k in range(2):
                    ins = nc.vector.tensor_scalar(angle[:, 0, t, k, :], freq[:, :], pos_f[:, t:t + 1], None, ALU.mult)
            link(ins)
            link(nc.vector.tensor_scalar(angle[:, 1, :, 0, :], angle[:, 0, :, 0, :], 1 / two_pi, 0.25, ALU.mult, ALU.add))
            link(nc.vector.tensor_scalar(angle[:, 1, :, 1, :], angle[:, 0, :, 1, :], 1 / two_pi, None, ALU.mult))
            link(nc.vector.tensor_scalar(angle[:, 2], angle[:, 1], turn, None, ALU.add))
            link(nc.vector.tensor_scalar(angle[:, 1], angle[:, 2], -turn, None, ALU.add))
            for q in (part1, part2, part3):
                link(nc.vector.scalar_tensor_tensor(out=angle[:, 0], in0=angle[:, 1], scalar=-q, in1=angle[:, 0],
                                                    op0=ALU.mult, op1=ALU.add))
            link(nc.vector.tensor_scalar(angle[:, 0, :, 0, :], angle[:, 0, :, 0, :], float(np.pi / 2), None, ALU.add))
            limit = float(np.nextafter(np.float32(np.pi), np.float32(0)))
            nc.vector.tensor_scalar(angle[:, 0], angle[:, 0], limit, -limit, ALU.min, ALU.max) \
                .then_inc(angles_ready.sem, 1)

            def mean_squares(l, n, outs):
                for k, (dst, src, width) in enumerate(outs):
                    ins = nc.vector.tensor_scalar(dst, src, 1.0 / width, EPS, ALU.mult, ALU.add)
                ins.then_inc(ms_ready.sem, 1)
                ve.wait_ge(*rstd_ready(l, n))

            def norm_x(l, which):
                ve.wait_ge(*x_squares(l, which + 1))
                mean_squares(l, 5 if which else 1, [(mean_sq[:, 0:T], sumsq[:, :, 0], D)])
                for t in range(T):
                    ins = nc.vector.tensor_scalar(xn[:, t, :], x_sb[:, t, :], rstd[:, t:t + 1], None, ALU.mult)
                ins.then_inc(xn_ready.sem, 1)

            def add_bias(s, bank):
                ve.wait_ge(*ada_sums(0, 4 * s + 4))
                ve.wait_ge(bias_loaded[s % 2].sem, 64 * (s // 2 + 1))
                if s:
                    ve.wait_ge(*ada_turned(0, s))
                    if s % 3 == 0:
                        ve.wait_ge(*gate_ready(s // 3 - 1, 2))
                    elif s % 3 == 2:
                        ve.wait_ge(*gate_ready(s // 3, 1))
                nc.vector.tensor_tensor(ada_row[:, :], psum[:, bank, :], ada_bias[:, s % 2, :], ALU.add) \
                    .then_inc(ada_row_ready.sem, 1)

            def gains(s):
                l, k = divmod(s, 3)
                ve.wait_ge(*mod_ready(0, s + 1))
                which = 0 if k == 0 else 1
                nc.vector.scalar_tensor_tensor(out=gain[:, l % 2, which, :], in0=sc_of(l, which), scalar=1.0,
                                               in1=col("g_ffn" if which else "g_mix", l, 0, C),
                                               op0=ALU.add, op1=ALU.mult).then_inc(gain_ready.sem, 1)
                ve.wait_ge(*gain_ready(l, which + 1))

            def modulate_half(l, which):
                for b in range(2, 4):
                    ve.wait_ge(*xnT_ready(l, 4 * which + b + 1))
                    for k in range(2):
                        q = 2 * b + k
                        ins = nc.vector.tensor_scalar(hT[:, q, :], psum[:, 3 + b, k * S:(k + 1) * S],
                                                      gain[:, l % 2, which, q:q + 1], sh_of(l, which)[:, q:q + 1],
                                                      ALU.mult, ALU.add)
                ins.then_inc(hT_dve.sem, 1)

            norm_x(0, 0)
            add_bias(0, 7)
            gains(0)

            for l in range(L):
                if l:
                    norm_x(l, 0)
                modulate_half(l, 0)

                ve.wait_ge(*lat_squares(l, T))
                mean_squares(l, 2, [(mean_sq[:, 0:T], sumsq[:, :, 0], QR), (mean_sq[:, T:2 * T], sumsq[:, :, 1], KR)])
                for t in range(T):
                    nc.vector.tensor_scalar(lat_n[:, t, 0:QR], psum[:, 2 + t, 0:QR], rstd[:, t:t + 1], None, ALU.mult)
                    nc.vector.tensor_scalar(lat_n[:, t, QR:], psum[:, 2 + t, QR:QR + KR], rstd[:, T + t:T + t + 1],
                                            None, ALU.mult)
                    nc.vector.tensor_copy(qk[:, t, 1, :, ND:],
                                          psum[:, 2 + t, QR + KR:LAT].unsqueeze(1).broadcast_to([P, NH, RD])) \
                        .then_inc(lat_ready.sem, 1)

                nc.vector.memset(u[:, :, 0:1], 0.0)
                nc.vector.memset(u[:, :, S + 1:S + 2], 0.0)
                for j in range(2):
                    ve.wait_ge(*cc_ready(l, j + 1))
                    ve.wait_ge(*unit_psum(l, 2 * j + 2))
                    nc.vector.tensor_tensor(u[:, 2 * j:2 * j + 2, 1:S + 1],
                                            psum[:, 1, :].rearrange("p (c s) -> p c s", c=2),
                                            cc_tmp[:, j, :].rearrange("p (c s) -> p c s", c=2), ALU.mult) \
                        .then_inc(u_ready.sem, 1)
                ve.wait_ge(*u_ready(l, 2))
                for k in range(3):
                    for m in range(NB):
                        w = col("conv", l, k * NB + m)
                        if k == 0:
                            ins = nc.vector.tensor_scalar(yc[:, m, :], u[:, m, 0:S], w, None, ALU.mult)
                        else:
                            ins = nc.vector.scalar_tensor_tensor(out=yc[:, m, :], in0=u[:, m, k:k + S], scalar=w,
                                                                 in1=yc[:, m, :], op0=ALU.mult, op1=ALU.add)
                    link(ins)
                for j in range(2):
                    ve.wait_ge(*unit_psum(l, 5 + j))
                    nc.vector.tensor_tensor(yc[:, 2 * j:2 * j + 2, :], psum[:, j, :].rearrange("p (c s) -> p c s", c=2),
                                            yc[:, 2 * j:2 * j + 2, :], ALU.mult).then_inc(conv_ready.sem, 1)

                for t in range(T):
                    ve.wait_ge(*qk_squares(l, t + 1))
                    link(nc.vector.tensor_reduce(rstd[:, :], sq[:, :, :], AX.X, ALU.add))
                    mean_squares(l, 3 + t, [(mean_sq[:, :], rstd[:, :], DH)])
                    flat = qk[:, t].rearrange("p a h d -> p (a h) d")
                    link(nc.vector.tensor_tensor(flat, flat, rstd[:, :].unsqueeze(2).broadcast_to([P, 2 * NH, DH]),
                                                 ALU.mult))
                    for a in range(2):
                        ins = nc.vector.tensor_tensor(qk[:, t, a], qk[:, t, a],
                                                      head_gain[:, l, a, :].unsqueeze(1).broadcast_to([P, NH, DH]),
                                                      ALU.mult)
                    link(ins)
                    if l == 0 and t == 0:
                        ve.wait_ge(*rope_ready(0))
                    x1, x2 = flat[:, :, ND:ND + HALF], flat[:, :, ND + HALF:]
                    cos, sin = (cos_sin[:, t, k, :].unsqueeze(1).broadcast_to([P, 2 * NH, HALF]) for k in range(2))
                    tmp = [rot_tmp[:, k] for k in range(4)]
                    for dst, a, b in ((tmp[0], x1, cos), (tmp[1], x2, sin), (tmp[2], x2, cos), (tmp[3], x1, sin)):
                        ins = nc.vector.tensor_tensor(dst, a, b, ALU.mult)
                    link(ins)
                    nc.vector.tensor_tensor(x1, tmp[0], tmp[1], ALU.subtract)
                    nc.vector.tensor_tensor(x2, tmp[2], tmp[3], ALU.add).then_inc(qk_ready.sem, 1)

                def gate_a(j):
                    ve.wait_ge(*ga_tanh(l, j + 1))
                    ve.wait_ge(*ya_ready(l, j + 1))
                    m = merged[:, 2 * j:2 * j + 2, :].rearrange("p c s -> p (c s)")
                    nc.vector.scalar_tensor_tensor(out=m, in0=tanh_a[:, j % 2, :], scalar=1.0, in1=m,
                                                   op0=ALU.add, op1=ALU.mult).then_inc(ga_used.sem, 1)

                def copy_oT(j):
                    ve.wait_ge(*pv_psum(l, 2 * j + 2))
                    nc.vector.tensor_copy(oT[:, j, :], psum[:, 7, 0:S]).then_inc(oT_ready.sem, 1)

                gate_a(0)
                for h in range(NH):
                    ve.wait_ge(*scores_psum(l, h + 1))
                    link(nc.vector.tensor_reduce(top[:, h % 2, :], psum[:, 4 + h % 2, :].rearrange("p (t s) -> p t s", t=T),
                                                 AX.X, ALU.max))
                    nc.vector.tensor_scalar(bias_m[:, h % 2, :], top[:, h % 2, :], -SCALE, None, ALU.mult) \
                        .then_inc(bias_ready.sem, 1)
                    ve.wait_ge(*exp_done(l, h + 1))
                    link(nc.vector.reciprocal(denom[:, h % 2, :], denom[:, h % 2, :]))
                    for t in range(T):
                        ins = nc.vector.tensor_scalar(probs[:, h % 2, t, :], probs[:, h % 2, t, :],
                                                      denom[:, h % 2, t:t + 1], None, ALU.mult)
                    ins.then_inc(probs_ready.sem, 1)
                    if h < 3:
                        gate_a(1 + h)
                    if h == 3:
                        add_bias(3 * l + 1, 3)
                    if h >= 2 and h % 2 == 0:
                        copy_oT(h // 2 - 1)
                add_bias(3 * l + 2, 3)
                copy_oT(NH // 2 - 1)
                gains(3 * l + 2)

                for j in range(4):
                    ve.wait_ge(*unit_psum(l, 19 + j))
                    ve.wait_ge(*gb_tanh(l, j + 1))
                    nc.vector.scalar_tensor_tensor(out=cc_tmp[:, j % 2, :],
                                                   in0=tanh_b[:, 2 * j:2 * j + 2, :].rearrange("p c s -> p (c s)"),
                                                   scalar=1.0, in1=psum[:, j % 2, :], op0=ALU.add, op1=ALU.mult) \
                        .then_inc(yb_gated.sem, 1)
                    ve.wait_ge(*yb_gated(l, j + 1))
                    m = merged[:, 2 * j:2 * j + 2, :].rearrange("p c s -> p (c s)")
                    nc.vector.scalar_tensor_tensor(out=m, in0=cc_tmp[:, j % 2, :], scalar=0.5, in1=m,
                                                   op0=ALU.mult, op1=ALU.add).then_inc(merged_ready.sem, 1)

                def add_gated(which, sig, order, done):
                    ve.wait_ge(*gate_ready(l, which + 1))
                    for n, (t, half) in enumerate(order):
                        if sig is mix_psum:
                            ve.wait_ge(*sig(l, n + 1))
                        tmp = cc_tmp[:, n % 2, :]
                        xs = x_sb[:, t, half * BANK:(half + 1) * BANK]
                        link(nc.vector.tensor_tensor(tmp, psum[:, 2 * t + half, :],
                                                     gate_rows[:, which, half * BANK:(half + 1) * BANK], ALU.mult))
                        ins = nc.vector.tensor_tensor(xs, xs, tmp, ALU.add)
                    ins.then_inc(done.sem, 1)

                add_gated(0, mix_psum, [(t, h) for h in range(2) for t in range(T)], mix_added)

                norm_x(l, 1)
                if l + 1 < L:
                    add_bias(3 * l + 3, 7)
                modulate_half(l, 1)

                if l + 1 < L:
                    gains(3 * l + 3)
                ve.wait_ge(*router_exp(l))
                R = lambda k: r_small[:, k, :]
                link(nc.vector.tensor_scalar(R(1), R(0), 1.0, None, ALU.add))
                link(nc.vector.reciprocal(R(2), R(1)))
                link(nc.vector.tensor_tensor(R(3).rearrange("p (t e) -> p t e", t=T),
                                             R(2).rearrange("p (t e) -> p t e", t=T),
                                             b_router_sb[:, :].unsqueeze(1).broadcast_to([P, T, E]), ALU.add))

                def first_ranks(values, groups, n, rank):
                    full = [P, groups, n, n]
                    v = values.rearrange("p (g i) -> p g i", i=n)
                    vi, vj = v.unsqueeze(3).broadcast_to(full), v.unsqueeze(2).broadcast_to(full)
                    low = lower[:, :, :].unsqueeze(1).broadcast_to(full)
                    a, b, d = (pairwise[:, k, 0:groups] for k in range(3))
                    nc.vector.tensor_tensor(a, vj, vi, ALU.is_gt)
                    link(nc.vector.tensor_tensor(b, vj, vi, ALU.is_equal))
                    link(nc.vector.tensor_tensor(d, b, low, ALU.mult))
                    link(nc.vector.tensor_tensor(b, a, d, ALU.add))
                    link(nc.vector.tensor_reduce(rank.rearrange("p (g i) -> p g i", i=n), b, AX.X, ALU.add))

                first_ranks(R(3), T * GRP, EPG, R(4))
                link(nc.vector.tensor_scalar(R(5), R(4), 2.0, None, ALU.is_lt))
                link(nc.vector.tensor_tensor(R(6), R(5), R(3), ALU.mult))
                sums = R(7)[:, 0:T * GRP]
                link(nc.vector.tensor_reduce(sums, R(6).rearrange("p (g i) -> p g i", i=EPG), AX.X, ALU.add))
                g_rank, g_sel = R(8)[:, 0:T * GRP], R(9)[:, 0:T * GRP]
                first_ranks(sums, T, GRP, g_rank)
                link(nc.vector.tensor_scalar(g_sel, g_rank, 1.0, None, ALU.is_lt))
                sel = R(10)
                link(nc.vector.tensor_tensor(sel.rearrange("p (g i) -> p g i", i=EPG),
                                             R(5).rearrange("p (g i) -> p g i", i=EPG),
                                             g_sel.unsqueeze(2).broadcast_to([P, T * GRP, EPG]), ALU.mult))
                nc.vector.tensor_copy(sel_b[:, :, :].rearrange("p t e -> p (t e)"), sel).then_inc(chosen.sem, 1)
                link(nc.vector.tensor_tensor(R(6), sel, R(2), ALU.mult))
                link(nc.vector.tensor_reduce(R(7)[:, 0:T], R(6).rearrange("p (t e) -> p t e", t=T), AX.X, ALU.add))
                link(nc.vector.reciprocal(R(7)[:, 0:T], R(7)[:, 0:T]))
                link(nc.vector.tensor_tensor(combine[:, :, :], R(6).rearrange("p (t e) -> p t e", t=T),
                                             R(7)[:, 0:T].unsqueeze(2).broadcast_to([P, T, E]), ALU.mult))

                ve.wait_ge(*rank_psum(l))
                link(nc.vector.scalar_tensor_tensor(out=slot_of[:, :, :], in0=sel.rearrange("p (t e) -> p t e", t=T),
                                                    scalar=float(-2 * S),
                                                    in1=psum[:, 7, 0:T * E].rearrange("p (t e) -> p t e", t=T),
                                                    op0=ALU.mult, op1=ALU.add))
                nc.vector.tensor_copy(lengths[:, :], psum[:, 7, T * E:(T + 1) * E]).then_inc(ranks_read.sem, 1)
                for t in range(T):
                    ins = nc.vector.tensor_tensor(onehot[:, t], slot_id[:, :].unsqueeze(1).broadcast_to([P, E, SLOTS]),
                                                  slot_of[:, t, :].unsqueeze(2).broadcast_to([P, E, SLOTS]),
                                                  ALU.is_equal)
                ins.then_inc(onehot_ready.sem, 1)
                ve.wait_ge(*s_tanh_ready(l))
                ve.wait_ge(*s_up_psum(l))
                flat_act = s_act.rearrange("p c s -> p (c s)")
                link(nc.vector.scalar_tensor_tensor(out=flat_act, in0=s_tanh.rearrange("p c s -> p (c s)"), scalar=1.0,
                                                    in1=psum[:, 4, :], op0=ALU.add, op1=ALU.mult))
                nc.vector.scalar_tensor_tensor(out=flat_act, in0=flat_act, scalar=0.5, in1=psum[:, 5, :],
                                               op0=ALU.mult, op1=ALU.mult).then_inc(s_act_ready.sem, 1)
                ve.wait_ge(*onehot_ready(l))
                for t in range(T):
                    ins = nc.vector.tensor_tensor(weighted[:, t], onehot[:, t],
                                                  combine[:, t, :].unsqueeze(2).broadcast_to([P, E, SLOTS]), ALU.mult)
                ins.then_inc(weighted_ready.sem, 1)

                for n in range(1, 2 * C, 2):
                    half, q = divmod(n, C)
                    ve.wait_ge(*gather_psum(l, n + 1))
                    nc.vector.tensor_scalar(hE[:, q, half * 8:half * 8 + 8, :].rearrange("p e s -> p (e s)"),
                                            psum[:, 4 + n % 4, :], gain[:, l % 2, 1, q:q + 1],
                                            sh_of(l, 1)[:, q:q + 1], ALU.mult, ALU.add).then_inc(hE_dve.sem, 1)
                for b in range(1, 4, 2):
                    ve.wait_ge(*combT_psum(l, b + 1))
                    nc.vector.tensor_copy(combT[:, 2 * b:2 * b + 2, :].rearrange("p j s -> p (j s)"),
                                          psum[:, 4 + b, :]).then_inc(combT_dve.sem, 1)

                def list_extras():
                    f3 = flags.rearrange("p (e g) -> p e g", e=E)
                    link(nc.vector.tensor_scalar(lengths[:, :], lengths[:, :], 1.0 / SLOTS, None, ALU.mult))
                    for k in range(2):
                        nc.vector.memset(run_sums[k][:, 0:LEAD], 0.0)
                    link(nc.vector.tensor_tensor(f3, lengths[:, :].unsqueeze(2).broadcast_to([P, E, GROUPS - 1]),
                                                 count_up[:, 1:GROUPS].unsqueeze(1).broadcast_to([P, E, GROUPS - 1]),
                                                 ALU.is_gt))
                    link(nc.vector.tensor_copy(run_sums[0][:, LEAD:], flags))
                    a, b, shift = run_sums[0], run_sums[1], 1
                    while shift < NF:
                        link(nc.vector.tensor_tensor(b[:, LEAD:], a[:, LEAD:], a[:, LEAD - shift:LEAD - shift + NF],
                                                     ALU.add))
                        a, b, shift = b, a, 2 * shift
                    full = [P, EXTRAS, E, GROUPS - 1]
                    m = match.rearrange("p k e g -> p k (e g)")
                    link(nc.vector.tensor_tensor(m, a[:, LEAD:].unsqueeze(1).broadcast_to([P, EXTRAS, NF]),
                                                 count_up[:, 1:EXTRAS + 1].unsqueeze(2).broadcast_to([P, EXTRAS, NF]),
                                                 ALU.is_equal))
                    link(nc.vector.tensor_tensor(m, m, flags.unsqueeze(1).broadcast_to([P, EXTRAS, NF]), ALU.mult))
                    nc.vector.tensor_reduce(is_expert, match, AX.X, ALU.add)
                    link(nc.vector.tensor_reduce(is_group, match.rearrange("p k e g -> p k g e"), AX.X, ALU.add))
                    nc.vector.tensor_tensor(is_group, is_group,
                                            count_up[:, 1:GROUPS].unsqueeze(1).broadcast_to([P, EXTRAS, GROUPS - 1]),
                                            ALU.mult)
                    link(nc.vector.tensor_tensor(scratch_e, is_expert,
                                                 count_up[:, 0:E].unsqueeze(1).broadcast_to([P, EXTRAS, E]), ALU.mult))
                    nc.vector.tensor_reduce(group_of, is_group, AX.X, ALU.add)
                    link(nc.vector.tensor_reduce(expert_f, scratch_e, AX.X, ALU.add))
                    nc.vector.tensor_copy(extra_expert[:, :], expert_f)
                    for src, dst in ((slot_of, slot_x), (combine, combine_x)):
                        for t in range(T):
                            link(nc.vector.tensor_tensor(scratch_e, is_expert,
                                                         src[:, t, :].unsqueeze(1).broadcast_to([P, EXTRAS, E]),
                                                         ALU.mult))
                            link(nc.vector.tensor_reduce(dst[:, t, :], scratch_e, AX.X, ALU.add))
                    link(nc.vector.tensor_scalar(group_of, group_of, float(-SLOTS), None, ALU.mult))
                    link(nc.vector.tensor_tensor(slot_x[:, :, :], slot_x[:, :, :],
                                                 group_of.unsqueeze(1).broadcast_to([P, T, EXTRAS]), ALU.add))
                    n_listed = a[:, LEAD + NF - 1:LEAD + NF]
                    nc.vector.tensor_copy(passes_before[:, :], passes_f[:, 0:1])
                    link(nc.vector.tensor_scalar(passes_f[:, 2:], count_up[:, 0:EXTRAS:2], n_listed, None, ALU.is_lt))
                    link(nc.vector.tensor_reduce(passes_f[:, 1:2], passes_f[:, 2:], AX.X, ALU.add))
                    link(nc.vector.tensor_tensor(passes_f[:, 0:1], passes_f[:, 0:1], passes_f[:, 1:2], ALU.add))
                    nc.vector.tensor_copy(n_extras[:, :], n_listed) \
                        .then_inc(extras_ready.sem, 1)

                for i in range(PAIRS + 1):
                    if i == 2:
                        list_extras()
                    if i < PAIRS:
                        ve.wait_ge(*tanh_ready(l, i + 1))
                        a = e_act[:, i % 2, :]
                        link(nc.vector.scalar_tensor_tensor(out=a, in0=e_tanh[:, i % 2, :], scalar=1.0,
                                                            in1=psum[:, 4 + i % 2, 0:F], op0=ALU.add, op1=ALU.mult))
                        nc.vector.scalar_tensor_tensor(out=a, in0=a, scalar=0.5, in1=psum[:, 4 + i % 2, F:2 * F],
                                                       op0=ALU.mult, op1=ALU.mult).then_inc(act_ready.sem, 1)
                    if i >= 1:
                        ve.wait_ge(*down_psum(l, 2 * i))
                        nc.vector.tensor_copy(y[:, BANK:], psum[:, 6, :]).then_inc(y_dve.sem, 1)

                ve.wait_ge(*extras_ready(l))
                listed = ve.value_load(n_extras[0:1, 0:1], min_val=0, max_val=EXTRAS)
                before = ve.value_load(passes_before[0:1, 0:1], min_val=0, max_val=L * ITERS)
                with ve.Fori(0, ITERS) as j:
                    with ve.If(listed > 2 * j):
                        for t in range(T):
                            for k in range(2):
                                ins = nc.vector.tensor_scalar(onehot_x[:, t, k, :], slot_id[:, :],
                                                              slot_x[:, t, bass.ds(2 * j + k, 1)], None, ALU.is_equal)
                        ins.then_inc(x_onehot.sem, 1)
                        ve.wait_ge(x_onehot.sem, j + before + 1)
                        for t in range(T):
                            for k in range(2):
                                ins = nc.vector.tensor_scalar(weighted_x[:, t, k, :], onehot_x[:, t, k, :],
                                                              combine_x[:, t, bass.ds(2 * j + k, 1)], None, ALU.mult)
                        ins.then_inc(x_weighted.sem, 1)
                        ve.wait_ge(x_gathered.sem, j + before + 1)
                        for q in range(1, C, 2):
                            ins = nc.vector.tensor_scalar(hE[:, q, 0:2, :].rearrange("p e s -> p (e s)"),
                                                          psum[:, 4 + q % 2, (q // 2) * P:(q // 2 + 1) * P],
                                                          gain[:, l % 2, 1, q:q + 1], sh_of(l, 1)[:, q:q + 1],
                                                          ALU.mult, ALU.add)
                        ins.then_inc(x_tokens_dve.sem, 1)
                        ve.wait_ge(x_tanh.sem, j + before + 1)
                        nc.vector.scalar_tensor_tensor(out=e_act[:, 0, :], in0=e_tanh[:, 0, :], scalar=1.0,
                                                       in1=psum[:, 7, 0:F], op0=ALU.add, op1=ALU.mult) \
                            .then_inc(x_act1.sem, 1)
                        ve.wait_ge(x_act1.sem, j + before + 1)
                        nc.vector.scalar_tensor_tensor(out=e_act[:, 0, :], in0=e_act[:, 0, :], scalar=0.5,
                                                       in1=psum[:, 7, F:2 * F], op0=ALU.mult, op1=ALU.mult) \
                            .then_inc(x_act.sem, 1)
                        ve.wait_ge(x_down.sem, j + before + 1)
                        nc.vector.tensor_copy(y[:, BANK:], psum[:, 5, :]).then_inc(x_y_dve.sem, 1)

                ve.wait_ge(*moe_psum(l))
                add_gated(1, moe_psum, [(t, h) for t in range(T) for h in range(2)], moe_added)

        @block.tensor
        def _(pe):
            def turn(dst, src):
                return nc.tensor.transpose(dst, src, ident[0:src.shape[0], 0:src.shape[0]])

            def ada_products(s, bank, parts=range(4)):
                for i in parts:
                    pe.wait_ge(*loaded(("ada", s, i)))
                    w = slot(("ada", s, i), 2)
                    for k in range(2):
                        q = 2 * i + k
                        for j in range(4):
                            ins = nc.tensor.matmul(psum[32 * j:32 * j + 32, bank, :], c_act[:, q, :],
                                                   w[:, k, j * BANK:(j + 1) * BANK], start=q == 0, stop=q == C - 1)
                    ins.then_inc(ada_sums.sem, 1)

            def ada_turn(s, bank):
                pe.wait_ge(*ada_row_ready(0, s + 1))
                for b in range(4):
                    ins = turn(psum[:, bank, b * P:(b + 1) * P], ada_row[:, b * P:(b + 1) * P])
                ins.then_inc(ada_turned.sem, 1)

            def turn_x(l, which):
                pe.wait_ge(*xn_ready(l, which + 1))
                for b in range(4):
                    for k in range(2):
                        for t in range(T):
                            q = 2 * b + k
                            ins = turn(psum[:, 3 + b, k * S + t * P:k * S + (t + 1) * P], xn[:, t, q * P:(q + 1) * P])
                    ins.then_inc(xnT_ready.sem, 1)

            def unit(l, n, w, src, k, a):
                b = n % 2
                if n >= 2:
                    pe.wait_ge(*bank_emptied(l, n))
                for m in range(2):
                    for q in range(k):
                        ins = nc.tensor.matmul(psum[:, b, m * S:(m + 1) * S], w[:, q, a + m * P:a + (m + 1) * P],
                                               src[:, q, :], start=q == 0, stop=q == k - 1)
                ins.then_inc(unit_psum.sem, 1)

            def bank_emptied(l, n):
                p = n - 2
                if p in (0, 2):
                    return cc_ready(l, p // 2 + 1)
                if p in (1, 3):
                    return u_ready(l, p // 2 + 1)
                if p in (4, 5):
                    return conv_ready(l, p - 3)
                if p < 10:
                    return ya_ready(l, p - 5)
                if p < 14:
                    return ga_tanh(l, p - 9)
                if p < 18:
                    return gb_tanh(l, p - 13)
                return yb_gated(l, p - 17)

            pe.wait_ge(*consts(0, 6))
            pe.wait_ge(params_loaded.sem, 16 * (7 * L + 3 + T))
            turn(psum[:, 6, 0:NROWS], rows[0:NROWS, :]).then_inc(cols_psum.sem, 1)
            pe.wait_ge(*c_ready(0))
            ada_products(0, 7)
            ada_turn(0, 7)

            for l in range(L):
                turn_x(l, 0)

                pe.wait_ge(*hT_act(l, 1))
                pe.wait_ge(*hT_dve(l, 1))
                pe.wait_ge(*loaded(("lat", l)))
                w = slot(("lat", l), C)
                for t in range(T):
                    for q in range(C):
                        ins = nc.tensor.matmul(psum[:, 2 + t, 0:LAT], hT[:, q, t * P:(t + 1) * P], w[:, q, 0:LAT],
                                               start=q == 0, stop=q == C - 1)
                    ins.then_inc(lat_psum.sem, 1)

                def conv_unit(n, key, a):
                    pe.wait_ge(*loaded((key, l)))
                    unit(l, n, slot((key, l), C), hT, C, a)

                conv_unit(0, "cc", 0)
                conv_unit(1, "cx", 0)
                for t in range(T):
                    pe.wait_ge(*lat_ready(l, t + 1))
                    for b in range(QB + 1):
                        ins = turn(psum[:, 4 + t, b * P:(b + 1) * P], lat_n[:, t, b * P:(b + 1) * P])
                    ins.then_inc(latT_psum.sem, 1)
                conv_unit(2, "cc", S)
                conv_unit(3, "cx", S)

                def up_q(t, bank):
                    for a, n in ((0, BANK), (BANK, NH * DH - BANK)):
                        for q in range(QB):
                            ins = nc.tensor.matmul(psum[:, bank + a // BANK, 0:n], latT[:, q, t * P:(t + 1) * P],
                                                   uq_sb[:, q, a:a + n], start=q == 0, stop=q == QB - 1)
                    ins.then_inc(up_psum.sem, 1)

                def up_kv(t, bank):
                    for a in range(2):
                        ins = nc.tensor.matmul(psum[:, bank + a, :], latT[:, QB, t * P:(t + 1) * P],
                                               ukv_sb[:, a * BANK:(a + 1) * BANK], start=True, stop=True)
                    ins.then_inc(up_psum.sem, 1)

                pe.wait_ge(*latT_ready(l, T))
                pe.wait_ge(latw_loaded.sem, 32 * (l + 1))
                up_q(0, 2)
                up_kv(0, 4)
                up_q(1, 6)
                conv_unit(4, "cb", 0)
                pe.wait_ge(*qkv_copied(l, 1))
                up_kv(1, 2)
                conv_unit(5, "cb", S)

                pe.wait_ge(*loaded(("conv", l)))
                pe.wait_ge(*conv_ready(l, 2))
                for j in range(4):
                    unit(l, 6 + j, slot(("conv", l), NB), yc, NB, j * S)

                def gate_unit(n):
                    key = ("ga%d" if n < 14 else "gb%d") % ((n - 10) % 4 // 2)
                    pe.wait_ge(*loaded((key, l)))
                    unit(l, n, slot((key, l), C), hT, C, (n % 2) * S)

                def turn_qk(h):
                    if h:
                        pe.wait_ge(*qkT_ready(l, h))
                    for a in range(2):
                        for t in range(T):
                            ins = turn(psum[0:DH, 2, a * S + t * P:a * S + (t + 1) * P], qk[:, t, a, h, :])
                    ins.then_inc(qkT_psum.sem, 1)

                def turn_probs(h):
                    pe.wait_ge(*probs_ready(l, h + 1))
                    if h:
                        pe.wait_ge(*pT_ready(l, h))
                    for k in range(T):
                        for t in range(T):
                            ins = turn(psum[:, 6, k * S + t * P:k * S + (t + 1) * P],
                                       probs[:, h % 2, t, k * P:(k + 1) * P])
                    ins.then_inc(pT_psum.sem, 1)

                def apply_probs(h):
                    pe.wait_ge(*pT_ready(l, h + 1))
                    if h >= 2 and h % 2 == 0:
                        pe.wait_ge(*oT_ready(l, h // 2))
                    a = (h % 2) * VD
                    for k in range(T):
                        ins = nc.tensor.matmul(psum[a:a + VD, 7, 0:S], v_sb[:, k, h, :], probsT[:, h % 2, k, :],
                                               start=k == 0, stop=k == T - 1)
                    ins.then_inc(pv_psum.sem, 1)

                gate_unit(10)
                pe.wait_ge(*qk_ready(l, T))
                pe.wait_ge(*qkv_copied(l, 4))
                turn_qk(0)
                for h in range(NH):
                    if h + 1 < NH:
                        turn_qk(h + 1)
                    pe.wait_ge(*qkT_ready(l, h + 1))
                    if h >= 2:
                        pe.wait_ge(*exp_done(l, h - 1))
                    for t in range(T):
                        ins = nc.tensor.matmul(psum[:, 4 + h % 2, t * S:(t + 1) * S],
                                               qkT[0:DH, h % 2, 0, t * P:(t + 1) * P], qkT[0:DH, h % 2, 1, :],
                                               start=True, stop=True)
                    ins.then_inc(scores_psum.sem, 1)
                    if h < 7:
                        gate_unit(11 + h)
                    if h < 4:
                        ada_products(3 * l + 1, 3, [h])
                    elif h == 4:
                        ada_turn(3 * l + 1, 3)
                    else:
                        if h == 5:
                            pe.wait_ge(*mod_ready(0, 3 * l + 2))
                        ada_products(3 * l + 2, 3, [h - 5] if h < 7 else [2, 3])
                    turn_probs(h)
                    if h:
                        apply_probs(h - 1)
                ada_turn(3 * l + 2, 3)
                apply_probs(NH - 1)

                pe.wait_ge(*oT_ready(l, NH // 2))
                pe.wait_ge(*loaded(("attn", l)))
                for j in range(4):
                    unit(l, 18 + j, slot(("attn", l), NB), oT, NB, j * S)

                pe.wait_ge(*merged_ready(l, 4))
                pe.wait_ge(*mod_ready(0, 3 * l + 3))
                for half in range(2):
                    pe.wait_ge(*loaded((f"wo{half}", l)))
                    w = slot((f"wo{half}", l), C)
                    for t in range(T):
                        for q in range(C):
                            ins = nc.tensor.matmul(psum[:, 2 * t + half, :], merged[:, q, t * P:(t + 1) * P], w[:, q, :],
                                                   start=q == 0, stop=q == C - 1)
                        ins.then_inc(mix_psum.sem, 1)

                if l + 1 < L:
                    ada_products(3 * l + 3, 7)
                turn_x(l, 1)
                if l + 1 < L:
                    ada_turn(3 * l + 3, 7)
                pe.wait_ge(*hT_act(l, 2))
                pe.wait_ge(*hT_dve(l, 2))
                for q in range(C):
                    ins = nc.tensor.matmul(psum[0:E, 5, 0:S], router_sb[:, q, :], hT[:, q, :], start=q == 0,
                                           stop=q == C - 1)
                ins.then_inc(router_psum.sem, 1)
                pe.wait_ge(*loaded(("shared", l)))
                w = slot(("shared", l), C)

                def shared_block(m, bank, sig=None):
                    for q in range(C):
                        ins = nc.tensor.matmul(psum[:, bank, (m % FC) * S:(m % FC + 1) * S], w[:, q, m * P:(m + 1) * P],
                                               hT[:, q, :], start=q == 0, stop=q == C - 1)
                    if sig:
                        ins.then_inc(sig.sem, 1)

                shared_block(0, 4)
                pe.wait_ge(*router_copied(l))
                for t in range(T):
                    ins = turn(psum[:, 6, t * E:(t + 1) * E], router_out[0:E, t * P:(t + 1) * P])
                ins.then_inc(routerT_psum.sem, 1)
                shared_block(1, 4, s_gate_psum)
                shared_block(2, 5)
                pe.wait_ge(*chosen(l))
                if l + 1 < L:
                    pe.wait_ge(*mod_ready(0, 3 * l + 4))
                nc.tensor.matmul(psum[:, 7, 0:E], tri[:, :], sel_b[:, 0, :], start=True, stop=True)
                nc.tensor.matmul(psum[:, 7, E:2 * E], ones[:, :], sel_b[:, 0, :], start=True, stop=False)
                nc.tensor.matmul(psum[:, 7, E:2 * E], tri[:, :], sel_b[:, 1, :], start=False, stop=True)
                nc.tensor.matmul(psum[:, 7, 2 * E:3 * E], ones[:, :], sel_b[:, 0, :], start=True, stop=False)
                nc.tensor.matmul(psum[:, 7, 2 * E:3 * E], ones[:, :], sel_b[:, 1, :], start=False, stop=True) \
                    .then_inc(rank_psum.sem, 1)
                shared_block(3, 5, s_up_psum)
                pe.wait_ge(*s_act_ready(l))
                pe.wait_ge(sdown_loaded.sem, 16 * (l + 1))
                for t in range(T):
                    for half in range(2):
                        for q in range(FC):
                            ins = nc.tensor.matmul(psum[:, 2 * t + half, :], s_act[:, q, t * P:(t + 1) * P],
                                                   sdown_sb[:, q, half * BANK:(half + 1) * BANK],
                                                   start=q == 0, stop=False)
                ins.then_inc(s_down_psum.sem, 1)

                pe.wait_ge(*onehot_ready(l))
                pe.wait_ge(*ranks_read(l))
                for n in range(2 * C):
                    half, q = divmod(n, C)
                    if n >= 4:
                        pe.wait_ge(*(hE_act if n % 2 == 0 else hE_dve)(l, (n - 4) // 2 + 1))
                    for t in range(T):
                        ins = nc.tensor.matmul(psum[:, 4 + n % 4, :], xn[:, t, q * P:(q + 1) * P],
                                               onehot[:, t, half * 8:half * 8 + 8, :].rearrange("p e s -> p (e s)"),
                                               start=t == 0, stop=t == T - 1)
                    ins.then_inc(gather_psum.sem, 1)
                pe.wait_ge(*weighted_ready(l))
                for b in range(4):
                    pe.wait_ge(*(hE_act if b % 2 == 0 else hE_dve)(l, (2 * C - 4 + b) // 2 + 1))
                    for k in range(2):
                        for t in range(T):
                            j = 2 * b + k
                            ins = turn(psum[:, 4 + b, k * S + t * P:k * S + (t + 1) * P],
                                       weighted[:, t, 2 * j:2 * j + 2, :].rearrange("p e s -> p (e s)"))
                    ins.then_inc(combT_psum.sem, 1)

                def gate_up(i):
                    pe.wait_ge(*loaded(("gu", l, 2 * i)))
                    pe.wait_ge(*loaded(("gu", l, 2 * i + 1)))
                    if i >= 2:
                        pe.wait_ge(*act_ready(l, i - 1))
                    elif i == 0:
                        pe.wait_ge(*combT_act(l, 2))
                        pe.wait_ge(*combT_dve(l, 2))
                    for q in range(C):
                        for k in range(2):
                            ins = nc.tensor.matmul(psum[k * SLOTS:(k + 1) * SLOTS, 4 + i % 2, :], hE[:, q, 2 * i + k, :],
                                                   slot(("gu", l, 2 * i + k), C)[:, q, :], start=q == 0,
                                                   stop=q == C - 1)
                    ins.then_inc(gu_psum.sem, 1)

                def turn_act(i):
                    pe.wait_ge(*act_ready(l, i + 1))
                    if i:
                        pe.wait_ge(*y_dve(l, i))
                    for q in range(FC):
                        ins = turn(psum[:, 6, q * P:(q + 1) * P], e_act[:, i % 2, q * P:(q + 1) * P])
                    ins.then_inc(aT_psum.sem, 1)

                def down(i):
                    pe.wait_ge(*loaded(("down", l, i)))
                    pe.wait_ge(*aT_ready(l, i + 1))
                    w = slot(("down", l, i), 2 * FC)
                    if i:
                        pe.wait_ge(*y_act(l, i))
                    for half in range(2):
                        for q in range(FC):
                            for k in range(2):
                                ins = nc.tensor.matmul(psum[k * SLOTS:(k + 1) * SLOTS, 7 - half, :],
                                                       aT[:, q, k * SLOTS:(k + 1) * SLOTS],
                                                       w[:, k * FC + q, half * BANK:(half + 1) * BANK],
                                                       start=q == 0, stop=q == FC - 1)
                        ins.then_inc(down_psum.sem, 1)

                def add_tokens(i):
                    pe.wait_ge(*y_act(l, i + 1))
                    pe.wait_ge(*y_dve(l, i + 1))
                    for t in range(T):
                        for half in range(2):
                            ins = nc.tensor.matmul(psum[:, 2 * t + half, :], combT[:, i, t * P:(t + 1) * P],
                                                   y[:, half * BANK:(half + 1) * BANK], start=False,
                                                   stop=i == PAIRS - 1)
                    ins.then_inc(added_psum.sem, 1)

                for i in range(PAIRS + 2):
                    if i < PAIRS:
                        gate_up(i)
                    if 1 <= i <= PAIRS:
                        turn_act(i - 1)
                    if i >= 2:
                        add_tokens(i - 2)
                    if 1 <= i <= PAIRS:
                        down(i - 1)

                if l == 0:
                    turn(psum[:, 7, 0:P], ident[:, :]).then_inc(x_free.sem, 1)
                pe.wait_ge(*extras_ready(l))
                listed = pe.value_load(n_extras[0:1, 0:1], min_val=0, max_val=EXTRAS)
                before = pe.value_load(passes_before[0:1, 0:1], min_val=0, max_val=L * ITERS)
                first = number["extra", l, 0]
                with pe.Fori(0, ITERS) as j:
                    with pe.If(listed > 2 * j):
                        pe.wait_ge(x_onehot.sem, j + before + 1)
                        for q in range(C):
                            for t in range(T):
                                ins = nc.tensor.matmul(psum[:, 4 + q % 2, (q // 2) * P:(q // 2 + 1) * P],
                                                       xn[:, t, q * P:(q + 1) * P],
                                                       onehot_x[:, t].rearrange("p e s -> p (e s)"),
                                                       start=t == 0, stop=t == T - 1)
                        ins.then_inc(x_gathered.sem, 1)
                        pe.wait_ge(x_weighted.sem, j + before + 1)
                        for t in range(T):
                            ins = turn(psum[:, 6, t * P:(t + 1) * P], weighted_x[:, t].rearrange("p e s -> p (e s)"))
                        ins.then_inc(x_turned.sem, 1)
                        pe.wait_ge(x_tokens_act.sem, j + before + 1)
                        pe.wait_ge(x_tokens_dve.sem, j + before + 1)
                        pe.wait_ge(x_loaded_w.sem, j * F_LOADED + before * F_LOADED + F_LOADED)
                        for q in range(C):
                            for k in range(2):
                                w = ring[:, (first + k) % RING, :].rearrange("p (c n) -> p c n", c=C)
                                ins = nc.tensor.matmul(psum[k * SLOTS:(k + 1) * SLOTS, 7, :], hE[:, q, k, :],
                                                       w[:, q, :], start=q == 0, stop=q == C - 1)
                        ins.then_inc(x_gu.sem, 1)
                        pe.wait_ge(x_act.sem, j + before + 1)
                        for q in range(FC):
                            ins = turn(psum[:, 6, q * P:(q + 1) * P], e_act[:, 0, q * P:(q + 1) * P])
                        ins.then_inc(x_aT_psum.sem, 1)
                        pe.wait_ge(x_aT.sem, j + before + 1)
                        w = ring[:, (first + 2) % RING, :].rearrange("p (k n) -> p k n", k=2 * FC)
                        for half in range(2):
                            for q in range(FC):
                                for k in range(2):
                                    ins = nc.tensor.matmul(psum[k * SLOTS:(k + 1) * SLOTS, 4 + half, :],
                                                           aT[:, q, k * SLOTS:(k + 1) * SLOTS],
                                                           w[:, k * FC + q, half * BANK:(half + 1) * BANK],
                                                           start=q == 0, stop=q == FC - 1)
                        ins.then_inc(x_down.sem, 1)
                        pe.wait_ge(x_y_act.sem, j + before + 1)
                        pe.wait_ge(x_y_dve.sem, j + before + 1)
                        for t in range(T):
                            for half in range(2):
                                ins = nc.tensor.matmul(psum[:, 2 * t + half, :], combT[:, 0, t * P:(t + 1) * P],
                                                       y[:, half * BANK:(half + 1) * BANK], start=False,
                                                       stop=True, skip_group_check=True)
                        ins.then_inc(x_free.sem, 1)
                turn(psum[:, 4, 0:P], ident[:, :]).then_inc(moe_psum.sem, 1)


_INS = ["x", "c", "positions", "w_ada", "b_ada", "g_mix", "g_ffn", "w_in", "conv_w", "g_q_a", "w_uq", "g_kv_a",
        "w_ukv", "g_qn", "g_kn", "w_conv_out", "w_attn_out", "w_o", "w_router", "b_router", "w_e_gate", "w_e_up",
        "w_e_down", "w_s_gate", "w_s_up", "w_s_down"]


def kernel(**inputs):
    import concourse.bacc as bacc
    from concourse.bass_utils import run_bass_kernel_spmd

    nc = bacc.Bacc("TRN2", target_bir_lowering=False, num_devices=1)
    arrays, args = {}, []
    for name in _INS:
        a = np.ascontiguousarray(inputs[name])
        arrays[f"in_{name}"] = a
        args.append(nc.dram_tensor(f"in_{name}", a.shape, mybir.dt.from_np(a.dtype), kind="ExternalInput").ap())
    shape = arrays["in_x"].shape
    args.append(nc.dram_tensor("out_0", shape, F32, kind="ExternalOutput").ap())
    trunk(nc, *args)
    r = run_bass_kernel_spmd(nc, [arrays], core_ids=[0])
    return r.results[0]["out_0"]
```

```python
from contextlib import ExitStack

import numpy as np

import concourse.bass as bass
from concourse import mybir
from concourse.alu_op_type import AluOpType as ALU

ACT = mybir.ActivationFunctionType
AX = mybir.AxisListType
F32 = mybir.dt.float32
BF16 = mybir.dt.bfloat16
I32 = mybir.dt.int32
F32R = mybir.dt.float32r

P = 128
EPS = 1e-6
ROPE_THETA = 10000.0
BANK = 512
SLOTS = 64
HIGH_BITS = -4096
CHUNK = 4096
RING = 5


class Signal:

    def __init__(self, sem, per_layer=1):
        self.sem, self.per_layer = sem, per_layer

    def __call__(self, layer, n=1):
        return self.sem, layer * self.per_layer + n


def trunk(nc, x, c, positions, w_ada, b_ada, g_mix, g_ffn, w_in, conv_w, g_q_a, w_uq, g_kv_a, w_ukv,
          g_qn, g_kn, w_conv_out, w_attn_out, w_o, w_router, b_router, w_e_gate, w_e_up, w_e_down,
          w_s_gate, w_s_up, w_s_down, out):
    _, S, D = x.shape
    L = w_in.shape[0]
    CW = w_conv_out.shape[1]
    QR, KR = w_uq.shape[1], w_ukv.shape[1]
    E, F = w_e_gate.shape[1], w_e_gate.shape[3]
    DH = g_qn.shape[1]
    NH = w_uq.shape[2] // DH
    VD = w_attn_out.shape[1] // NH
    ND = w_ukv.shape[2] // NH - VD
    RD = DH - ND
    HALF = RD // 2
    GRP = 4
    EPG = E // GRP
    T = S // P
    C = D // P
    NB = CW // P
    LAT = QR + KR + RD
    QB = QR // P
    PAIRS = E // 2
    GROUPS = S // SLOTS
    EXTRAS = 8
    assert 2 * S // SLOTS <= EXTRAS
    STEPS = PAIRS + 1
    ITERS = EXTRAS // 2 - 1
    SCALE = DH ** -0.5
    FC = F // P
    UNITS = 22
    F_LOADED = 6 * 16
    assert (S, D, CW, QR, KR, F, E, NH, DH, VD) == (256, 1024, 512, 256, 128, 256, 16, 8, 96, 64)

    o_cb, o_cc, o_cx = 0, CW, 2 * CW
    o_lat = 3 * CW
    o_ga = o_lat + LAT
    o_gb = o_ga + D

    with ExitStack() as ctx:
        def sb(name, shape, dt=F32):
            return ctx.enter_context(nc.sbuf_tensor(name, shape, dt))

        def signal(name, per_layer=1):
            return Signal(ctx.enter_context(nc.semaphore(name)), per_layer)

        ring = sb("ring", [P, RING, CHUNK])
        w_lat = sb("w_lat", [P, QB * NH * DH + NH * (ND + VD)])
        uq_sb = w_lat[:, 0:QB * NH * DH].rearrange("p (k n) -> p k n", k=QB)
        ukv_sb = w_lat[:, QB * NH * DH:]
        sdown_sb = sb("sdown_sb", [P, FC, D])
        router_sb = sb("router_sb", [P, C, E])
        x_sb = sb("x_sb", [P, T, D])
        gate_rows = sb("gate_rows", [P, 2, D])
        ada_row = sb("ada_row", [P, BANK])
        ada_bias = sb("ada_bias", [P, 2, BANK])
        mod_cols = sb("mod_cols", [P, 2, 3, 2 * C])
        gain = sb("gain", [P, 2, 2, C])
        ident = sb("ident", [P, P])
        tri = sb("tri", [P, P], BF16)
        ones = sb("ones", [P, P], BF16)
        ones_f = sb("ones_f", [P, 32])
        slot_id = sb("slot_id", [P, SLOTS])
        count_up = sb("count_up", [P, E + 1])
        lower = sb("lower", [P, GRP, EPG])
        b_router_sb = sb("b_router_sb", [P, E])
        head_gain = sb("head_gain", [P, L, 2, DH])
        NPRM = 2 * C + QB + 1 + 3 * NB
        cols = sb("cols", [P, L * NPRM])
        c_act = sb("c_act", [P, C, 32])
        c_tmp = sb("c_tmp", [P, 2, C])
        cos_sin = sb("cos_sin", [P, T, 2, HALF])
        freq = sb("freq", [P, HALF])
        pos_i = sb("pos_i", [P, T], I32)
        pos_f = sb("pos_f", [P, T])
        sumsq = sb("sumsq", [P, T, 2])
        mean_sq = sb("mean_sq", [P, 2 * NH])
        rstd = sb("rstd", [P, 2 * NH])
        minus_half = sb("minus_half", [P, 2 * NH])
        top = sb("top", [P, 2, T])
        bias_m = sb("bias_m", [P, 2, T])
        denom = sb("denom", [P, 2, T])
        r_small = sb("r_small", [P, 12, T * E])
        pairwise = sb("pairwise", [P, 3, T * GRP, EPG, EPG])
        sel_b = sb("sel_b", [P, T, E], BF16)
        slot_of = sb("slot_of", [P, T, E])
        combine = sb("combine", [P, T, E])
        lengths = sb("lengths", [P, E])
        slot_x = sb("slot_x", [P, T, EXTRAS])
        combine_x = sb("combine_x", [P, T, EXTRAS])
        extra_expert = sb("extra_expert", [P, EXTRAS], I32)
        slot_weight = sb("slot_weight", [P, PAIRS + 1])
        n_extras = sb("n_extras", [P, 1], I32)
        passes_before = sb("passes_before", [P, 1], I32)
        passes_f = sb("passes_f", [P, 2 + ITERS])

        hT = sb("hT", [P, C, S])
        hT_end = nc.sbuf_base
        work = sb("work", [P, 17928])
        work_end = nc.sbuf_base

        def over(name, start, shape):
            nc.sbuf_base = start
            t = nc.alloc_sbuf_tensor(name, shape, F32R)
            nc.sbuf_base = work_end
            return t

        def work_address(a):
            return work_end - 4 * (17928 - a)

        def part(a, *shape):
            n = int(np.prod(shape))
            names = "abcd"[:len(shape)]
            v = work[:, a:a + n]
            if len(shape) == 1:
                return v
            return v.rearrange(f"p ({' '.join(names)}) -> p {' '.join(names)}",
                               **{k: s for k, s in zip(names, shape)})

        xn = part(0, T, D)
        merged = part(0, C, S)
        cc_tmp = part(2048, 2, BANK)
        u = part(3072, NB, S + 2)
        yc = part(4104, NB, S)
        qk = part(5128, T, 2, NH, DH)
        sq = part(8200, 2 * NH, DH)
        lat_n = part(8200, T, QR + KR)
        ada_acc = part(3072, 4 * BANK)
        v_sb = part(9736, T, NH, VD)
        qkT = part(10760, 2, 2, S)
        tanh_b = part(11784, C, S)
        oT = part(13832, NH // 2, S)
        probs = part(14856, 2, T, S)
        rot_tmp = part(14856, 4, 2 * NH, HALF)
        probsT = part(15880, 2, T, S)
        latT = part(15880, QB + 1, S)
        tanh_a = part(16904, 2, BANK)
        unused = part(16904, T, QR + KR)
        angle = part(11784, 3, T, 2, HALF)
        rows = part(13832, P)
        c_rows = part(14200, P)[0:C, :]
        ids_i = part(14000, SLOTS).bitcast(I32)
        count_i = part(14100, E + 1).bitcast(I32)
        onehot = over("onehot", work_address(2048), [P, T, E, SLOTS])
        weighted = part(4096, T, E, SLOTS)
        combT = over("combT", work_address(6144), [P, PAIRS, S])
        y = w_lat[:, 0:D]
        y_masked = w_lat[:, D:2 * D]
        y_high = over("y_high", work_address(2048), [P, D])
        y_low = over("y_low", work_address(2048 + D), [P, D])
        combT_weighted = w_lat[:, 0:PAIRS * S].rearrange("p (j s) -> p j s", j=PAIRS)
        hE = part(8192, C, E, SLOTS)
        e_tanh = part(16384, 2, F)
        e_act = part(16896, 2, F)
        s_tanh = part(16384, FC, S)
        s_act = part(16896, FC, S)
        aT = part(17408, FC, P)
        router_out = part(17664, S)
        x_masked = part(8192, T, D)
        x_low = over("x_low", work_address(0), [P, T, D])
        x_high = over("x_high", hT_end - 4 * C * S, [P, T, D])
        listing = part(4096, 2048)
        NF = E * (GROUPS - 1)
        LEAD = 32
        flags = listing[:, 0:NF]
        run_sums = [listing[:, 64 + k * 96:64 + k * 96 + LEAD + NF] for k in range(2)]
        match = listing[:, 256:256 + EXTRAS * NF].rearrange("p (k e g) -> p k e g", k=EXTRAS, e=E)
        is_expert = listing[:, 640:640 + EXTRAS * E].rearrange("p (k e) -> p k e", k=EXTRAS)
        scratch_e = listing[:, 768:768 + EXTRAS * E].rearrange("p (k e) -> p k e", k=EXTRAS)
        is_group = listing[:, 896:896 + EXTRAS * (GROUPS - 1)].rearrange("p (k g) -> p k g", k=EXTRAS)
        group_of = listing[:, 928:928 + EXTRAS]
        expert_f = listing[:, 936:936 + EXTRAS]
        onehot_x = over("onehot_x", work_address(4096 + 1024), [P, T, 2, SLOTS])
        combT_weighted_x = listing[:, 1792:1792 + S]
        weighted_x = listing[:, 1280:1536].rearrange("p (t e s) -> p t e s", t=T, e=2)

        psum = ctx.enter_context(nc.psum_tensor("psum", [P, 8, BANK], F32))

        slot_loaded = [signal(f"slot{i}_loaded") for i in range(RING)]
        x_loaded = signal("x_loaded")
        c_loaded = signal("c_loaded")
        c_psum = signal("c_column_in_psum")
        params_loaded = signal("params_loaded")
        bias_loaded = [signal(f"ada_bias{i}_loaded") for i in range(2)]
        latw_loaded = signal("latw_loaded")
        sdown_loaded = signal("sdown_loaded")
        out_stored = signal("out_stored")
        consts = signal("consts_ready")
        vconsts = signal("vector_consts_ready")
        cols_psum = signal("param_columns_in_psum")
        cols_ready = signal("param_columns_ready")
        c_tanh = signal("c_tanh_ready")
        c_ready = signal("c_act_ready")
        angles_ready = signal("angles_ready")
        rope_ready = signal("cos_sin_ready")
        dve = signal("vector_step_done")
        pool = signal("pool_step_done")
        ada_products_done = signal("ada_products_done", 4)
        ada_scaled = signal("ada_rows_scaled", 8)
        ada_in_psum = signal("ada_in_psum", 2)
        ada_row_ready = signal("ada_row_ready")
        ada_turned = signal("ada_turned")
        mod_ready = signal("mod_columns_ready")
        gate_ready = signal("gate_row_ready", 2)
        gain_ready = signal("gain_ready", 2)
        x_squares = signal("x_squares_ready", 2)
        ms_ready = signal("mean_squares_ready", 5)
        rstd_ready = signal("rstd_ready", 5)
        xn_ready = signal("x_normed", 2)
        xnT_ready = signal("x_turned", 8)
        hT_act = signal("hT_half_by_scalar", 2)
        hT_dve = signal("hT_half_by_vector", 2)
        lat_psum = signal("latents_in_psum", T)
        lat_squares = signal("latent_squares_ready", T)
        lat_ready = signal("latents_normed", T)
        latT_psum = signal("latents_turned", T)
        latT_ready = signal("latT_ready", T)
        up_psum = signal("up_projections_in_psum", 2 * T)
        qkv_copied = signal("qkv_copied", 2 * T)
        qk_squares = signal("qk_squares_ready", T)
        qk_ready = signal("qk_normed_rotated", T)
        unit_psum = signal("unit_in_psum", UNITS)
        cc_ready = signal("cc_copied", 2)
        u_ready = signal("u_ready", 2)
        conv_ready = signal("conv_gated", 2)
        ya_ready = signal("ya_copied", 4)
        ga_tanh = signal("gate_a_tanh", 4)
        ga_used = signal("gate_a_used", 4)
        gb_tanh = signal("gate_b_tanh", 4)
        qkT_psum = signal("qk_turned", NH)
        qkT_ready = signal("qkT_ready", NH)
        scores_psum = signal("scores_in_psum", NH)
        bias_ready = signal("score_bias_ready", NH)
        exp_done = signal("exp_done", NH)
        probs_ready = signal("probs_ready", NH)
        pT_psum = signal("probs_turned", NH)
        pT_ready = signal("probsT_ready", NH)
        pv_psum = signal("pv_in_psum", NH)
        oT_ready = signal("oT_pair_ready", NH // 2)
        yb_gated = signal("gated_yb_ready", 4)
        merged_ready = signal("merged_ready", 4)
        mix_psum = signal("mixer_out_in_psum", 2 * T)
        mix_added = signal("mixer_added", 1)
        router_psum = signal("router_in_psum")
        router_copied = signal("router_copied")
        routerT_psum = signal("router_turned")
        router_exp = signal("router_exp_ready")
        chosen = signal("experts_chosen")
        rank_psum = signal("ranks_in_psum")
        ranks_read = signal("ranks_read")
        onehot_ready = signal("onehot_ready")
        masked_ready = signal("high_part_masked")
        low_ready = signal("low_part_ready")
        high_ready = signal("high_part_ready")
        weighted_ready = signal("weighted_onehot_ready")
        s_gate_psum = signal("shared_gate_in_psum")
        s_tanh_ready = signal("shared_tanh_ready")
        s_up_psum = signal("shared_up_in_psum")
        s_act_ready = signal("shared_act_ready")
        s_down_psum = signal("shared_down_issued")
        gather_psum = signal("gathered_in_psum", 2 * C)
        hE_act = signal("gathered_by_scalar", C)
        hE_dve = signal("gathered_by_vector", C)
        combT_psum = signal("weighted_turned", 4)
        weights_read = signal("slot_weights_ready", 4)
        combT_ready = signal("combT_ready", 4)
        gu_psum = signal("gate_up_in_psum", 2 * STEPS)
        tanh_ready = signal("expert_tanh_ready", STEPS)
        act_ready = signal("expert_act_ready", STEPS)
        aT_psum = signal("expert_act_turned", STEPS)
        aT_ready = signal("aT_ready", STEPS)
        down_psum = signal("down_in_psum", 2 * STEPS)
        y_act = signal("y_by_scalar", STEPS)
        y_dve = signal("y_by_vector", STEPS)
        y_masked_ready = signal("y_masked", STEPS)
        y_high_ready = signal("y_high_ready", STEPS)
        y_low_ready = signal("y_low_ready", STEPS)
        added_psum = signal("added_to_tokens", STEPS)
        moe_psum = signal("moe_out_in_psum")
        moe_added = signal("moe_added", 1)
        extras_ready = signal("extras_listed")
        first_onehot = signal("first_extras_onehot_ready")
        first_weighted = signal("first_extras_weighted_ready")
        first_gathered = signal("first_extras_gathered", 2)
        first_tokens = signal("first_extras_tokens_ready", 2)
        first_turned = signal("first_extras_turned")
        first_weights = signal("first_extras_weights_ready")
        first_combT = signal("first_extras_combT_ready")
        x_loaded_w = signal("extra_weights_loaded")
        x_onehot = signal("extra_onehot_ready")
        x_weighted = signal("extra_weighted_ready")
        x_gathered = signal("extra_gathered")
        x_turned = signal("extra_onehot_turned")
        x_tokens_act = signal("extra_tokens_by_scalar")
        x_tokens_dve = signal("extra_tokens_by_vector")
        x_gu = signal("extra_gate_up")
        x_tanh = signal("extra_tanh_ready")
        x_act1 = signal("extra_act_begun")
        x_act = signal("extra_act_ready")
        x_aT_psum = signal("extra_act_turned")
        x_aT = signal("extra_aT_ready")
        x_down = signal("extra_down")
        x_y_act = signal("extra_y_by_scalar")
        x_y_dve = signal("extra_y_by_vector")
        x_weights = signal("extra_slot_weights_ready")
        x_combT = signal("extra_combT_ready")
        x_y_masked = signal("extra_y_masked")
        x_y_high = signal("extra_y_high_ready")
        x_y_low = signal("extra_y_low_ready")
        x_free = signal("extra_pass_done")
        x_slots_free = signal("extra_slots_free")

        chunks, number = [], {}

        def chunk(key, pieces, freed_by):
            number[key] = len(chunks)
            chunks.append((pieces, freed_by))

        def ada_chunks(s, parts=range(4)):
            w = w_ada[s // 3, :, (s % 3) * 4 * BANK:(s % 3 + 1) * 4 * BANK].rearrange("(c p) n -> p c n", p=P)
            for i in parts:
                chunk(("ada", s, i), [(2, 0, 0, w[:, 2 * i:2 * i + 2, :])],
                      ada_scaled(s // 3, 4 * (s % 3) - 3 + i) if s % 3 else ada_products_done(s // 3, i + 1))

        def in_chunk(l, key, a, n, freed_by):
            chunk((key, l), [(C, 0, 0, w_in[l, :, a:a + n].rearrange("(c p) n -> p c n", p=P))], freed_by)

        def expert_rows(w, l, i, k, a, n):
            if i < PAIRS:
                return w[l, 2 * i + k, a:a + n].rearrange("(c p) n -> p c n", p=P)
            return lambda experts: w[l, bass.ds(experts[k], 1), a:a + n].rearrange("e (c p) n -> p (e c) n", p=P)

        ada_chunks(0)
        for l in range(L):
            in_chunk(l, "lat", o_lat, LAT, lat_psum(l, T))
            in_chunk(l, "cc", o_cc, CW, unit_psum(l, 3))
            in_chunk(l, "cx", o_cx, CW, unit_psum(l, 4))
            in_chunk(l, "cb", o_cb, CW, unit_psum(l, 6))
            chunk(("conv", l), [(NB, 0, 0, w_conv_out[l].rearrange("(c p) n -> p c n", p=P))], unit_psum(l, 10))
            in_chunk(l, "ga0", o_ga, BANK, unit_psum(l, 12))
            ada_chunks(3 * l + 1, [0])
            in_chunk(l, "ga1", o_ga + BANK, BANK, unit_psum(l, 14))
            ada_chunks(3 * l + 1, [1, 2])
            in_chunk(l, "gb0", o_gb, BANK, unit_psum(l, 16))
            ada_chunks(3 * l + 1, [3])
            in_chunk(l, "gb1", o_gb + BANK, BANK, unit_psum(l, 18))
            ada_chunks(3 * l + 2, [0, 1])
            chunk(("attn", l), [(NB, 0, 0, w_attn_out[l].rearrange("(c p) n -> p c n", p=P))], unit_psum(l, UNITS))
            ada_chunks(3 * l + 2, [2, 3])
            for i in range(2):
                chunk((f"wo{i}", l), [(C, 0, 0, w_o[l, :, i * BANK:(i + 1) * BANK].rearrange("(c p) n -> p c n", p=P))],
                      mix_psum(l, 2 + 2 * i))
            if l + 1 < L:
                ada_chunks(3 * l + 3)
            chunk(("shared", l), [(C, 0, 0, w_s_gate[l].rearrange("(c p) n -> p c n", p=P)),
                                  (C, 0, F, w_s_up[l].rearrange("(c p) n -> p c n", p=P))], s_up_psum(l))
            for i in range(STEPS + 1):
                for part_no in range(2 if i < STEPS else 0):
                    chunk(("gu", l, i, part_no),
                          [(C, k * C // 2, at, expert_rows(w, l, i, k, part_no * D // 2, D // 2))
                           for k in range(2) for at, w in ((0, w_e_gate), (F, w_e_up))],
                          gu_psum(l, 2 * i + 1 + part_no))
                if i:
                    if i <= PAIRS:
                        pieces = [(2 * FC, 0, 0, w_e_down[l, 2 * i - 2:2 * i].rearrange("e (c p) n -> p (e c) n", p=P))]
                    else:
                        pieces = [(2 * FC, k * FC, 0, expert_rows(w_e_down, l, PAIRS, k, 0, F)) for k in range(2)]
                    chunk(("down", l, i - 1), pieces, down_psum(l, 2 * i))

        def slot(key, k):
            return ring[:, number[key] % RING, :].rearrange("p (k n) -> p k n", k=k)

        def loaded(key):
            n = number[key]
            return slot_loaded[n % RING].sem, 16 * len(pieces_before(n))

        def pieces_before(n):
            return [q for i in range(n % RING, n + 1, RING) for q in chunks[i][0]]

        PRM = {}
        at = 0
        for name, n in (("g_mix", C), ("g_ffn", C), ("g_q_a", QB), ("g_kv_a", 1), ("conv", 3 * NB)):
            for l in range(L):
                PRM[name, l] = at
                at += n
        NROWS = at

        def col(name, l, i, n=1):
            return cols[:, PRM[name, l] + i:PRM[name, l] + i + n]

        sc_of = lambda l, which: mod_cols[:, l % 2, 0, C:2 * C] if which == 0 else mod_cols[:, l % 2, 2, 0:C]
        sh_of = lambda l, which: mod_cols[:, l % 2, 0, 0:C] if which == 0 else mod_cols[:, l % 2, 1, C:2 * C]

        block = ctx.enter_context(nc.Block())

        @block.sync
        def _(sp):
            sp.wait_ge(c_loaded.sem, 16)

            def listed_expert(k):
                return sp.value_load(extra_expert[0:1, bass.ds(k, 1)], min_val=0, max_val=E - 1)

            def load_further_extras(l):
                listed = sp.value_load(n_extras[0:1, 0:1], min_val=0, max_val=EXTRAS)
                before = sp.value_load(passes_before[0:1, 0:1], min_val=0, max_val=L * ITERS)
                first = number["down", l, PAIRS] - 2
                slots = [ring[:, (first + k) % RING, :] for k in range(3)]
                with sp.Fori(0, ITERS) as j:
                    with sp.If(listed > 2 * j + 2):
                        sp.wait_ge(*down_psum(l, 2 * STEPS))
                        for k in range(2):
                            e = listed_expert(2 * j + (k + 2))
                            dst = slots[k].rearrange("p (c n) -> p c n", c=C)
                            for at, w in ((0, w_e_gate), (F, w_e_up)):
                                sp.dma_start(dst[:, :, at:at + F],
                                             w[l, bass.ds(e, 1)].rearrange("e (c p) n -> p (e c) n", p=P)) \
                                    .then_inc(x_loaded_w.sem, 16)
                            dst = slots[2].rearrange("p (k n) -> p k n", k=2 * FC)
                            sp.dma_start(dst[:, k * FC:(k + 1) * FC, :],
                                         w_e_down[l, bass.ds(e, 1)].rearrange("e (c p) n -> p (e c) n", p=P)) \
                                .then_inc(x_loaded_w.sem, 16)
                        sp.wait_ge(x_free.sem, j + before + 1)
                        sp.sem_inc(x_slots_free.sem, 1)

            experts = None
            for n, (pieces, _) in enumerate(chunks):
                for l in range(L):
                    if n == number["gu", l, PAIRS, 0]:
                        sp.wait_ge(*extras_ready(l))
                        experts = [listed_expert(k) for k in range(2)]
                    if n == number["down", l, PAIRS] + RING - 2:
                        load_further_extras(l)
                if n >= RING:
                    sp.wait_ge(*chunks[n - RING][1])
                for rows, a, at, src in pieces:
                    if callable(src):
                        src = src(experts)
                    width = src.shape[2]
                    dst = ring[:, n % RING, :].rearrange("p (k n) -> p k n", k=rows)[:, a:a + src.shape[1], at:at + width]
                    sp.dma_start(dst, src).then_inc(slot_loaded[n % RING].sem, 16)
                if n == 0:
                    sp.dma_start(x_sb[:, :, :], x[0].rearrange("(t p) d -> p t d", p=P)).then_inc(x_loaded.sem, 16)
                if n == 1:
                    sp.wait_ge(params_loaded.sem, 16 * (9 + T))
                for l in range(L):
                    if n == number["cc", l]:
                        if l:
                            sp.wait_ge(*moe_psum(l - 1))
                        sp.dma_start(uq_sb, w_uq[l].rearrange("(c p) n -> p c n", p=P)).then_inc(latw_loaded.sem, 16)
                        sp.dma_start(ukv_sb, w_ukv[l]).then_inc(latw_loaded.sem, 16)
                    if n == number["shared", l]:
                        if l:
                            sp.wait_ge(*s_down_psum(l - 1))
                        sp.dma_start(sdown_sb[:, :, :], w_s_down[l].rearrange("(c p) n -> p c n", p=P)) \
                            .then_inc(sdown_loaded.sem, 16)
            load_further_extras(L - 1)
            sp.wait_ge(*moe_added(L - 1))
            sp.dma_start(out[0].rearrange("(t p) d -> p t d", p=P), x_sb[:, :, :]).then_inc(out_stored.sem, 16)
            sp.wait_ge(out_stored.sem, 16)

        @block.gpsimd
        def _(gp):
            step = [0]

            def link(ins):
                step[0] += 1
                ins.then_inc(pool.sem, 1)
                gp.wait_ge(pool.sem, step[0])

            link(gp.memset(ident[:, :], 0.0))
            gp.affine_select(out=ident[:, :], in_=ident[:, :], compare_op=ALU.not_equal, fill=1.0, base=0,
                             pattern=[[-1, P]], channel_multiplier=1).then_inc(consts.sem, 1)
            link(gp.memset(tri[:, :], 1.0))
            gp.affine_select(out=tri[:, :], in_=tri[:, :], compare_op=ALU.is_gt, fill=0.0, base=0,
                             pattern=[[1, P]], channel_multiplier=-1).then_inc(consts.sem, 1)
            gp.memset(ones[:, :], 1.0).then_inc(consts.sem, 1)
            gp.memset(ones_f[:, :], 1.0).then_inc(consts.sem, 1)
            gp.iota(ids_i, pattern=[[1, SLOTS]], base=-2 * S, channel_multiplier=0).then_inc(consts.sem, 1)
            gp.iota(count_i, pattern=[[1, E + 1]], base=0, channel_multiplier=0).then_inc(consts.sem, 1)
            gp.memset(minus_half[:, :], -0.5).then_inc(consts.sem, 1)
            gp.wait_ge(*consts(0, 7))

            def power(l, n, width):
                gp.wait_ge(*ms_ready(l, n))
                gp.tensor_tensor(rstd[:, 0:width], mean_sq[:, 0:width], minus_half[:, 0:width], ALU.pow) \
                    .then_inc(rstd_ready.sem, 1)
                gp.wait_ge(*rstd_ready(l, n))

            def gates(l, which):
                gp.wait_ge(*ada_row_ready(0, 3 * l + 2 + which))
                if l:
                    gp.wait_ge(*(mix_added if which == 0 else moe_added)(l - 1))
                first = 0 if which == 0 else 2
                for j in range(2):
                    q = 32 * (first + j)
                    ins = gp.partition_broadcast(gate_rows[:, which, j * BANK:(j + 1) * BANK], ada_row[q:q + 1, :], P)
                    if j == 0:
                        link(ins)
                ins.then_inc(gate_ready.sem, 1)
                gp.wait_ge(*gate_ready(l, which + 1))

            for l in range(L):
                power(l, 1, T)
                power(l, 2, 2 * T)
                power(l, 3, 2 * NH)
                power(l, 4, 2 * NH)
                gates(l, 0)
                gates(l, 1)
                power(l, 5, T)

        @block.scalar
        def _(act):
            def load_bias(s):
                if s >= 2:
                    act.wait_ge(*ada_row_ready(0, s - 1))
                for j in range(4):
                    a = ((s % 3) * 4 + j) * BANK
                    act.dma_start(ada_bias[32 * j:32 * j + 32, s % 2, :],
                                  b_ada[s // 3, a:a + BANK].partition_broadcast(32)) \
                        .then_inc(bias_loaded[s % 2].sem, 16)

            act.dma_start(c_rows, c[0].rearrange("(c p) -> c p", p=P)).then_inc(c_loaded.sem, 16)
            act.wait_ge(*c_psum(0))
            nc.scalar.activation(c_tmp[:, 0, :], psum[:, 5, 0:C], ACT.Tanh, scale=0.5) \
                .then_inc(c_tanh.sem, 1)
            load_bias(0)
            for name, src in (("g_mix", g_mix), ("g_ffn", g_ffn), ("g_q_a", g_q_a), ("g_kv_a", g_kv_a)):
                at = PRM[name, 0]
                n = L * src.shape[1] // P
                act.dma_start(rows[at:at + n, :], src.rearrange("l (c p) -> (l c) p", p=P)).then_inc(params_loaded.sem, 16)
            at = PRM["conv", 0]
            act.dma_start(rows[at:at + L * 3 * NB, :], conv_w.rearrange("l k (c p) -> (l k c) p", p=P)) \
                .then_inc(params_loaded.sem, 16)
            act.dma_start(head_gain[:, :, 0, :], g_qn.partition_broadcast(P)).then_inc(params_loaded.sem, 16)
            act.dma_start(head_gain[:, :, 1, :], g_kn.partition_broadcast(P)).then_inc(params_loaded.sem, 16)
            act.dma_start(b_router_sb[:, :], b_router.partition_broadcast(P)).then_inc(params_loaded.sem, 16)
            act.dma_start(router_sb[:, :, :], w_router.rearrange("(c p) e -> p c e", p=P)) \
                .then_inc(params_loaded.sem, 16)
            for t in range(T):
                act.dma_start(pos_i[:, t:t + 1], positions[0, t * P:(t + 1) * P].rearrange("(p o) -> p o", o=1)) \
                    .then_inc(params_loaded.sem, 16)

            def mod_columns(s, bank):
                act.wait_ge(*ada_turned(0, s + 1))
                src = psum[:, bank, :].rearrange("p (b j r) -> p j b r", b=4, r=32)[:, :, :, 0]
                nc.scalar.activation(mod_cols[:, (s // 3) % 2, s % 3, :].rearrange("p (j b) -> p j b", b=4), src,
                                     ACT.Identity).then_inc(mod_ready.sem, 1)
                if s + 2 < 3 * L:
                    load_bias(s + 2)

            def square_x(l, which):
                if which:
                    act.wait_ge(*mix_added(l))
                elif l:
                    act.wait_ge(*moe_added(l - 1))
                else:
                    act.wait_ge(x_loaded.sem, 16)
                for t in range(T):
                    ins = nc.scalar.activation(xn[:, t, :], x_sb[:, t, :], ACT.Square, accum_out=sumsq[:, t, 0:1])
                ins.then_inc(x_squares.sem, 1)

            def modulate_half(l, which):
                act.wait_ge(*gain_ready(l, which + 1))
                for b in range(2):
                    act.wait_ge(*xnT_ready(l, 4 * which + b + 1))
                    for k in range(2):
                        q = 2 * b + k
                        ins = nc.scalar.activation(hT[:, q, :], psum[:, 3 + b, k * S:(k + 1) * S], ACT.Identity,
                                                   bias=sh_of(l, which)[:, q:q + 1],
                                                   scale=gain[:, l % 2, which, q:q + 1])
                ins.then_inc(hT_act.sem, 1)

            load_bias(1)
            act.wait_ge(*angles_ready(0))
            nc.scalar.activation(cos_sin[:, :, :, :], angle[:, 0], ACT.Sin).then_inc(rope_ready.sem, 1)
            square_x(0, 0)
            mod_columns(0, 7)

            for l in range(L):
                if l:
                    square_x(l, 0)
                modulate_half(l, 0)

                for t in range(T):
                    act.wait_ge(*lat_psum(l, t + 1))
                    nc.scalar.activation(unused[:, t, 0:QR], psum[:, 2 + t, 0:QR], ACT.Square,
                                         accum_out=sumsq[:, t, 0:1])
                    nc.scalar.activation(unused[:, t, QR:], psum[:, 2 + t, QR:QR + KR], ACT.Square,
                                         accum_out=sumsq[:, t, 1:2]).then_inc(lat_squares.sem, 1)

                def copy_cc(j):
                    act.wait_ge(*unit_psum(l, 2 * j + 1))
                    nc.scalar.activation(cc_tmp[:, j, :], psum[:, 0, :], ACT.Identity).then_inc(cc_ready.sem, 1)

                copy_cc(0)
                for t in range(T):
                    act.wait_ge(*latT_psum(l, t + 1))
                    for b in range(QB + 1):
                        g = col("g_q_a", l, b) if b < QB else col("g_kv_a", l, 0)
                        ins = nc.scalar.activation(latT[:, b, t * P:(t + 1) * P], psum[:, 4 + t, b * P:(b + 1) * P],
                                                   ACT.Identity, scale=g)
                    ins.then_inc(latT_ready.sem, 1)
                copy_cc(1)

                for n, (t, what, bank) in enumerate(((0, "q", 2), (0, "kv", 4), (1, "q", 6), (1, "kv", 2))):
                    act.wait_ge(*up_psum(l, n + 1))
                    if what == "q":
                        flat = qk[:, t, 0].rearrange("p h d -> p (h d)")
                        nc.scalar.activation(flat[:, 0:BANK], psum[:, bank, :], ACT.Identity)
                        nc.scalar.activation(flat[:, BANK:], psum[:, bank + 1, 0:NH * DH - BANK], ACT.Identity) \
                            .then_inc(qkv_copied.sem, 1)
                    else:
                        src = psum[:, bank:bank + 2, :].rearrange("p b (h d) -> p (b h) d", d=ND + VD)
                        nc.scalar.activation(qk[:, t, 1, :, 0:ND], src[:, :, 0:ND], ACT.Identity)
                        nc.scalar.activation(v_sb[:, t, :, :], src[:, :, ND:], ACT.Identity) \
                            .then_inc(qkv_copied.sem, 1)

                def square_qk(t):
                    act.wait_ge(*qkv_copied(l, 2 * t + 2))
                    act.wait_ge(*lat_ready(l, t + 1))
                    if t:
                        act.wait_ge(*ms_ready(l, 3))
                    nc.scalar.activation(sq[:, :, :], qk[:, t].rearrange("p a h d -> p (a h) d"), ACT.Square) \
                        .then_inc(qk_squares.sem, 1)

                def copy_ya(j):
                    act.wait_ge(*unit_psum(l, 7 + j))
                    nc.scalar.activation(merged[:, 2 * j:2 * j + 2, :].rearrange("p c s -> p (c s)"),
                                         psum[:, j % 2, :], ACT.Identity, scale=0.5).then_inc(ya_ready.sem, 1)

                def tanh_unit(n):
                    act.wait_ge(*unit_psum(l, n + 1))
                    if n < 14:
                        j = n - 10
                        if j >= 2:
                            act.wait_ge(*ga_used(l, j - 1))
                        nc.scalar.activation(tanh_a[:, j % 2, :], psum[:, n % 2, :], ACT.Tanh, scale=0.5) \
                            .then_inc(ga_tanh.sem, 1)
                    else:
                        j = n - 14
                        nc.scalar.activation(tanh_b[:, 2 * j:2 * j + 2, :].rearrange("p c s -> p (c s)"),
                                             psum[:, n % 2, :], ACT.Tanh, scale=0.5).then_inc(gb_tanh.sem, 1)

                square_qk(0)
                copy_ya(0)
                copy_ya(1)
                square_qk(1)
                copy_ya(2)
                copy_ya(3)
                tanh_unit(10)

                def copy_qkT(h):
                    act.wait_ge(*qkT_psum(l, h + 1))
                    if h >= 2:
                        act.wait_ge(*scores_psum(l, h - 1))
                    nc.scalar.activation(qkT[0:DH, h % 2].rearrange("p a s -> p (a s)"), psum[0:DH, 2, :],
                                         ACT.Identity).then_inc(qkT_ready.sem, 1)

                copy_qkT(0)
                for h in range(NH):
                    if h + 1 < NH:
                        copy_qkT(h + 1)
                    act.wait_ge(*bias_ready(l, h + 1))
                    if h >= 2:
                        act.wait_ge(*pT_psum(l, h - 1))
                    for t in range(T):
                        ins = nc.scalar.activation(probs[:, h % 2, t, :], psum[:, 4 + h % 2, t * S:(t + 1) * S], ACT.Exp,
                                                   bias=bias_m[:, h % 2, t:t + 1], scale=SCALE,
                                                   accum_out=denom[:, h % 2, t:t + 1])
                    ins.then_inc(exp_done.sem, 1)
                    if h != 6:
                        tanh_unit(min(11 + h, 17))
                    if h == 5:
                        mod_columns(3 * l + 1, 3)
                    act.wait_ge(*pT_psum(l, h + 1))
                    if h >= 2:
                        act.wait_ge(*pv_psum(l, h - 1))
                    nc.scalar.activation(probsT[:, h % 2].rearrange("p a s -> p (a s)"), psum[:, 6, :],
                                         ACT.Identity).then_inc(pT_ready.sem, 1)
                mod_columns(3 * l + 2, 4)

                square_x(l, 1)
                modulate_half(l, 1)
                if l + 1 < L:
                    mod_columns(3 * l + 3, 7)
                act.wait_ge(*router_psum(l))
                nc.scalar.activation(router_out[0:E, :], psum[0:E, 5, 0:S], ACT.Identity).then_inc(router_copied.sem, 1)
                act.wait_ge(*routerT_psum(l))
                nc.scalar.activation(r_small[:, 0, :], psum[:, 6, 0:T * E], ACT.Exp, scale=-1.0) \
                    .then_inc(router_exp.sem, 1)
                act.wait_ge(*s_gate_psum(l))
                nc.scalar.activation(s_tanh.rearrange("p c s -> p (c s)"), psum[:, 4, :], ACT.Tanh, scale=0.5) \
                    .then_inc(s_tanh_ready.sem, 1)
                act.wait_ge(*s_up_psum(l))
                act.wait_ge(*masked_ready(l))
                nc.scalar.activation(x_high[:, :, :], x_masked, ACT.Identity).then_inc(high_ready.sem, 1)
                for n in range(0, 2 * C, 2):
                    half, q = divmod(n, C)
                    act.wait_ge(*gather_psum(l, n + 1))
                    nc.scalar.activation(hE[:, q, half * 8:half * 8 + 8, :].rearrange("p e s -> p (e s)"),
                                         psum[:, 4 + n % 4, :], ACT.Identity, bias=sh_of(l, 1)[:, q:q + 1],
                                         scale=gain[:, l % 2, 1, q:q + 1]).then_inc(hE_act.sem, 1)
                for b in range(4):
                    act.wait_ge(*combT_psum(l, b + 1))
                    for k in range(2):
                        ins = nc.scalar.activation(combT_weighted[:, 2 * b + k, :], psum[:, 4 + b, k * S:(k + 1) * S],
                                                   ACT.Identity, accum_out=slot_weight[:, 2 * b + k:2 * b + k + 1])
                    ins.then_inc(weights_read.sem, 1)
                act.wait_ge(*weights_read(l, 4))

                def weight_y(i):
                    act.wait_ge(*down_psum(l, 2 * i + 1))
                    if i:
                        act.wait_ge(*y_low_ready(l, i))
                    nc.scalar.activation(y[:, 0:BANK], psum[:, 7, :], ACT.Identity, scale=slot_weight[:, i:i + 1]) \
                        .then_inc(y_act.sem, 1)
                    act.wait_ge(*y_masked_ready(l, i + 1))
                    nc.scalar.activation(y_high[:, :], y_masked, ACT.Identity).then_inc(y_high_ready.sem, 1)

                for i in range(STEPS + 1):
                    if i < STEPS:
                        act.wait_ge(*gu_psum(l, 2 * i + 2))
                        nc.scalar.activation(e_tanh[:, i % 2, :], psum[:, 4 + i % 2, 0:F], ACT.Tanh, scale=0.5) \
                            .then_inc(tanh_ready.sem, 1)
                    if i >= 1:
                        act.wait_ge(*aT_psum(l, i))
                        nc.scalar.activation(aT.rearrange("p c s -> p (c s)"), psum[:, 6, 0:FC * P], ACT.Identity) \
                            .then_inc(aT_ready.sem, 1)
                        if i in (4, 5):
                            act.wait_ge(*first_gathered(l, i - 3))
                            for m in range(C // 2):
                                q = (i - 4) * C // 2 + m
                                ins = nc.scalar.activation(hE[:, q, 0:2, :].rearrange("p e s -> p (e s)"),
                                                           psum[:, 7, m * P:(m + 1) * P], ACT.Identity,
                                                           bias=sh_of(l, 1)[:, q:q + 1],
                                                           scale=gain[:, l % 2, 1, q:q + 1])
                            ins.then_inc(first_tokens.sem, 1)
                        elif i == 6:
                            act.wait_ge(*first_turned(l))
                            nc.scalar.activation(combT_weighted_x, psum[:, 7, 0:S], ACT.Identity,
                                                 accum_out=slot_weight[:, PAIRS:]).then_inc(first_weights.sem, 1)
                            act.wait_ge(*first_weights(l))
                        weight_y(i - 1)

                act.wait_ge(*extras_ready(l))
                listed = act.value_load(n_extras[0:1, 0:1], min_val=0, max_val=EXTRAS)
                before = act.value_load(passes_before[0:1, 0:1], min_val=0, max_val=L * ITERS)
                with act.Fori(0, ITERS) as j:
                    with act.If(listed > 2 * j + 2):
                        act.wait_ge(x_gathered.sem, j + before + 1)
                        for q in range(0, C, 2):
                            ins = nc.scalar.activation(hE[:, q, 0:2, :].rearrange("p e s -> p (e s)"),
                                                       psum[:, 4 + q % 2, (q // 2) * P:(q // 2 + 1) * P],
                                                       ACT.Identity, bias=sh_of(l, 1)[:, q:q + 1],
                                                       scale=gain[:, l % 2, 1, q:q + 1])
                        ins.then_inc(x_tokens_act.sem, 1)
                        act.wait_ge(x_turned.sem, j + before + 1)
                        nc.scalar.activation(combT_weighted_x, psum[:, 6, 0:S], ACT.Identity,
                                             accum_out=slot_weight[:, PAIRS:]).then_inc(x_weights.sem, 1)
                        act.wait_ge(x_gu.sem, j + before + 1)
                        nc.scalar.activation(e_tanh[:, 0, :], psum[:, 7, 0:F], ACT.Tanh, scale=0.5) \
                            .then_inc(x_tanh.sem, 1)
                        act.wait_ge(x_aT_psum.sem, j + before + 1)
                        nc.scalar.activation(aT.rearrange("p c s -> p (c s)"), psum[:, 6, 0:FC * P],
                                             ACT.Identity).then_inc(x_aT.sem, 1)
                        act.wait_ge(x_down.sem, j + before + 1)
                        act.wait_ge(x_weights.sem, j + before + 1)
                        nc.scalar.activation(y[:, 0:BANK], psum[:, 4, :], ACT.Identity,
                                             scale=slot_weight[:, PAIRS:]).then_inc(x_y_act.sem, 1)
                        act.wait_ge(x_y_masked.sem, j + before + 1)
                        nc.scalar.activation(y_high[:, :], y_masked, ACT.Identity).then_inc(x_y_high.sem, 1)

        @block.vector
        def _(ve):
            step = [0]

            def link(ins):
                step[0] += 1
                ins.then_inc(dve.sem, 1)
                ve.wait_ge(dve.sem, step[0])

            for i in range(HALF):
                nc.vector.memset(freq[:, i:i + 1], float(np.float32(ROPE_THETA ** (-i / HALF))))
            nc.vector.memset(passes_f[:, :], 0.0)
            link(nc.vector.memset(lower[:, :, :], 0.0))
            for i in range(1, GRP):
                ins = nc.vector.memset(lower[:, i, 0:i], 1.0)
            link(ins)
            ve.wait_ge(*consts(0, 7))
            nc.vector.tensor_copy(slot_id[:, :], ids_i)
            link(nc.vector.tensor_copy(count_up[:, :], count_i))

            ve.wait_ge(*c_tanh(0))
            link(nc.vector.scalar_tensor_tensor(out=c_tmp[:, 1, :], in0=c_tmp[:, 0, :], scalar=1.0,
                                                in1=psum[:, 5, 0:C], op0=ALU.add, op1=ALU.mult))
            nc.vector.tensor_scalar(c_act[:, :, :], c_tmp[:, 1, :].unsqueeze(2).broadcast_to([P, C, 32]), 0.5, None,
                                    ALU.mult).then_inc(c_ready.sem, 1)

            ve.wait_ge(params_loaded.sem, 16 * (9 + T))
            link(nc.vector.tensor_copy(pos_f[:, :], pos_i[:, :]))
            two_pi = 2 * np.pi
            part1 = 6.28125
            part2 = float(round((two_pi - part1) * 2 ** 20)) / 2 ** 20
            part3 = float(np.float32(two_pi - part1 - part2))
            turn = 1.5 * 2.0 ** 23
            for t in range(T):
                for k in range(2):
                    ins = nc.vector.tensor_scalar(angle[:, 0, t, k, :], freq[:, :], pos_f[:, t:t + 1], None, ALU.mult)
            link(ins)
            link(nc.vector.tensor_scalar(angle[:, 1, :, 0, :], angle[:, 0, :, 0, :], 1 / two_pi, 0.25, ALU.mult, ALU.add))
            link(nc.vector.tensor_scalar(angle[:, 1, :, 1, :], angle[:, 0, :, 1, :], 1 / two_pi, None, ALU.mult))
            link(nc.vector.tensor_scalar(angle[:, 2], angle[:, 1], turn, None, ALU.add))
            link(nc.vector.tensor_scalar(angle[:, 1], angle[:, 2], -turn, None, ALU.add))
            for q in (part1, part2, part3):
                link(nc.vector.scalar_tensor_tensor(out=angle[:, 0], in0=angle[:, 1], scalar=-q, in1=angle[:, 0],
                                                    op0=ALU.mult, op1=ALU.add))
            link(nc.vector.tensor_scalar(angle[:, 0, :, 0, :], angle[:, 0, :, 0, :], float(np.pi / 2), None, ALU.add))
            limit = float(np.nextafter(np.float32(np.pi), np.float32(0)))
            nc.vector.tensor_scalar(angle[:, 0], angle[:, 0], limit, -limit, ALU.min, ALU.max) \
                .then_inc(angles_ready.sem, 1)

            def mean_squares(l, n, outs):
                for k, (dst, src, width) in enumerate(outs):
                    ins = nc.vector.tensor_scalar(dst, src, 1.0 / width, EPS, ALU.mult, ALU.add)
                ins.then_inc(ms_ready.sem, 1)
                ve.wait_ge(*rstd_ready(l, n))

            def norm_x(l, which):
                ve.wait_ge(*x_squares(l, which + 1))
                mean_squares(l, 5 if which else 1, [(mean_sq[:, 0:T], sumsq[:, :, 0], D)])
                for t in range(T):
                    ins = nc.vector.tensor_scalar(xn[:, t, :], x_sb[:, t, :], rstd[:, t:t + 1], None, ALU.mult)
                ins.then_inc(xn_ready.sem, 1)

            def add_bias(s, bank):
                ve.wait_ge(*(ada_in_psum(s // 3, s % 3) if s % 3 else ada_products_done(s // 3, 4)))
                ve.wait_ge(bias_loaded[s % 2].sem, 64 * (s // 2 + 1))
                if s:
                    ve.wait_ge(*ada_turned(0, s))
                    if s % 3 == 0:
                        ve.wait_ge(*gate_ready(s // 3 - 1, 2))
                    elif s % 3 == 2:
                        ve.wait_ge(*gate_ready(s // 3, 1))
                nc.vector.tensor_tensor(ada_row[:, :], psum[:, bank, :], ada_bias[:, s % 2, :], ALU.add) \
                    .then_inc(ada_row_ready.sem, 1)

            def gains(s):
                l, k = divmod(s, 3)
                ve.wait_ge(*mod_ready(0, s + 1))
                which = 0 if k == 0 else 1
                nc.vector.scalar_tensor_tensor(out=gain[:, l % 2, which, :], in0=sc_of(l, which), scalar=1.0,
                                               in1=col("g_ffn" if which else "g_mix", l, 0, C),
                                               op0=ALU.add, op1=ALU.mult).then_inc(gain_ready.sem, 1)
                ve.wait_ge(*gain_ready(l, which + 1))

            def modulate_half(l, which):
                for b in range(2, 4):
                    ve.wait_ge(*xnT_ready(l, 4 * which + b + 1))
                    for k in range(2):
                        q = 2 * b + k
                        ins = nc.vector.tensor_scalar(hT[:, q, :], psum[:, 3 + b, k * S:(k + 1) * S],
                                                      gain[:, l % 2, which, q:q + 1], sh_of(l, which)[:, q:q + 1],
                                                      ALU.mult, ALU.add)
                ins.then_inc(hT_dve.sem, 1)

            norm_x(0, 0)
            ve.wait_ge(*cols_psum(0))
            nc.vector.tensor_copy(cols[:, 0:NROWS], psum[:, 6, 0:NROWS]).then_inc(cols_ready.sem, 1)
            ve.wait_ge(*cols_ready(0))
            add_bias(0, 7)
            gains(0)

            for l in range(L):
                if l:
                    norm_x(l, 0)
                modulate_half(l, 0)

                ve.wait_ge(*lat_squares(l, T))
                mean_squares(l, 2, [(mean_sq[:, 0:T], sumsq[:, :, 0], QR), (mean_sq[:, T:2 * T], sumsq[:, :, 1], KR)])
                for t in range(T):
                    nc.vector.tensor_scalar(lat_n[:, t, 0:QR], psum[:, 2 + t, 0:QR], rstd[:, t:t + 1], None, ALU.mult)
                    nc.vector.tensor_scalar(lat_n[:, t, QR:], psum[:, 2 + t, QR:QR + KR], rstd[:, T + t:T + t + 1],
                                            None, ALU.mult)
                    nc.vector.tensor_copy(qk[:, t, 1, :, ND:],
                                          psum[:, 2 + t, QR + KR:LAT].unsqueeze(1).broadcast_to([P, NH, RD])) \
                        .then_inc(lat_ready.sem, 1)

                nc.vector.memset(u[:, :, 0:1], 0.0)
                nc.vector.memset(u[:, :, S + 1:S + 2], 0.0)
                for j in range(2):
                    ve.wait_ge(*cc_ready(l, j + 1))
                    ve.wait_ge(*unit_psum(l, 2 * j + 2))
                    nc.vector.tensor_tensor(u[:, 2 * j:2 * j + 2, 1:S + 1],
                                            psum[:, 1, :].rearrange("p (c s) -> p c s", c=2),
                                            cc_tmp[:, j, :].rearrange("p (c s) -> p c s", c=2), ALU.mult) \
                        .then_inc(u_ready.sem, 1)
                ve.wait_ge(*u_ready(l, 2))
                for k in range(3):
                    for m in range(NB):
                        w = col("conv", l, k * NB + m)
                        if k == 0:
                            ins = nc.vector.tensor_scalar(yc[:, m, :], u[:, m, 0:S], w, None, ALU.mult)
                        else:
                            ins = nc.vector.scalar_tensor_tensor(out=yc[:, m, :], in0=u[:, m, k:k + S], scalar=w,
                                                                 in1=yc[:, m, :], op0=ALU.mult, op1=ALU.add)
                    link(ins)
                for j in range(2):
                    ve.wait_ge(*unit_psum(l, 5 + j))
                    nc.vector.tensor_tensor(yc[:, 2 * j:2 * j + 2, :], psum[:, j, :].rearrange("p (c s) -> p c s", c=2),
                                            yc[:, 2 * j:2 * j + 2, :], ALU.mult).then_inc(conv_ready.sem, 1)

                for t in range(T):
                    ve.wait_ge(*qk_squares(l, t + 1))
                    link(nc.vector.tensor_reduce(rstd[:, :], sq[:, :, :], AX.X, ALU.add))
                    mean_squares(l, 3 + t, [(mean_sq[:, :], rstd[:, :], DH)])
                    flat = qk[:, t].rearrange("p a h d -> p (a h) d")
                    link(nc.vector.tensor_tensor(flat, flat, rstd[:, :].unsqueeze(2).broadcast_to([P, 2 * NH, DH]),
                                                 ALU.mult))
                    for a in range(2):
                        ins = nc.vector.tensor_tensor(qk[:, t, a], qk[:, t, a],
                                                      head_gain[:, l, a, :].unsqueeze(1).broadcast_to([P, NH, DH]),
                                                      ALU.mult)
                    link(ins)
                    if l == 0 and t == 0:
                        ve.wait_ge(*rope_ready(0))
                    x1, x2 = flat[:, :, ND:ND + HALF], flat[:, :, ND + HALF:]
                    cos, sin = (cos_sin[:, t, k, :].unsqueeze(1).broadcast_to([P, 2 * NH, HALF]) for k in range(2))
                    tmp = [rot_tmp[:, k] for k in range(4)]
                    for dst, a, b in ((tmp[0], x1, cos), (tmp[1], x2, sin), (tmp[2], x2, cos), (tmp[3], x1, sin)):
                        ins = nc.vector.tensor_tensor(dst, a, b, ALU.mult)
                    link(ins)
                    nc.vector.tensor_tensor(x1, tmp[0], tmp[1], ALU.subtract)
                    nc.vector.tensor_tensor(x2, tmp[2], tmp[3], ALU.add).then_inc(qk_ready.sem, 1)

                def gate_a(j):
                    ve.wait_ge(*ga_tanh(l, j + 1))
                    ve.wait_ge(*ya_ready(l, j + 1))
                    m = merged[:, 2 * j:2 * j + 2, :].rearrange("p c s -> p (c s)")
                    nc.vector.scalar_tensor_tensor(out=m, in0=tanh_a[:, j % 2, :], scalar=1.0, in1=m,
                                                   op0=ALU.add, op1=ALU.mult).then_inc(ga_used.sem, 1)

                def copy_oT(j):
                    ve.wait_ge(*pv_psum(l, 2 * j + 2))
                    nc.vector.tensor_copy(oT[:, j, :], psum[:, 7, 0:S]).then_inc(oT_ready.sem, 1)

                def scale_rows(s, i, parts=range(2)):
                    ve.wait_ge(*loaded(("ada", s, i)))
                    w = slot(("ada", s, i), 2)
                    for k in parts:
                        q = 2 * i + k
                        if q == 0:
                            ins = nc.vector.tensor_scalar(ada_acc, w[:, 0, :], c_act[:, 0, 0:1], None, ALU.mult)
                        else:
                            ins = nc.vector.scalar_tensor_tensor(out=ada_acc, in0=w[:, k, :], scalar=c_act[:, q, 0:1],
                                                                 in1=ada_acc, op0=ALU.mult, op1=ALU.add)
                        if k == 0:
                            link(ins)
                        else:
                            ins.then_inc(ada_scaled.sem, 1)
                            ve.wait_ge(*ada_scaled(s // 3, 4 * (s % 3) - 3 + i))

                gate_a(0)
                for h in range(NH):
                    ve.wait_ge(*scores_psum(l, h + 1))
                    link(nc.vector.tensor_reduce(top[:, h % 2, :], psum[:, 4 + h % 2, :].rearrange("p (t s) -> p t s", t=T),
                                                 AX.X, ALU.max))
                    nc.vector.tensor_scalar(bias_m[:, h % 2, :], top[:, h % 2, :], -SCALE, None, ALU.mult) \
                        .then_inc(bias_ready.sem, 1)
                    ve.wait_ge(*exp_done(l, h + 1))
                    link(nc.vector.reciprocal(denom[:, h % 2, :], denom[:, h % 2, :]))
                    for t in range(T):
                        ins = nc.vector.tensor_scalar(probs[:, h % 2, t, :], probs[:, h % 2, t, :],
                                                      denom[:, h % 2, t:t + 1], None, ALU.mult)
                    ins.then_inc(probs_ready.sem, 1)
                    if h < 3:
                        gate_a(1 + h)
                    if h < 4:
                        if h == 0:
                            ve.wait_ge(*unit_psum(l, 10))
                        scale_rows(3 * l + 1, h)
                    elif h < 6:
                        if h == 4:
                            add_bias(3 * l + 1, 3)
                        scale_rows(3 * l + 2, h - 4)
                    if h >= 2 and h % 2 == 0:
                        copy_oT(h // 2 - 1)
                copy_oT(NH // 2 - 1)

                for j in range(4):
                    ve.wait_ge(*unit_psum(l, 19 + j))
                    ve.wait_ge(*gb_tanh(l, j + 1))
                    nc.vector.scalar_tensor_tensor(out=cc_tmp[:, j % 2, :],
                                                   in0=tanh_b[:, 2 * j:2 * j + 2, :].rearrange("p c s -> p (c s)"),
                                                   scalar=1.0, in1=psum[:, j % 2, :], op0=ALU.add, op1=ALU.mult) \
                        .then_inc(yb_gated.sem, 1)
                    ve.wait_ge(*yb_gated(l, j + 1))
                    m = merged[:, 2 * j:2 * j + 2, :].rearrange("p c s -> p (c s)")
                    nc.vector.scalar_tensor_tensor(out=m, in0=cc_tmp[:, j % 2, :], scalar=0.5, in1=m,
                                                   op0=ALU.mult, op1=ALU.add).then_inc(merged_ready.sem, 1)
                    if j < 2:
                        scale_rows(3 * l + 2, 2, [j])
                scale_rows(3 * l + 2, 3)

                def add_gated(which, sig, order, done, first=0):
                    ve.wait_ge(*gate_ready(l, which + 1))
                    for n, (t, half) in enumerate(order):
                        if sig is mix_psum:
                            ve.wait_ge(*sig(l, first + n + 1))
                        tmp = cc_tmp[:, n % 2, :]
                        xs = x_sb[:, t, half * BANK:(half + 1) * BANK]
                        link(nc.vector.tensor_tensor(tmp, psum[:, 2 * t + half, :],
                                                     gate_rows[:, which, half * BANK:(half + 1) * BANK], ALU.mult))
                        ins = nc.vector.tensor_tensor(xs, xs, tmp, ALU.add)
                    if done:
                        ins.then_inc(done.sem, 1)
                    else:
                        link(ins)

                add_gated(0, mix_psum, [(t, 0) for t in range(T)], None)
                add_bias(3 * l + 2, 4)
                add_gated(0, mix_psum, [(t, 1) for t in range(T)], mix_added, T)

                norm_x(l, 1)
                gains(3 * l + 2)
                if l + 1 < L:
                    add_bias(3 * l + 3, 7)
                modulate_half(l, 1)

                if l + 1 < L:
                    gains(3 * l + 3)
                nc.vector.tensor_scalar(x_masked.bitcast(I32), xn.bitcast(I32), HIGH_BITS, None, ALU.bitwise_and) \
                    .then_inc(masked_ready.sem, 1)
                ve.wait_ge(*masked_ready(l))
                nc.vector.tensor_tensor(x_low[:, :, :], xn, x_masked, ALU.subtract).then_inc(low_ready.sem, 1)
                ve.wait_ge(*router_exp(l))
                R = lambda k: r_small[:, k, :]
                link(nc.vector.tensor_scalar(R(1), R(0), 1.0, None, ALU.add))
                link(nc.vector.reciprocal(R(2), R(1)))
                link(nc.vector.tensor_tensor(R(3).rearrange("p (t e) -> p t e", t=T),
                                             R(2).rearrange("p (t e) -> p t e", t=T),
                                             b_router_sb[:, :].unsqueeze(1).broadcast_to([P, T, E]), ALU.add))

                def first_ranks(values, groups, n, rank):
                    full = [P, groups, n, n]
                    v = values.rearrange("p (g i) -> p g i", i=n)
                    vi, vj = v.unsqueeze(3).broadcast_to(full), v.unsqueeze(2).broadcast_to(full)
                    low = lower[:, :, :].unsqueeze(1).broadcast_to(full)
                    a, b, d = (pairwise[:, k, 0:groups] for k in range(3))
                    nc.vector.tensor_tensor(a, vj, vi, ALU.is_gt)
                    link(nc.vector.tensor_tensor(b, vj, vi, ALU.is_equal))
                    link(nc.vector.tensor_tensor(d, b, low, ALU.mult))
                    link(nc.vector.tensor_tensor(b, a, d, ALU.add))
                    link(nc.vector.tensor_reduce(rank.rearrange("p (g i) -> p g i", i=n), b, AX.X, ALU.add))

                first_ranks(R(3), T * GRP, EPG, R(4))
                link(nc.vector.tensor_scalar(R(5), R(4), 2.0, None, ALU.is_lt))
                link(nc.vector.tensor_tensor(R(6), R(5), R(3), ALU.mult))
                sums = R(7)[:, 0:T * GRP]
                link(nc.vector.tensor_reduce(sums, R(6).rearrange("p (g i) -> p g i", i=EPG), AX.X, ALU.add))
                g_rank, g_sel = R(8)[:, 0:T * GRP], R(9)[:, 0:T * GRP]
                first_ranks(sums, T, GRP, g_rank)
                link(nc.vector.tensor_scalar(g_sel, g_rank, 1.0, None, ALU.is_lt))
                sel = R(10)
                link(nc.vector.tensor_tensor(sel.rearrange("p (g i) -> p g i", i=EPG),
                                             R(5).rearrange("p (g i) -> p g i", i=EPG),
                                             g_sel.unsqueeze(2).broadcast_to([P, T * GRP, EPG]), ALU.mult))
                nc.vector.tensor_copy(sel_b[:, :, :].rearrange("p t e -> p (t e)"), sel).then_inc(chosen.sem, 1)
                link(nc.vector.tensor_tensor(R(6), sel, R(2), ALU.mult))
                link(nc.vector.tensor_reduce(R(7)[:, 0:T], R(6).rearrange("p (t e) -> p t e", t=T), AX.X, ALU.add))
                link(nc.vector.reciprocal(R(7)[:, 0:T], R(7)[:, 0:T]))
                link(nc.vector.tensor_tensor(combine[:, :, :], R(6).rearrange("p (t e) -> p t e", t=T),
                                             R(7)[:, 0:T].unsqueeze(2).broadcast_to([P, T, E]), ALU.mult))

                ve.wait_ge(*rank_psum(l))
                link(nc.vector.scalar_tensor_tensor(out=slot_of[:, :, :], in0=sel.rearrange("p (t e) -> p t e", t=T),
                                                    scalar=float(-2 * S),
                                                    in1=psum[:, 7, 0:T * E].rearrange("p (t e) -> p t e", t=T),
                                                    op0=ALU.mult, op1=ALU.add))
                nc.vector.tensor_copy(lengths[:, :], psum[:, 7, T * E:(T + 1) * E]).then_inc(ranks_read.sem, 1)
                for t in range(T):
                    ins = nc.vector.tensor_tensor(onehot[:, t], slot_id[:, :].unsqueeze(1).broadcast_to([P, E, SLOTS]),
                                                  slot_of[:, t, :].unsqueeze(2).broadcast_to([P, E, SLOTS]),
                                                  ALU.is_equal)
                ins.then_inc(onehot_ready.sem, 1)
                ve.wait_ge(*s_tanh_ready(l))
                ve.wait_ge(*s_up_psum(l))
                flat_act = s_act.rearrange("p c s -> p (c s)")
                link(nc.vector.scalar_tensor_tensor(out=flat_act, in0=s_tanh.rearrange("p c s -> p (c s)"), scalar=1.0,
                                                    in1=psum[:, 4, :], op0=ALU.add, op1=ALU.mult))
                nc.vector.scalar_tensor_tensor(out=flat_act, in0=flat_act, scalar=0.5, in1=psum[:, 5, :],
                                               op0=ALU.mult, op1=ALU.mult).then_inc(s_act_ready.sem, 1)
                ve.wait_ge(*onehot_ready(l))
                for t in range(T):
                    ins = nc.vector.tensor_tensor(weighted[:, t], onehot[:, t].bitcast(F32),
                                                  combine[:, t, :].unsqueeze(2).broadcast_to([P, E, SLOTS]), ALU.mult)
                ins.then_inc(weighted_ready.sem, 1)

                for n in range(1, 2 * C, 2):
                    half, q = divmod(n, C)
                    ve.wait_ge(*gather_psum(l, n + 1))
                    nc.vector.tensor_scalar(hE[:, q, half * 8:half * 8 + 8, :].rearrange("p e s -> p (e s)"),
                                            psum[:, 4 + n % 4, :], gain[:, l % 2, 1, q:q + 1],
                                            sh_of(l, 1)[:, q:q + 1], ALU.mult, ALU.add).then_inc(hE_dve.sem, 1)
                for b in range(4):
                    ve.wait_ge(*weights_read(l, b + 1))
                    nc.vector.tensor_scalar(combT[:, 2 * b:2 * b + 2, :], combT_weighted[:, 2 * b:2 * b + 2, :], 0.0, None,
                                            ALU.is_gt).then_inc(combT_ready.sem, 1)

                def list_extras():
                    f3 = flags.rearrange("p (e g) -> p e g", e=E)
                    link(nc.vector.tensor_scalar(lengths[:, :], lengths[:, :], 1.0 / SLOTS, None, ALU.mult))
                    for k in range(2):
                        nc.vector.memset(run_sums[k][:, 0:LEAD], 0.0)
                    link(nc.vector.tensor_tensor(f3, lengths[:, :].unsqueeze(2).broadcast_to([P, E, GROUPS - 1]),
                                                 count_up[:, 1:GROUPS].unsqueeze(1).broadcast_to([P, E, GROUPS - 1]),
                                                 ALU.is_gt))
                    link(nc.vector.tensor_copy(run_sums[0][:, LEAD:], flags))
                    a, b, shift = run_sums[0], run_sums[1], 1
                    while shift < NF:
                        link(nc.vector.tensor_tensor(b[:, LEAD:], a[:, LEAD:], a[:, LEAD - shift:LEAD - shift + NF],
                                                     ALU.add))
                        a, b, shift = b, a, 2 * shift
                    full = [P, EXTRAS, E, GROUPS - 1]
                    m = match.rearrange("p k e g -> p k (e g)")
                    link(nc.vector.tensor_tensor(m, a[:, LEAD:].unsqueeze(1).broadcast_to([P, EXTRAS, NF]),
                                                 count_up[:, 1:EXTRAS + 1].unsqueeze(2).broadcast_to([P, EXTRAS, NF]),
                                                 ALU.is_equal))
                    link(nc.vector.tensor_tensor(m, m, flags.unsqueeze(1).broadcast_to([P, EXTRAS, NF]), ALU.mult))
                    nc.vector.tensor_reduce(is_expert, match, AX.X, ALU.add)
                    link(nc.vector.tensor_reduce(is_group, match.rearrange("p k e g -> p k g e"), AX.X, ALU.add))
                    nc.vector.tensor_tensor(is_group, is_group,
                                            count_up[:, 1:GROUPS].unsqueeze(1).broadcast_to([P, EXTRAS, GROUPS - 1]),
                                            ALU.mult)
                    link(nc.vector.tensor_tensor(scratch_e, is_expert,
                                                 count_up[:, 0:E].unsqueeze(1).broadcast_to([P, EXTRAS, E]), ALU.mult))
                    nc.vector.tensor_reduce(group_of, is_group, AX.X, ALU.add)
                    link(nc.vector.tensor_reduce(expert_f, scratch_e, AX.X, ALU.add))
                    nc.vector.tensor_copy(extra_expert[:, :], expert_f)
                    for src, dst in ((slot_of, slot_x), (combine, combine_x)):
                        for t in range(T):
                            link(nc.vector.tensor_tensor(scratch_e, is_expert,
                                                         src[:, t, :].unsqueeze(1).broadcast_to([P, EXTRAS, E]),
                                                         ALU.mult))
                            link(nc.vector.tensor_reduce(dst[:, t, :], scratch_e, AX.X, ALU.add))
                    link(nc.vector.tensor_scalar(group_of, group_of, float(-SLOTS), None, ALU.mult))
                    link(nc.vector.tensor_tensor(slot_x[:, :, :], slot_x[:, :, :],
                                                 group_of.unsqueeze(1).broadcast_to([P, T, EXTRAS]), ALU.add))
                    n_listed = a[:, LEAD + NF - 1:LEAD + NF]
                    nc.vector.tensor_copy(passes_before[:, :], passes_f[:, 0:1])
                    link(nc.vector.tensor_scalar(passes_f[:, 2:], count_up[:, 2:EXTRAS:2], n_listed, None, ALU.is_lt))
                    link(nc.vector.tensor_reduce(passes_f[:, 1:2], passes_f[:, 2:], AX.X, ALU.add))
                    link(nc.vector.tensor_tensor(passes_f[:, 0:1], passes_f[:, 0:1], passes_f[:, 1:2], ALU.add))
                    nc.vector.tensor_copy(n_extras[:, :], n_listed) \
                        .then_inc(extras_ready.sem, 1)

                for i in range(STEPS + 1):
                    if i == 2:
                        list_extras()
                        for t in range(T):
                            for k in range(2):
                                ins = nc.vector.tensor_scalar(onehot_x[:, t, k, :], slot_id[:, :],
                                                              slot_x[:, t, k:k + 1], None, ALU.is_equal)
                        ins.then_inc(first_onehot.sem, 1)
                        ve.wait_ge(*first_onehot(l))
                        for t in range(T):
                            for k in range(2):
                                ins = nc.vector.tensor_scalar(weighted_x[:, t, k, :], onehot_x[:, t, k, :].bitcast(F32),
                                                              combine_x[:, t, k:k + 1], None, ALU.mult)
                        ins.then_inc(first_weighted.sem, 1)
                    if i == 7:
                        ve.wait_ge(*first_weights(l))
                        nc.vector.tensor_scalar(combT[:, 0, :], combT_weighted_x, 0.0, None, ALU.is_gt) \
                            .then_inc(first_combT.sem, 1)
                    if i < STEPS:
                        ve.wait_ge(*tanh_ready(l, i + 1))
                        a = e_act[:, i % 2, :]
                        link(nc.vector.scalar_tensor_tensor(out=a, in0=e_tanh[:, i % 2, :], scalar=1.0,
                                                            in1=psum[:, 4 + i % 2, 0:F], op0=ALU.add, op1=ALU.mult))
                        nc.vector.scalar_tensor_tensor(out=a, in0=a, scalar=0.5, in1=psum[:, 4 + i % 2, F:2 * F],
                                                       op0=ALU.mult, op1=ALU.mult).then_inc(act_ready.sem, 1)
                    if i >= 1:
                        ve.wait_ge(*down_psum(l, 2 * i))
                        ve.wait_ge(*weights_read(l, 4))
                        nc.vector.tensor_scalar(y[:, BANK:], psum[:, 6, :], slot_weight[:, i - 1:i], None, ALU.mult) \
                            .then_inc(y_dve.sem, 1)
                        ve.wait_ge(*y_dve(l, i))
                        ve.wait_ge(*y_act(l, i))
                        if i >= 2:
                            ve.wait_ge(*y_high_ready(l, i - 1))
                        nc.vector.tensor_scalar(y_masked.bitcast(I32), y.bitcast(I32), HIGH_BITS, None,
                                                ALU.bitwise_and).then_inc(y_masked_ready.sem, 1)
                        ve.wait_ge(*y_masked_ready(l, i))
                        nc.vector.tensor_tensor(y_low[:, :], y, y_masked, ALU.subtract).then_inc(y_low_ready.sem, 1)

                ve.wait_ge(*extras_ready(l))
                listed = ve.value_load(n_extras[0:1, 0:1], min_val=0, max_val=EXTRAS)
                before = ve.value_load(passes_before[0:1, 0:1], min_val=0, max_val=L * ITERS)
                with ve.Fori(0, ITERS) as j:
                    with ve.If(listed > 2 * j + 2):
                        for t in range(T):
                            for k in range(2):
                                ins = nc.vector.tensor_scalar(onehot_x[:, t, k, :], slot_id[:, :],
                                                              slot_x[:, t, bass.ds(2 * j + (k + 2), 1)], None, ALU.is_equal)
                        ins.then_inc(x_onehot.sem, 1)
                        ve.wait_ge(x_onehot.sem, j + before + 1)
                        for t in range(T):
                            for k in range(2):
                                ins = nc.vector.tensor_scalar(weighted_x[:, t, k, :], onehot_x[:, t, k, :].bitcast(F32),
                                                              combine_x[:, t, bass.ds(2 * j + (k + 2), 1)], None, ALU.mult)
                        ins.then_inc(x_weighted.sem, 1)
                        ve.wait_ge(x_gathered.sem, j + before + 1)
                        for q in range(1, C, 2):
                            ins = nc.vector.tensor_scalar(hE[:, q, 0:2, :].rearrange("p e s -> p (e s)"),
                                                          psum[:, 4 + q % 2, (q // 2) * P:(q // 2 + 1) * P],
                                                          gain[:, l % 2, 1, q:q + 1], sh_of(l, 1)[:, q:q + 1],
                                                          ALU.mult, ALU.add)
                        ins.then_inc(x_tokens_dve.sem, 1)
                        ve.wait_ge(x_weights.sem, j + before + 1)
                        nc.vector.tensor_scalar(combT[:, 0, :], combT_weighted_x, 0.0, None, ALU.is_gt) \
                            .then_inc(x_combT.sem, 1)
                        ve.wait_ge(x_tanh.sem, j + before + 1)
                        nc.vector.scalar_tensor_tensor(out=e_act[:, 0, :], in0=e_tanh[:, 0, :], scalar=1.0,
                                                       in1=psum[:, 7, 0:F], op0=ALU.add, op1=ALU.mult) \
                            .then_inc(x_act1.sem, 1)
                        ve.wait_ge(x_act1.sem, j + before + 1)
                        nc.vector.scalar_tensor_tensor(out=e_act[:, 0, :], in0=e_act[:, 0, :], scalar=0.5,
                                                       in1=psum[:, 7, F:2 * F], op0=ALU.mult, op1=ALU.mult) \
                            .then_inc(x_act.sem, 1)
                        ve.wait_ge(x_down.sem, j + before + 1)
                        ve.wait_ge(x_weights.sem, j + before + 1)
                        nc.vector.tensor_scalar(y[:, BANK:], psum[:, 5, :], slot_weight[:, PAIRS:], None, ALU.mult) \
                            .then_inc(x_y_dve.sem, 1)
                        ve.wait_ge(x_y_dve.sem, j + before + 1)
                        ve.wait_ge(x_y_act.sem, j + before + 1)
                        nc.vector.tensor_scalar(y_masked.bitcast(I32), y.bitcast(I32), HIGH_BITS, None,
                                                ALU.bitwise_and).then_inc(x_y_masked.sem, 1)
                        ve.wait_ge(x_y_masked.sem, j + before + 1)
                        nc.vector.tensor_tensor(y_low[:, :], y, y_masked, ALU.subtract).then_inc(x_y_low.sem, 1)

                ve.wait_ge(*moe_psum(l))
                add_gated(1, moe_psum, [(t, h) for t in range(T) for h in range(2)], moe_added)

        @block.tensor
        def _(pe):
            def turn(dst, src):
                return nc.tensor.transpose(dst, src, ident[0:src.shape[0], 0:src.shape[0]])

            def ada_products(s, bank):
                for i in range(4):
                    pe.wait_ge(*loaded(("ada", s, i)))
                    w = slot(("ada", s, i), 2)
                    for k in range(2):
                        q = 2 * i + k
                        for j in range(4):
                            ins = nc.tensor.matmul(psum[32 * j:32 * j + 32, bank, :], c_act[:, q, :],
                                                   w[:, k, j * BANK:(j + 1) * BANK], start=q == 0, stop=q == C - 1)
                    ins.then_inc(ada_products_done.sem, 1)

            def ada_reduce(s, bank):
                pe.wait_ge(*ada_scaled(s // 3, 4 * (s % 3)))
                for j in range(4):
                    ins = nc.tensor.matmul(psum[32 * j:32 * j + 32, bank, :], ones_f[:, :],
                                           ada_acc[:, j * BANK:(j + 1) * BANK], start=True, stop=True)
                ins.then_inc(ada_in_psum.sem, 1)

            def ada_turn(s, bank):
                pe.wait_ge(*ada_row_ready(0, s + 1))
                for b in range(4):
                    ins = turn(psum[:, bank, b * P:(b + 1) * P], ada_row[:, b * P:(b + 1) * P])
                ins.then_inc(ada_turned.sem, 1)

            def turn_x(l, which):
                pe.wait_ge(*xn_ready(l, which + 1))
                for b in range(4):
                    for k in range(2):
                        for t in range(T):
                            q = 2 * b + k
                            ins = turn(psum[:, 3 + b, k * S + t * P:k * S + (t + 1) * P], xn[:, t, q * P:(q + 1) * P])
                    ins.then_inc(xnT_ready.sem, 1)

            def unit(l, n, w, src, k, a, blocks=range(2)):
                b = n % 2
                if n >= 2:
                    pe.wait_ge(*bank_emptied(l, n))
                for m in blocks:
                    for q in range(k):
                        ins = nc.tensor.matmul(psum[:, b, m * S:(m + 1) * S], w[:, q, a + m * P:a + (m + 1) * P],
                                               src[:, q, :], start=q == 0, stop=q == k - 1)
                if m == 1:
                    ins.then_inc(unit_psum.sem, 1)

            def bank_emptied(l, n):
                p = n - 2
                if p in (0, 2):
                    return cc_ready(l, p // 2 + 1)
                if p in (1, 3):
                    return u_ready(l, p // 2 + 1)
                if p in (4, 5):
                    return conv_ready(l, p - 3)
                if p < 10:
                    return ya_ready(l, p - 5)
                if p < 14:
                    return ga_tanh(l, p - 9)
                if p < 18:
                    return gb_tanh(l, p - 13)
                return yb_gated(l, p - 17)

            pe.wait_ge(*consts(0, 7))
            pe.wait_ge(c_loaded.sem, 16)
            turn(psum[:, 5, 0:C], c_rows).then_inc(c_psum.sem, 1)
            pe.wait_ge(*c_ready(0))
            ada_products(0, 7)
            pe.wait_ge(params_loaded.sem, 16 * (9 + T))
            turn(psum[:, 6, 0:NROWS], rows[0:NROWS, :]).then_inc(cols_psum.sem, 1)
            ada_turn(0, 7)

            for l in range(L):
                turn_x(l, 0)

                pe.wait_ge(*hT_act(l, 1))
                pe.wait_ge(*hT_dve(l, 1))
                pe.wait_ge(*loaded(("lat", l)))
                w = slot(("lat", l), C)
                for t in range(T):
                    for q in range(C):
                        ins = nc.tensor.matmul(psum[:, 2 + t, 0:LAT], hT[:, q, t * P:(t + 1) * P], w[:, q, 0:LAT],
                                               start=q == 0, stop=q == C - 1)
                    ins.then_inc(lat_psum.sem, 1)

                def conv_unit(n, key, a):
                    pe.wait_ge(*loaded((key, l)))
                    unit(l, n, slot((key, l), C), hT, C, a)

                conv_unit(0, "cc", 0)
                conv_unit(1, "cx", 0)
                for t in range(T):
                    pe.wait_ge(*lat_ready(l, t + 1))
                    for b in range(QB + 1):
                        ins = turn(psum[:, 4 + t, b * P:(b + 1) * P], lat_n[:, t, b * P:(b + 1) * P])
                    ins.then_inc(latT_psum.sem, 1)
                conv_unit(2, "cc", S)
                conv_unit(3, "cx", S)

                def up_q(t, bank):
                    for a, n in ((0, BANK), (BANK, NH * DH - BANK)):
                        for q in range(QB):
                            ins = nc.tensor.matmul(psum[:, bank + a // BANK, 0:n], latT[:, q, t * P:(t + 1) * P],
                                                   uq_sb[:, q, a:a + n], start=q == 0, stop=q == QB - 1)
                    ins.then_inc(up_psum.sem, 1)

                def up_kv(t, bank):
                    for a in range(2):
                        ins = nc.tensor.matmul(psum[:, bank + a, :], latT[:, QB, t * P:(t + 1) * P],
                                               ukv_sb[:, a * BANK:(a + 1) * BANK], start=True, stop=True)
                    ins.then_inc(up_psum.sem, 1)

                pe.wait_ge(*latT_ready(l, T))
                pe.wait_ge(latw_loaded.sem, 32 * (l + 1))
                up_q(0, 2)
                up_kv(0, 4)
                up_q(1, 6)
                conv_unit(4, "cb", 0)
                pe.wait_ge(*qkv_copied(l, 1))
                up_kv(1, 2)
                conv_unit(5, "cb", S)

                pe.wait_ge(*loaded(("conv", l)))
                pe.wait_ge(*conv_ready(l, 2))
                for j in range(4):
                    unit(l, 6 + j, slot(("conv", l), NB), yc, NB, j * S)

                def gate_unit(n, blocks=range(2)):
                    key = ("ga%d" if n < 14 else "gb%d") % ((n - 10) % 4 // 2)
                    pe.wait_ge(*loaded((key, l)))
                    unit(l, n, slot((key, l), C), hT, C, (n % 2) * S, blocks)

                def turn_qk(h):
                    if h:
                        pe.wait_ge(*qkT_ready(l, h))
                    for a in range(2):
                        for t in range(T):
                            ins = turn(psum[0:DH, 2, a * S + t * P:a * S + (t + 1) * P], qk[:, t, a, h, :])
                    ins.then_inc(qkT_psum.sem, 1)

                def turn_probs(h):
                    pe.wait_ge(*probs_ready(l, h + 1))
                    if h:
                        pe.wait_ge(*pT_ready(l, h))
                    for k in range(T):
                        for t in range(T):
                            ins = turn(psum[:, 6, k * S + t * P:k * S + (t + 1) * P],
                                       probs[:, h % 2, t, k * P:(k + 1) * P])
                    ins.then_inc(pT_psum.sem, 1)

                def apply_probs(h):
                    pe.wait_ge(*pT_ready(l, h + 1))
                    if h >= 2 and h % 2 == 0:
                        pe.wait_ge(*oT_ready(l, h // 2))
                    a = (h % 2) * VD
                    for k in range(T):
                        ins = nc.tensor.matmul(psum[a:a + VD, 7, 0:S], v_sb[:, k, h, :], probsT[:, h % 2, k, :],
                                               start=k == 0, stop=k == T - 1)
                    ins.then_inc(pv_psum.sem, 1)

                gate_unit(10)
                pe.wait_ge(*qk_ready(l, T))
                pe.wait_ge(*qkv_copied(l, 4))
                turn_qk(0)
                for h in range(NH):
                    if h + 1 < NH:
                        turn_qk(h + 1)
                    pe.wait_ge(*qkT_ready(l, h + 1))
                    if h >= 2:
                        pe.wait_ge(*exp_done(l, h - 1))
                    for t in range(T):
                        ins = nc.tensor.matmul(psum[:, 4 + h % 2, t * S:(t + 1) * S],
                                               qkT[0:DH, h % 2, 0, t * P:(t + 1) * P], qkT[0:DH, h % 2, 1, :],
                                               start=True, stop=True)
                    ins.then_inc(scores_psum.sem, 1)
                    if h < 6:
                        gate_unit(11 + h)
                    else:
                        gate_unit(17, [h - 6])
                    if h == 4:
                        ada_reduce(3 * l + 1, 3)
                    elif h == 5:
                        ada_turn(3 * l + 1, 3)
                    turn_probs(h)
                    if h:
                        apply_probs(h - 1)
                apply_probs(NH - 1)

                pe.wait_ge(*oT_ready(l, NH // 2))
                pe.wait_ge(*loaded(("attn", l)))
                for j in range(4):
                    unit(l, 18 + j, slot(("attn", l), NB), oT, NB, j * S)

                pe.wait_ge(*merged_ready(l, 4))
                pe.wait_ge(*mod_ready(0, 3 * l + 2))
                for half in range(2):
                    if half:
                        ada_reduce(3 * l + 2, 4)
                    pe.wait_ge(*loaded((f"wo{half}", l)))
                    w = slot((f"wo{half}", l), C)
                    for t in range(T):
                        for q in range(C):
                            ins = nc.tensor.matmul(psum[:, 2 * t + half, :], merged[:, q, t * P:(t + 1) * P], w[:, q, :],
                                                   start=q == 0, stop=q == C - 1)
                        ins.then_inc(mix_psum.sem, 1)
                        if half and t == 0:
                            ada_turn(3 * l + 2, 4)

                if l + 1 < L:
                    ada_products(3 * l + 3, 7)
                pe.wait_ge(*mod_ready(0, 3 * l + 3))
                turn_x(l, 1)
                if l + 1 < L:
                    ada_turn(3 * l + 3, 7)
                pe.wait_ge(*hT_act(l, 2))
                pe.wait_ge(*hT_dve(l, 2))
                for q in range(C):
                    ins = nc.tensor.matmul(psum[0:E, 5, 0:S], router_sb[:, q, :], hT[:, q, :], start=q == 0,
                                           stop=q == C - 1)
                ins.then_inc(router_psum.sem, 1)
                pe.wait_ge(*loaded(("shared", l)))
                w = slot(("shared", l), C)

                def shared_block(m, bank, sig=None):
                    for q in range(C):
                        ins = nc.tensor.matmul(psum[:, bank, (m % FC) * S:(m % FC + 1) * S], w[:, q, m * P:(m + 1) * P],
                                               hT[:, q, :], start=q == 0, stop=q == C - 1)
                    if sig:
                        ins.then_inc(sig.sem, 1)

                shared_block(0, 4)
                pe.wait_ge(*router_copied(l))
                for t in range(T):
                    ins = turn(psum[:, 6, t * E:(t + 1) * E], router_out[0:E, t * P:(t + 1) * P])
                ins.then_inc(routerT_psum.sem, 1)
                shared_block(1, 4, s_gate_psum)
                shared_block(2, 5)
                pe.wait_ge(*chosen(l))
                if l + 1 < L:
                    pe.wait_ge(*mod_ready(0, 3 * l + 4))
                nc.tensor.matmul(psum[:, 7, 0:E], tri[:, :], sel_b[:, 0, :], start=True, stop=True)
                nc.tensor.matmul(psum[:, 7, E:2 * E], ones[:, :], sel_b[:, 0, :], start=True, stop=False)
                nc.tensor.matmul(psum[:, 7, E:2 * E], tri[:, :], sel_b[:, 1, :], start=False, stop=True)
                nc.tensor.matmul(psum[:, 7, 2 * E:3 * E], ones[:, :], sel_b[:, 0, :], start=True, stop=False)
                nc.tensor.matmul(psum[:, 7, 2 * E:3 * E], ones[:, :], sel_b[:, 1, :], start=False, stop=True) \
                    .then_inc(rank_psum.sem, 1)
                shared_block(3, 5, s_up_psum)
                pe.wait_ge(*s_act_ready(l))
                pe.wait_ge(sdown_loaded.sem, 16 * (l + 1))
                for t in range(T):
                    for half in range(2):
                        for q in range(FC):
                            ins = nc.tensor.matmul(psum[:, 2 * t + half, :], s_act[:, q, t * P:(t + 1) * P],
                                                   sdown_sb[:, q, half * BANK:(half + 1) * BANK],
                                                   start=q == 0, stop=False)
                ins.then_inc(s_down_psum.sem, 1)

                pe.wait_ge(*onehot_ready(l))
                pe.wait_ge(*ranks_read(l))
                pe.wait_ge(*high_ready(l))
                pe.wait_ge(*low_ready(l))
                for n in range(2 * C):
                    half, q = divmod(n, C)
                    if n >= 4:
                        pe.wait_ge(*(hE_act if n % 2 == 0 else hE_dve)(l, (n - 4) // 2 + 1))
                    for t in range(T):
                        for part_x in (x_high, x_low):
                            ins = nc.tensor.matmul(psum[:, 4 + n % 4, :], part_x[:, t, q * P:(q + 1) * P],
                                                   onehot[:, t, half * 8:half * 8 + 8, :]
                                                   .rearrange("p e s -> p (e s)"),
                                                   start=t == 0 and part_x is x_high,
                                                   stop=t == T - 1 and part_x is x_low)
                    ins.then_inc(gather_psum.sem, 1)
                pe.wait_ge(*weighted_ready(l))
                for b in range(4):
                    pe.wait_ge(*(hE_act if b % 2 == 0 else hE_dve)(l, (2 * C - 4 + b) // 2 + 1))
                    for k in range(2):
                        for t in range(T):
                            j = 2 * b + k
                            ins = turn(psum[:, 4 + b, k * S + t * P:k * S + (t + 1) * P],
                                       weighted[:, t, 2 * j:2 * j + 2, :].rearrange("p e s -> p (e s)"))
                    ins.then_inc(combT_psum.sem, 1)

                def turned_read(b):
                    pe.wait_ge(*weights_read(l, b + 1))

                def gate_up(i):
                    if i >= 2:
                        pe.wait_ge(*act_ready(l, i - 1))
                    else:
                        turned_read(i)
                    if i == PAIRS:
                        pe.wait_ge(*first_tokens(l, 2))
                    for part_no in range(2):
                        pe.wait_ge(*loaded(("gu", l, i, part_no)))
                        w = ring[:, number["gu", l, i, part_no] % RING, :].rearrange("p (k c n) -> p k c n", k=2, n=BANK)
                        for m in range(C // 2):
                            q = part_no * C // 2 + m
                            for k in range(2):
                                ins = nc.tensor.matmul(psum[k * SLOTS:(k + 1) * SLOTS, 4 + i % 2, :],
                                                       hE[:, q, (2 * i + k) % E, :], w[:, k, m, :], start=q == 0,
                                                       stop=q == C - 1)
                        ins.then_inc(gu_psum.sem, 1)

                def turn_act(i):
                    pe.wait_ge(*act_ready(l, i + 1))
                    if i:
                        pe.wait_ge(*y_dve(l, i))
                    else:
                        turned_read(2)
                    for q in range(FC):
                        ins = turn(psum[:, 6, q * P:(q + 1) * P], e_act[:, i % 2, q * P:(q + 1) * P])
                    ins.then_inc(aT_psum.sem, 1)

                def down(i):
                    pe.wait_ge(*loaded(("down", l, i)))
                    pe.wait_ge(*aT_ready(l, i + 1))
                    w = slot(("down", l, i), 2 * FC)
                    if i:
                        pe.wait_ge(*y_act(l, i))
                    else:
                        turned_read(3)
                    if i in (3, 4):
                        pe.wait_ge(*first_tokens(l, i - 2))
                    elif i == 5:
                        pe.wait_ge(*first_weights(l))
                    for half in range(2):
                        for q in range(FC):
                            for k in range(2):
                                ins = nc.tensor.matmul(psum[k * SLOTS:(k + 1) * SLOTS, 7 - half, :],
                                                       aT[:, q, k * SLOTS:(k + 1) * SLOTS],
                                                       w[:, k * FC + q, half * BANK:(half + 1) * BANK],
                                                       start=q == 0, stop=q == FC - 1)
                        ins.then_inc(down_psum.sem, 1)

                def add_tokens(i):
                    pe.wait_ge(*combT_ready(l, 4))
                    if i == PAIRS:
                        pe.wait_ge(*first_combT(l))
                    pe.wait_ge(*y_high_ready(l, i + 1))
                    pe.wait_ge(*y_low_ready(l, i + 1))
                    for t in range(T):
                        for half in range(2):
                            for part_y in (y_high, y_low):
                                ins = nc.tensor.matmul(psum[:, 2 * t + half, :], combT[:, i % PAIRS, t * P:(t + 1) * P],
                                                       part_y[:, half * BANK:(half + 1) * BANK], start=False,
                                                       stop=i == STEPS - 1 and part_y is y_low)
                    ins.then_inc(added_psum.sem, 1)

                def first_extras(i):
                    pe.wait_ge(*y_act(l, i - 1))
                    if i < 6:
                        pe.wait_ge(*first_onehot(l))
                        for m in range(C // 2):
                            q = (i - 4) * C // 2 + m
                            for t in range(T):
                                for part_x in (x_high, x_low):
                                    ins = nc.tensor.matmul(psum[:, 7, m * P:(m + 1) * P],
                                                           part_x[:, t, q * P:(q + 1) * P],
                                                           onehot_x[:, t].rearrange("p e s -> p (e s)"),
                                                           start=t == 0 and part_x is x_high,
                                                           stop=t == T - 1 and part_x is x_low)
                        ins.then_inc(first_gathered.sem, 1)
                    else:
                        pe.wait_ge(*first_weighted(l))
                        for t in range(T):
                            ins = turn(psum[:, 7, t * P:(t + 1) * P], weighted_x[:, t].rearrange("p e s -> p (e s)"))
                        ins.then_inc(first_turned.sem, 1)

                for i in range(STEPS + 2):
                    if i < STEPS:
                        gate_up(i)
                    if 1 <= i <= STEPS:
                        turn_act(i - 1)
                    if i >= 2:
                        add_tokens(i - 2)
                    if i in (4, 5, 6):
                        first_extras(i)
                    if 1 <= i <= STEPS:
                        down(i - 1)

                pe.wait_ge(*extras_ready(l))
                listed = pe.value_load(n_extras[0:1, 0:1], min_val=0, max_val=EXTRAS)
                before = pe.value_load(passes_before[0:1, 0:1], min_val=0, max_val=L * ITERS)
                first = number["down", l, PAIRS] - 2
                with pe.Fori(0, ITERS) as j:
                    with pe.If(listed > 2 * j + 2):
                        pe.wait_ge(x_onehot.sem, j + before + 1)
                        for q in range(C):
                            for t in range(T):
                                for part_x in (x_high, x_low):
                                    ins = nc.tensor.matmul(psum[:, 4 + q % 2, (q // 2) * P:(q // 2 + 1) * P],
                                                           part_x[:, t, q * P:(q + 1) * P],
                                                           onehot_x[:, t].rearrange("p e s -> p (e s)"),
                                                           start=t == 0 and part_x is x_high,
                                                           stop=t == T - 1 and part_x is x_low)
                        ins.then_inc(x_gathered.sem, 1)
                        pe.wait_ge(x_weighted.sem, j + before + 1)
                        for t in range(T):
                            ins = turn(psum[:, 6, t * P:(t + 1) * P], weighted_x[:, t].rearrange("p e s -> p (e s)"))
                        ins.then_inc(x_turned.sem, 1)
                        pe.wait_ge(x_tokens_act.sem, j + before + 1)
                        pe.wait_ge(x_tokens_dve.sem, j + before + 1)
                        pe.wait_ge(x_loaded_w.sem, j * F_LOADED + before * F_LOADED + F_LOADED)
                        for q in range(C):
                            for k in range(2):
                                w = ring[:, (first + k) % RING, :].rearrange("p (c n) -> p c n", c=C)
                                ins = nc.tensor.matmul(psum[k * SLOTS:(k + 1) * SLOTS, 7, :], hE[:, q, k, :],
                                                       w[:, q, :], start=q == 0, stop=q == C - 1)
                        ins.then_inc(x_gu.sem, 1)
                        pe.wait_ge(x_act.sem, j + before + 1)
                        for q in range(FC):
                            ins = turn(psum[:, 6, q * P:(q + 1) * P], e_act[:, 0, q * P:(q + 1) * P])
                        ins.then_inc(x_aT_psum.sem, 1)
                        pe.wait_ge(x_aT.sem, j + before + 1)
                        w = ring[:, (first + 2) % RING, :].rearrange("p (k n) -> p k n", k=2 * FC)
                        for half in range(2):
                            for q in range(FC):
                                for k in range(2):
                                    ins = nc.tensor.matmul(psum[k * SLOTS:(k + 1) * SLOTS, 4 + half, :],
                                                           aT[:, q, k * SLOTS:(k + 1) * SLOTS],
                                                           w[:, k * FC + q, half * BANK:(half + 1) * BANK],
                                                           start=q == 0, stop=q == FC - 1)
                        ins.then_inc(x_down.sem, 1)
                        pe.wait_ge(x_combT.sem, j + before + 1)
                        pe.wait_ge(x_y_high.sem, j + before + 1)
                        pe.wait_ge(x_y_low.sem, j + before + 1)
                        for t in range(T):
                            for half in range(2):
                                for part_y in (y_high, y_low):
                                    ins = nc.tensor.matmul(psum[:, 2 * t + half, :], combT[:, 0, t * P:(t + 1) * P],
                                                           part_y[:, half * BANK:(half + 1) * BANK], start=False,
                                                           stop=True, skip_group_check=True)
                        ins.then_inc(x_free.sem, 1)
                turn(psum[:, 4, 0:P], ident[:, :]).then_inc(moe_psum.sem, 1)


_INS = ["x", "c", "positions", "w_ada", "b_ada", "g_mix", "g_ffn", "w_in", "conv_w", "g_q_a", "w_uq", "g_kv_a",
        "w_ukv", "g_qn", "g_kn", "w_conv_out", "w_attn_out", "w_o", "w_router", "b_router", "w_e_gate", "w_e_up",
        "w_e_down", "w_s_gate", "w_s_up", "w_s_down"]


def kernel(**inputs):
    import concourse.bacc as bacc
    from concourse.bass_utils import run_bass_kernel_spmd

    nc = bacc.Bacc("TRN2", target_bir_lowering=False, num_devices=1)
    arrays, args = {}, []
    for name in _INS:
        a = np.ascontiguousarray(inputs[name])
        arrays[f"in_{name}"] = a
        args.append(nc.dram_tensor(f"in_{name}", a.shape, mybir.dt.from_np(a.dtype), kind="ExternalInput").ap())
    shape = arrays["in_x"].shape
    args.append(nc.dram_tensor("out_0", shape, F32, kind="ExternalOutput").ap())
    trunk(nc, *args)
    r = run_bass_kernel_spmd(nc, [arrays], core_ids=[0])
    return r.results[0]["out_0"]
```

```python
from contextlib import ExitStack

import numpy as np

import concourse.bass as bass
from concourse import mybir
from concourse.alu_op_type import AluOpType as ALU

ACT = mybir.ActivationFunctionType
AX = mybir.AxisListType
F32 = mybir.dt.float32
BF16 = mybir.dt.bfloat16
I32 = mybir.dt.int32
F32R = mybir.dt.float32r

P = 128
EPS = 1e-6
ROPE_THETA = 10000.0
BANK = 512
SLOTS = 64
HIGH_BITS = -4096
CHUNK = 4096
RING = 5


class Signal:

    def __init__(self, sem, per_layer=1):
        self.sem, self.per_layer = sem, per_layer

    def __call__(self, layer, n=1):
        return self.sem, layer * self.per_layer + n


def trunk(nc, x, c, positions, w_ada, b_ada, g_mix, g_ffn, w_in, conv_w, g_q_a, w_uq, g_kv_a, w_ukv,
          g_qn, g_kn, w_conv_out, w_attn_out, w_o, w_router, b_router, w_e_gate, w_e_up, w_e_down,
          w_s_gate, w_s_up, w_s_down, out):
    _, S, D = x.shape
    L = w_in.shape[0]
    CW = w_conv_out.shape[1]
    QR, KR = w_uq.shape[1], w_ukv.shape[1]
    E, F = w_e_gate.shape[1], w_e_gate.shape[3]
    DH = g_qn.shape[1]
    NH = w_uq.shape[2] // DH
    VD = w_attn_out.shape[1] // NH
    ND = w_ukv.shape[2] // NH - VD
    RD = DH - ND
    HALF = RD // 2
    GRP = 4
    EPG = E // GRP
    T = S // P
    C = D // P
    NB = CW // P
    LAT = QR + KR + RD
    QB = QR // P
    PAIRS = E // 2
    GROUPS = S // SLOTS
    EXTRAS = 8
    assert 2 * S // SLOTS <= EXTRAS
    STEPS = PAIRS + 1
    ITERS = EXTRAS // 2 - 1
    SCALE = DH ** -0.5
    FC = F // P
    UNITS = 22
    GATHERED_FIRST = 10
    WO_ORDER = ((1, 0), (0, 1))
    TURN_BANKS = (5, 6, 7, 6)
    F_LOADED = 6 * 16
    assert (S, D, CW, QR, KR, F, E, NH, DH, VD) == (256, 1024, 512, 256, 128, 256, 16, 8, 96, 64)

    o_cb, o_cc, o_cx = 0, CW, 2 * CW
    o_lat = 3 * CW
    o_ga = o_lat + LAT
    o_gb = o_ga + D

    with ExitStack() as ctx:
        def sb(name, shape, dt=F32):
            return ctx.enter_context(nc.sbuf_tensor(name, shape, dt))

        def signal(name, per_layer=1):
            return Signal(ctx.enter_context(nc.semaphore(name)), per_layer)

        ring = sb("ring", [P, RING, CHUNK])
        w_lat = sb("w_lat", [P, QB * NH * DH + NH * (ND + VD)])
        uq_sb = w_lat[:, 0:QB * NH * DH].rearrange("p (k n) -> p k n", k=QB)
        ukv_sb = w_lat[:, QB * NH * DH:]
        sdown_sb = sb("sdown_sb", [P, FC, D])
        router_sb = sb("router_sb", [P, C, E])
        x_sb = sb("x_sb", [P, T, D])
        gate_rows = sb("gate_rows", [P, 2, D])
        ada_row = sb("ada_row", [P, BANK])
        ada_bias = sb("ada_bias", [P, 2, BANK])
        mod_cols = sb("mod_cols", [P, 2, 3, 2 * C])
        gain = sb("gain", [P, 2, 2, C])
        ident = sb("ident", [P, P])
        tri = sb("tri", [P, P], BF16)
        ones = sb("ones", [P, P], BF16)
        ones_f = sb("ones_f", [P, 32])
        slot_id = sb("slot_id", [P, SLOTS])
        count_up = sb("count_up", [P, E + 1])
        lower = sb("lower", [P, GRP, EPG])
        b_router_sb = sb("b_router_sb", [P, E])
        head_gain = sb("head_gain", [P, L, 2, DH])
        NPRM = 2 * C + QB + 1 + 3 * NB
        cols = sb("cols", [P, L * NPRM])
        c_act = sb("c_act", [P, C, 32])
        c_tmp = sb("c_tmp", [P, 2, C])
        cos_sin = sb("cos_sin", [P, T, 2, HALF])
        freq = sb("freq", [P, HALF])
        pos_i = sb("pos_i", [P, T], I32)
        pos_f = sb("pos_f", [P, T])
        sumsq = sb("sumsq", [P, T, 2])
        mean_sq = sb("mean_sq", [P, 2 * NH])
        rstd = sb("rstd", [P, 2 * NH])
        minus_half = sb("minus_half", [P, 2 * NH])
        top = sb("top", [P, 2, T])
        bias_m = sb("bias_m", [P, 2, T])
        denom = sb("denom", [P, 2, T])
        r_small = sb("r_small", [P, 12, T * E])
        pairwise = sb("pairwise", [P, 3, T * GRP, EPG, EPG])
        sel_b = sb("sel_b", [P, T, E], BF16)
        slot_of = sb("slot_of", [P, T, E])
        combine = sb("combine", [P, T, E])
        lengths = sb("lengths", [P, E])
        slot_x = sb("slot_x", [P, T, EXTRAS])
        combine_x = sb("combine_x", [P, T, EXTRAS])
        extra_expert = sb("extra_expert", [P, EXTRAS], I32)
        slot_weight = sb("slot_weight", [P, PAIRS + 1])
        n_extras = sb("n_extras", [P, 1], I32)
        passes_before = sb("passes_before", [P, 1], I32)
        passes_f = sb("passes_f", [P, 2 + ITERS])

        hT = sb("hT", [P, C, S])
        hT_end = nc.sbuf_base
        work = sb("work", [P, 17928])
        work_end = nc.sbuf_base

        def over(name, start, shape):
            nc.sbuf_base = start
            t = nc.alloc_sbuf_tensor(name, shape, F32R)
            nc.sbuf_base = work_end
            return t

        def work_address(a):
            return work_end - 4 * (17928 - a)

        def part(a, *shape):
            n = int(np.prod(shape))
            names = "abcd"[:len(shape)]
            v = work[:, a:a + n]
            if len(shape) == 1:
                return v
            return v.rearrange(f"p ({' '.join(names)}) -> p {' '.join(names)}",
                               **{k: s for k, s in zip(names, shape)})

        xn = part(0, T, D)
        merged = part(0, C, S)
        cc_tmp = part(2048, 2, BANK)
        u = part(3072, NB, S + 2)
        yc = part(4104, NB, S)
        qk = part(5128, T, 2, NH, DH)
        sq = part(8200, 2 * NH, DH)
        lat_n = part(8200, T, QR + KR)
        ada_acc = part(3072, 4 * BANK)
        v_sb = part(9736, T, NH, VD)
        qkT = part(10760, 2, 2, S)
        tanh_b = part(11784, C, S)
        oT = part(13832, NH // 2, S)
        probs = part(14856, 2, T, S)
        rot_tmp = part(14856, 4, 2 * NH, HALF)
        probsT = part(15880, 2, T, S)
        latT = part(15880, QB + 1, S)
        tanh_a = part(16904, 2, BANK)
        unused = part(16904, T, QR + KR)
        x_squared = part(10760, T, D)
        angle = part(11784, 3, T, 2, HALF)
        rows = part(13832, P)
        c_rows = part(14200, P)[0:C, :]
        ids_i = part(14000, SLOTS).bitcast(I32)
        count_i = part(14100, E + 1).bitcast(I32)
        onehot = over("onehot", work_address(2048), [P, T, E, SLOTS])
        weighted = part(4096, T, E, SLOTS)
        combT = over("combT", work_address(6144), [P, PAIRS, S])
        y = w_lat[:, 0:D]
        y_masked = w_lat[:, D:2 * D]
        y_high = over("y_high", work_address(4096), [P, D])
        y_low = over("y_low", work_address(4096 + D), [P, D])
        combT_weighted = w_lat[:, 0:PAIRS * S].rearrange("p (j s) -> p j s", j=PAIRS)
        hE = part(8192, C, E, SLOTS)
        e_tanh = part(16384, 2, F)
        e_act = part(16896, 2, F)
        s_tanh = part(16384, FC, S)
        s_act = w_lat[:, 2 * D:2 * D + FC * S].rearrange("p (c s) -> p c s", c=FC)
        aT = part(17408, FC, P)
        router_out = part(17664, S)
        x_masked = part(8192, T, D)
        x_low = over("x_low", work_address(0), [P, T, D])
        x_high = over("x_high", hT_end - 4 * C * S, [P, T, D])
        listing = part(2048, 2048)
        NF = E * (GROUPS - 1)
        LEAD = 32
        flags = listing[:, 0:NF]
        run_sums = [listing[:, 64 + k * 96:64 + k * 96 + LEAD + NF] for k in range(2)]
        match = listing[:, 256:256 + EXTRAS * NF].rearrange("p (k e g) -> p k e g", k=EXTRAS, e=E)
        is_expert = listing[:, 640:640 + EXTRAS * E].rearrange("p (k e) -> p k e", k=EXTRAS)
        scratch_e = listing[:, 768:768 + EXTRAS * E].rearrange("p (k e) -> p k e", k=EXTRAS)
        is_group = listing[:, 896:896 + EXTRAS * (GROUPS - 1)].rearrange("p (k g) -> p k g", k=EXTRAS)
        group_of = listing[:, 928:928 + EXTRAS]
        expert_f = listing[:, 936:936 + EXTRAS]
        onehot_x = over("onehot_x", work_address(2048 + 1024), [P, T, 2, SLOTS])
        combT_weighted_x = listing[:, 1792:1792 + S]
        weighted_x = listing[:, 1280:1536].rearrange("p (t e s) -> p t e s", t=T, e=2)

        psum = ctx.enter_context(nc.psum_tensor("psum", [P, 8, BANK], F32))

        slot_loaded = [signal(f"slot{i}_loaded") for i in range(RING)]
        x_loaded = signal("x_loaded")
        c_loaded = signal("c_loaded")
        c_psum = signal("c_column_in_psum")
        params_loaded = signal("params_loaded")
        late_loaded = signal("late_params_loaded", 16 * 4)
        bias_loaded = [signal(f"ada_bias{i}_loaded") for i in range(2)]
        latw_loaded = signal("latw_loaded")
        sdown_loaded = signal("sdown_loaded")
        out_stored = signal("out_stored")
        consts = signal("consts_ready")
        cols_psum = signal("param_columns_in_psum")
        cols_ready = signal("param_columns_ready")
        c_tanh = signal("c_tanh_ready")
        c_ready = signal("c_act_ready")
        angles_ready = signal("angles_ready")
        rope_ready = signal("cos_sin_ready")
        dve = signal("vector_step_done")
        pool = signal("pool_step_done")
        ada_products_done = signal("ada_products_done", 4)
        ada_scaled = signal("ada_rows_scaled", 8)
        ada_in_psum = signal("ada_in_psum", 2)
        ada_row_ready = signal("ada_row_ready")
        ada_turned = signal("ada_turned")
        mod_ready = signal("mod_columns_ready")
        gate_ready = signal("gate_row_ready", 2)
        gain_ready = signal("gain_ready", 2)
        x_squares = signal("x_squares_ready", 2)
        ms_ready = signal("mean_squares_ready", 5)
        rstd_ready = signal("rstd_ready", 5)
        xn_ready = signal("x_normed", 2 * T)
        xnT_ready = signal("x_turned", 8)
        hT_act = signal("hT_blocks_by_scalar", 4)
        hT_dve = signal("hT_blocks_by_vector", 4)
        lat_psum = signal("latents_in_psum", T)
        lat_squares = signal("latent_squares_ready", T)
        lat_ready = signal("latents_normed", T)
        latT_psum = signal("latents_turned", T)
        latT_ready = signal("latT_ready", T)
        up_psum = signal("up_projections_in_psum", 2 * T)
        qkv_copied = signal("qkv_copied", 2 * T)
        qk_squares = signal("qk_squares_ready", T)
        qk_ready = signal("qk_normed_rotated", T)
        unit_psum = signal("unit_in_psum", UNITS)
        cc_ready = signal("cc_copied", 2)
        u_ready = signal("u_ready", 2)
        conv_ready = signal("conv_gated", 2)
        ya_ready = signal("ya_copied", 4)
        ga_tanh = signal("gate_a_tanh", 4)
        ga_used = signal("gate_a_used", 4)
        gb_tanh = signal("gate_b_tanh", 4)
        qkT_psum = signal("qk_turned", NH)
        qkT_ready = signal("qkT_ready", NH)
        scores_psum = signal("scores_in_psum", NH)
        bias_ready = signal("score_bias_ready", NH)
        exp_done = signal("exp_done", NH)
        probs_ready = signal("probs_ready", NH)
        pT_psum = signal("probs_turned", NH)
        pT_ready = signal("probsT_ready", NH)
        pv_psum = signal("pv_in_psum", NH)
        oT_ready = signal("oT_pair_ready", NH // 2)
        yb_gated = signal("gated_yb_ready", 4)
        merged_ready = signal("merged_ready", 4)
        mix_psum = signal("mixer_out_in_psum", 2 * T)
        mix_added = signal("mixer_added", T)
        router_psum = signal("router_in_psum")
        router_copied = signal("router_copied")
        routerT_psum = signal("router_turned")
        router_exp = signal("router_exp_ready")
        chosen = signal("experts_chosen")
        rank_psum = signal("ranks_in_psum")
        ranks_read = signal("ranks_read")
        onehot_ready = signal("onehot_ready")
        masked_ready = signal("high_part_masked")
        low_ready = signal("low_part_ready")
        high_ready = signal("high_part_ready", 2)
        weighted_ready = signal("weighted_onehot_ready")
        s_gate_psum = signal("shared_gate_in_psum")
        s_tanh_ready = signal("shared_tanh_ready")
        s_up_psum = signal("shared_up_in_psum")
        s_act_ready = signal("shared_act_ready")
        s_down_psum = signal("shared_down_issued")
        gather_psum = signal("gathered_in_psum", 2 * C)
        hE_act = signal("gathered_by_scalar", C)
        hE_dve = signal("gathered_by_vector", C)
        combT_psum = signal("weighted_turned", 4)
        weights_read = signal("slot_weights_ready", 4)
        combT_ready = signal("combT_ready", 4)
        gu_psum = signal("gate_up_in_psum", 2 * STEPS)
        tanh_ready = signal("expert_tanh_ready", STEPS)
        act_ready = signal("expert_act_ready", STEPS)
        aT_psum = signal("expert_act_turned", STEPS)
        aT_ready = signal("aT_ready", STEPS)
        down_psum = signal("down_in_psum", 2 * STEPS)
        sdown_gated = signal("sdown_gated")
        y_read = signal("y_weighted", 2 * STEPS)
        y_masked_ready = signal("y_masked", 2 * STEPS)
        y_high_ready = signal("y_high_ready", 2 * STEPS)
        y_low_ready = signal("y_low_ready", 2 * STEPS)
        added_psum = signal("added_to_tokens", STEPS)
        moe_psum = signal("moe_out_in_psum")
        moe_added = signal("moe_added", T)
        extras_ready = signal("extras_listed")
        first_onehot = signal("first_extras_onehot_ready")
        first_weighted = signal("first_extras_weighted_ready")
        first_gathered = signal("first_extras_gathered", 2)
        first_tokens = signal("first_extras_tokens_ready", 2)
        first_turned = signal("first_extras_turned")
        first_weights = signal("first_extras_weights_ready")
        first_combT = signal("first_extras_combT_ready")
        x_loaded_w = signal("extra_weights_loaded")
        x_onehot = signal("extra_onehot_ready")
        x_weighted = signal("extra_weighted_ready")
        x_gathered = signal("extra_gathered")
        x_turned = signal("extra_onehot_turned")
        x_tokens_act = signal("extra_tokens_by_scalar")
        x_tokens_dve = signal("extra_tokens_by_vector")
        x_gu = signal("extra_gate_up")
        x_tanh = signal("extra_tanh_ready")
        x_act1 = signal("extra_act_begun")
        x_act = signal("extra_act_ready")
        x_aT_psum = signal("extra_act_turned")
        x_aT = signal("extra_aT_ready")
        x_down = signal("extra_down")
        x_y = signal("extra_y_weighted")
        x_weights = signal("extra_slot_weights_ready")
        x_combT = signal("extra_combT_ready")
        x_y_masked = signal("extra_y_masked")
        x_y_high = signal("extra_y_high_ready")
        x_y_low = signal("extra_y_low_ready")
        x_free = signal("extra_pass_done")
        x_slots_free = signal("extra_slots_free")

        chunks, number = [], {}

        def chunk(key, pieces, freed_by):
            number[key] = len(chunks)
            chunks.append((pieces, freed_by))

        def ada_chunks(s, parts=range(4)):
            w = w_ada[s // 3, :, (s % 3) * 4 * BANK:(s % 3 + 1) * 4 * BANK].rearrange("(c p) n -> p c n", p=P)
            for i in parts:
                chunk(("ada", s, i), [(2, 0, 0, w[:, 2 * i:2 * i + 2, :])],
                      ada_scaled(s // 3, 4 * (s % 3) - 3 + i) if s % 3 else ada_products_done(s // 3, i + 1))

        def in_chunk(l, key, a, n, freed_by):
            chunk((key, l), [(C, 0, 0, w_in[l, :, a:a + n].rearrange("(c p) n -> p c n", p=P))], freed_by)

        def expert_rows(w, l, i, k, a, n):
            if i < PAIRS:
                return w[l, 2 * i + k, a:a + n].rearrange("(c p) n -> p c n", p=P)
            return lambda experts: w[l, bass.ds(experts[k], 1), a:a + n].rearrange("e (c p) n -> p (e c) n", p=P)

        ada_chunks(0)
        for l in range(L):
            in_chunk(l, "lat", o_lat, LAT, lat_psum(l, T))
            in_chunk(l, "cc", o_cc, CW, unit_psum(l, 3))
            in_chunk(l, "cx", o_cx, CW, unit_psum(l, 4))
            in_chunk(l, "cb", o_cb, CW, unit_psum(l, 6))
            chunk(("conv", l), [(NB, 0, 0, w_conv_out[l].rearrange("(c p) n -> p c n", p=P))], unit_psum(l, 10))
            in_chunk(l, "ga0", o_ga, BANK, unit_psum(l, 12))
            ada_chunks(3 * l + 1, [0])
            in_chunk(l, "ga1", o_ga + BANK, BANK, unit_psum(l, 14))
            ada_chunks(3 * l + 1, [1, 2])
            in_chunk(l, "gb0", o_gb, BANK, unit_psum(l, 16))
            ada_chunks(3 * l + 1, [3])
            in_chunk(l, "gb1", o_gb + BANK, BANK, unit_psum(l, 18))
            ada_chunks(3 * l + 2, [0, 1])
            chunk(("attn", l), [(NB, 0, 0, w_attn_out[l].rearrange("(c p) n -> p c n", p=P))], unit_psum(l, UNITS))
            ada_chunks(3 * l + 2, [2, 3])
            for i in range(2):
                chunk((f"wo{i}", l), [(C, 0, 0, w_o[l, :, i * BANK:(i + 1) * BANK].rearrange("(c p) n -> p c n", p=P))],
                      mix_psum(l, 2 + 2 * i))
            if l + 1 < L:
                ada_chunks(3 * l + 3)
            chunk(("shared", l), [(C, 0, 0, w_s_gate[l].rearrange("(c p) n -> p c n", p=P)),
                                  (C, 0, F, w_s_up[l].rearrange("(c p) n -> p c n", p=P))], s_up_psum(l))
            for i in range(STEPS + 1):
                for part_no in range(2 if i < STEPS else 0):
                    chunk(("gu", l, i, part_no),
                          [(C, k * C // 2, at, expert_rows(w, l, i, k, part_no * D // 2, D // 2))
                           for k in range(2) for at, w in ((0, w_e_gate), (F, w_e_up))],
                          gu_psum(l, 2 * i + 1 + part_no))
                if i:
                    if i <= PAIRS:
                        pieces = [(2 * FC, 0, 0, w_e_down[l, 2 * i - 2:2 * i].rearrange("e (c p) n -> p (e c) n", p=P))]
                    else:
                        pieces = [(2 * FC, k * FC, 0, expert_rows(w_e_down, l, PAIRS, k, 0, F)) for k in range(2)]
                    chunk(("down", l, i - 1), pieces, down_psum(l, 2 * i))

        def slot(key, k):
            return ring[:, number[key] % RING, :].rearrange("p (k n) -> p k n", k=k)

        def loaded(key):
            n = number[key]
            return slot_loaded[n % RING].sem, 16 * len(pieces_before(n))

        def pieces_before(n):
            return [q for i in range(n % RING, n + 1, RING) for q in chunks[i][0]]

        PRM = {}
        at = 0
        for name, n in (("g_mix", C), ("g_ffn", C), ("g_q_a", QB), ("g_kv_a", 1), ("conv", 3 * NB)):
            for l in range(L):
                PRM[name, l] = at
                at += n
        NROWS = at

        def col(name, l, i, n=1):
            return cols[:, PRM[name, l] + i:PRM[name, l] + i + n]

        sc_of = lambda l, which: mod_cols[:, l % 2, 0, C:2 * C] if which == 0 else mod_cols[:, l % 2, 2, 0:C]
        sh_of = lambda l, which: mod_cols[:, l % 2, 0, 0:C] if which == 0 else mod_cols[:, l % 2, 1, C:2 * C]

        block = ctx.enter_context(nc.Block())

        @block.sync
        def _(sp):
            sp.wait_ge(c_loaded.sem, 16)

            def listed_expert(k):
                return sp.value_load(extra_expert[0:1, bass.ds(k, 1)], min_val=0, max_val=E - 1)

            def load_further_extras(l):
                listed = sp.value_load(n_extras[0:1, 0:1], min_val=0, max_val=EXTRAS)
                before = sp.value_load(passes_before[0:1, 0:1], min_val=0, max_val=L * ITERS)
                first = number["down", l, PAIRS] - 2
                slots = [ring[:, (first + k) % RING, :] for k in range(3)]
                with sp.If(listed > 2):
                    with sp.Fori(0, ITERS) as j:
                        with sp.If(listed > 2 * j + 2):
                            sp.wait_ge(*down_psum(l, 2 * STEPS))
                            for k in range(2):
                                e = listed_expert(2 * j + (k + 2))
                                dst = slots[k].rearrange("p (c n) -> p c n", c=C)
                                for at, w in ((0, w_e_gate), (F, w_e_up)):
                                    sp.dma_start(dst[:, :, at:at + F],
                                                 w[l, bass.ds(e, 1)].rearrange("e (c p) n -> p (e c) n", p=P)) \
                                        .then_inc(x_loaded_w.sem, 16)
                                dst = slots[2].rearrange("p (k n) -> p k n", k=2 * FC)
                                sp.dma_start(dst[:, k * FC:(k + 1) * FC, :],
                                             w_e_down[l, bass.ds(e, 1)].rearrange("e (c p) n -> p (e c) n", p=P)) \
                                    .then_inc(x_loaded_w.sem, 16)
                            sp.wait_ge(x_free.sem, j + before + 1)
                            sp.sem_inc(x_slots_free.sem, 1)

            experts = None
            for n, (pieces, _) in enumerate(chunks):
                for l in range(L):
                    if n == number["gu", l, PAIRS, 0]:
                        sp.wait_ge(*extras_ready(l))
                        experts = [listed_expert(k) for k in range(2)]
                    if n == number["down", l, PAIRS] + 2:
                        load_further_extras(l)
                if n >= RING:
                    sp.wait_ge(*chunks[n - RING][1])
                for rows, a, at, src in pieces:
                    if callable(src):
                        src = src(experts)
                    width = src.shape[2]
                    dst = ring[:, n % RING, :].rearrange("p (k n) -> p k n", k=rows)[:, a:a + src.shape[1], at:at + width]
                    sp.dma_start(dst, src).then_inc(slot_loaded[n % RING].sem, 16)
                if n == 0:
                    sp.dma_start(x_sb[:, :, :], x[0].rearrange("(t p) d -> p t d", p=P)).then_inc(x_loaded.sem, 16)
                if n == 1:
                    sp.wait_ge(params_loaded.sem, 16 * (5 + T))
                for l in range(L):
                    if n == number["cc", l]:
                        if l:
                            sp.wait_ge(*moe_psum(l - 1))
                        sp.dma_start(uq_sb, w_uq[l].rearrange("(c p) n -> p c n", p=P)).then_inc(latw_loaded.sem, 16)
                        sp.dma_start(ukv_sb, w_ukv[l]).then_inc(latw_loaded.sem, 16)
                    if n == number["shared", l]:
                        if l:
                            sp.wait_ge(*s_down_psum(l - 1))
                        sp.dma_start(sdown_sb[:, :, :], w_s_down[l].rearrange("(c p) n -> p c n", p=P)) \
                            .then_inc(sdown_loaded.sem, 16)
            load_further_extras(L - 1)
            for t in range(T):
                sp.wait_ge(*moe_added(L - 1, t + 1))
                sp.dma_start(out[0, t * P:(t + 1) * P, :], x_sb[:, t, :]).then_inc(out_stored.sem, 16)
            sp.wait_ge(out_stored.sem, 16 * T)

        @block.gpsimd
        def _(gp):
            step = [0]

            def link(ins):
                step[0] += 1
                ins.then_inc(pool.sem, 1)
                gp.wait_ge(pool.sem, step[0])

            link(gp.memset(ident[:, :], 0.0))
            gp.affine_select(out=ident[:, :], in_=ident[:, :], compare_op=ALU.not_equal, fill=1.0, base=0,
                             pattern=[[-1, P]], channel_multiplier=1).then_inc(consts.sem, 1)
            link(gp.memset(tri[:, :], 1.0))
            gp.affine_select(out=tri[:, :], in_=tri[:, :], compare_op=ALU.is_gt, fill=0.0, base=0,
                             pattern=[[1, P]], channel_multiplier=-1).then_inc(consts.sem, 1)
            gp.memset(ones[:, :], 1.0).then_inc(consts.sem, 1)
            gp.memset(ones_f[:, :], 1.0).then_inc(consts.sem, 1)
            gp.iota(ids_i, pattern=[[1, SLOTS]], base=-2 * S, channel_multiplier=0).then_inc(consts.sem, 1)
            gp.iota(count_i, pattern=[[1, E + 1]], base=0, channel_multiplier=0).then_inc(consts.sem, 1)
            gp.memset(minus_half[:, :], -0.5).then_inc(consts.sem, 1)
            gp.wait_ge(*consts(0, 7))

            def power(l, n, width):
                gp.wait_ge(*ms_ready(l, n))
                gp.tensor_tensor(rstd[:, 0:width], mean_sq[:, 0:width], minus_half[:, 0:width], ALU.pow) \
                    .then_inc(rstd_ready.sem, 1)
                gp.wait_ge(*rstd_ready(l, n))

            def gates(l, which):
                gp.wait_ge(*ada_row_ready(0, 3 * l + 2 + which))
                if l:
                    gp.wait_ge(*(mix_added if which == 0 else moe_added)(l - 1, T))
                first = 0 if which == 0 else 2
                for j in range(2):
                    q = 32 * (first + j)
                    ins = gp.partition_broadcast(gate_rows[:, which, j * BANK:(j + 1) * BANK], ada_row[q:q + 1, :], P)
                    if j == 0:
                        link(ins)
                ins.then_inc(gate_ready.sem, 1)
                gp.wait_ge(*gate_ready(l, which + 1))

            for l in range(L):
                power(l, 1, T)
                power(l, 2, 2 * T)
                power(l, 3, 2 * NH)
                power(l, 4, 2 * NH)
                gates(l, 0)
                gates(l, 1)
                power(l, 5, T)

        @block.scalar
        def _(act):
            def load_bias(s):
                if s >= 2:
                    act.wait_ge(*ada_row_ready(0, s - 1))
                for j in range(4):
                    a = ((s % 3) * 4 + j) * BANK
                    act.dma_start(ada_bias[32 * j:32 * j + 32, s % 2, :],
                                  b_ada[s // 3, a:a + BANK].partition_broadcast(32)) \
                        .then_inc(bias_loaded[s % 2].sem, 16)

            act.dma_start(c_rows, c[0].rearrange("(c p) -> c p", p=P)).then_inc(c_loaded.sem, 16)
            act.wait_ge(*c_psum(0))
            nc.scalar.activation(c_tmp[:, 0, :], psum[:, 5, 0:C], ACT.Tanh, scale=0.5) \
                .then_inc(c_tanh.sem, 1)
            load_bias(0)
            for name, src in (("g_mix", g_mix), ("g_ffn", g_ffn), ("g_q_a", g_q_a), ("g_kv_a", g_kv_a)):
                at = PRM[name, 0]
                n = L * src.shape[1] // P
                act.dma_start(rows[at:at + n, :], src.rearrange("l (c p) -> (l c) p", p=P)).then_inc(params_loaded.sem, 16)
            at = PRM["conv", 0]
            act.dma_start(rows[at:at + L * 3 * NB, :], conv_w.rearrange("l k (c p) -> (l k c) p", p=P)) \
                .then_inc(params_loaded.sem, 16)
            for t in range(T):
                act.dma_start(pos_i[:, t:t + 1], positions[0, t * P:(t + 1) * P].rearrange("(p o) -> p o", o=1)) \
                    .then_inc(params_loaded.sem, 16)

            def mod_columns(s, bank):
                act.wait_ge(*ada_turned(0, s + 1))
                src = psum[:, bank, :].rearrange("p (b j r) -> p j b r", b=4, r=32)[:, :, :, 0]
                nc.scalar.activation(mod_cols[:, (s // 3) % 2, s % 3, :].rearrange("p (j b) -> p j b", b=4), src,
                                     ACT.Identity).then_inc(mod_ready.sem, 1)
                if s + 2 < 3 * L:
                    load_bias(s + 2)

            def square_x(l, which):
                if not which and not l:
                    act.wait_ge(x_loaded.sem, 16)
                for t in range(T):
                    if which:
                        act.wait_ge(*mix_added(l, t + 1))
                    elif l:
                        act.wait_ge(*moe_added(l - 1, t + 1))
                    ins = nc.scalar.activation(x_squared[:, t, :], x_sb[:, t, :], ACT.Square, accum_out=sumsq[:, t, 0:1])
                ins.then_inc(x_squares.sem, 1)

            def modulate_half(l, which):
                act.wait_ge(*gain_ready(l, which + 1))
                for b in range(2):
                    act.wait_ge(*xnT_ready(l, 4 * which + b + 1))
                    for k in range(2):
                        q = 2 * b + k
                        ins = nc.scalar.activation(hT[:, q, :], psum[:, 3 + b, k * S:(k + 1) * S], ACT.Identity,
                                                   bias=sh_of(l, which)[:, q:q + 1],
                                                   scale=gain[:, l % 2, which, q:q + 1])
                    ins.then_inc(hT_act.sem, 1)

            load_bias(1)
            act.wait_ge(*angles_ready(0))
            nc.scalar.activation(cos_sin[:, :, :, :], angle[:, 0], ACT.Sin).then_inc(rope_ready.sem, 1)
            act.wait_ge(*rope_ready(0))
            square_x(0, 0)
            act.dma_start(head_gain[:, :, 0, :], g_qn.partition_broadcast(P)).then_inc(late_loaded.sem, 16)
            act.dma_start(head_gain[:, :, 1, :], g_kn.partition_broadcast(P)).then_inc(late_loaded.sem, 16)
            act.dma_start(b_router_sb[:, :], b_router.partition_broadcast(P)).then_inc(late_loaded.sem, 16)
            act.dma_start(router_sb[:, :, :], w_router.rearrange("(c p) e -> p c e", p=P)) \
                .then_inc(late_loaded.sem, 16)
            mod_columns(0, 7)

            for l in range(L):
                if l:
                    square_x(l, 0)
                modulate_half(l, 0)

                for t in range(T):
                    act.wait_ge(*lat_psum(l, t + 1))
                    nc.scalar.activation(unused[:, t, 0:QR], psum[:, 2 + t, 0:QR], ACT.Square,
                                         accum_out=sumsq[:, t, 0:1])
                    nc.scalar.activation(unused[:, t, QR:], psum[:, 2 + t, QR:QR + KR], ACT.Square,
                                         accum_out=sumsq[:, t, 1:2]).then_inc(lat_squares.sem, 1)

                def copy_cc(j):
                    act.wait_ge(*unit_psum(l, 2 * j + 1))
                    nc.scalar.activation(cc_tmp[:, j, :], psum[:, 0, :], ACT.Identity).then_inc(cc_ready.sem, 1)

                copy_cc(0)
                for t in range(T):
                    act.wait_ge(*latT_psum(l, t + 1))
                    for b in range(QB + 1):
                        g = col("g_q_a", l, b) if b < QB else col("g_kv_a", l, 0)
                        ins = nc.scalar.activation(latT[:, b, t * P:(t + 1) * P], psum[:, 4 + t, b * P:(b + 1) * P],
                                                   ACT.Identity, scale=g)
                    ins.then_inc(latT_ready.sem, 1)
                copy_cc(1)

                for n, (t, what, bank) in enumerate(((0, "q", 2), (0, "kv", 4), (1, "q", 6), (1, "kv", 2))):
                    act.wait_ge(*up_psum(l, n + 1))
                    if what == "q":
                        flat = qk[:, t, 0].rearrange("p h d -> p (h d)")
                        nc.scalar.activation(flat[:, 0:BANK], psum[:, bank, :], ACT.Identity)
                        nc.scalar.activation(flat[:, BANK:], psum[:, bank + 1, 0:NH * DH - BANK], ACT.Identity) \
                            .then_inc(qkv_copied.sem, 1)
                    else:
                        src = psum[:, bank:bank + 2, :].rearrange("p b (h d) -> p (b h) d", d=ND + VD)
                        nc.scalar.activation(qk[:, t, 1, :, 0:ND], src[:, :, 0:ND], ACT.Identity)
                        nc.scalar.activation(v_sb[:, t, :, :], src[:, :, ND:], ACT.Identity) \
                            .then_inc(qkv_copied.sem, 1)

                def square_qk(t):
                    act.wait_ge(*qkv_copied(l, 2 * t + 2))
                    act.wait_ge(*lat_ready(l, t + 1))
                    if t:
                        act.wait_ge(*ms_ready(l, 3))
                    nc.scalar.activation(sq[:, :, :], qk[:, t].rearrange("p a h d -> p (a h) d"), ACT.Square) \
                        .then_inc(qk_squares.sem, 1)

                def copy_ya(j):
                    act.wait_ge(*unit_psum(l, 7 + j))
                    nc.scalar.activation(merged[:, 2 * j:2 * j + 2, :].rearrange("p c s -> p (c s)"),
                                         psum[:, j % 2, :], ACT.Identity, scale=0.5).then_inc(ya_ready.sem, 1)

                def tanh_unit(n):
                    act.wait_ge(*unit_psum(l, n + 1))
                    if n < 14:
                        j = n - 10
                        if j >= 2:
                            act.wait_ge(*ga_used(l, j - 1))
                        nc.scalar.activation(tanh_a[:, j % 2, :], psum[:, n % 2, :], ACT.Tanh, scale=0.5) \
                            .then_inc(ga_tanh.sem, 1)
                    else:
                        j = n - 14
                        nc.scalar.activation(tanh_b[:, 2 * j:2 * j + 2, :].rearrange("p c s -> p (c s)"),
                                             psum[:, n % 2, :], ACT.Tanh, scale=0.5).then_inc(gb_tanh.sem, 1)

                square_qk(0)
                copy_ya(0)
                copy_ya(1)
                square_qk(1)
                copy_ya(2)
                copy_ya(3)
                tanh_unit(10)

                def copy_qkT(h):
                    act.wait_ge(*qkT_psum(l, h + 1))
                    if h >= 2:
                        act.wait_ge(*scores_psum(l, h - 1))
                    nc.scalar.activation(qkT[0:DH, h % 2].rearrange("p a s -> p (a s)"), psum[0:DH, 2, :],
                                         ACT.Identity).then_inc(qkT_ready.sem, 1)

                copy_qkT(0)
                for h in range(NH):
                    if h + 1 < NH:
                        copy_qkT(h + 1)
                    act.wait_ge(*bias_ready(l, h + 1))
                    if h >= 2:
                        act.wait_ge(*pT_psum(l, h - 1))
                    for t in range(T):
                        ins = nc.scalar.activation(probs[:, h % 2, t, :], psum[:, 4 + h % 2, t * S:(t + 1) * S], ACT.Exp,
                                                   bias=bias_m[:, h % 2, t:t + 1], scale=SCALE,
                                                   accum_out=denom[:, h % 2, t:t + 1])
                    ins.then_inc(exp_done.sem, 1)
                    if h != 6:
                        tanh_unit(min(11 + h, 17))
                    if h == 5:
                        mod_columns(3 * l + 1, 3)
                    act.wait_ge(*pT_psum(l, h + 1))
                    if h >= 2:
                        act.wait_ge(*pv_psum(l, h - 1))
                    nc.scalar.activation(probsT[:, h % 2].rearrange("p a s -> p (a s)"), psum[:, 6, :],
                                         ACT.Identity).then_inc(pT_ready.sem, 1)
                mod_columns(3 * l + 2, 4)

                square_x(l, 1)
                modulate_half(l, 1)
                if l + 1 < L:
                    mod_columns(3 * l + 3, 7)
                act.wait_ge(*router_psum(l))
                nc.scalar.activation(router_out[0:E, :], psum[0:E, 0, 0:S], ACT.Identity).then_inc(router_copied.sem, 1)
                act.wait_ge(*routerT_psum(l))
                nc.scalar.activation(r_small[:, 0, :], psum[:, 6, 0:T * E], ACT.Exp, scale=-1.0) \
                    .then_inc(router_exp.sem, 1)
                act.wait_ge(*s_gate_psum(l))
                nc.scalar.activation(s_tanh.rearrange("p c s -> p (c s)"), psum[:, 4, :], ACT.Tanh, scale=0.5) \
                    .then_inc(s_tanh_ready.sem, 1)
                act.wait_ge(*s_up_psum(l))
                act.wait_ge(*masked_ready(l))
                for half in range(2):
                    at = slice(half * D // 2, (half + 1) * D // 2)
                    nc.scalar.activation(x_high[:, :, at], x_masked[:, :, at], ACT.Identity).then_inc(high_ready.sem, 1)
                def modulate_gathered(n, bank):
                    half, q = divmod(n, C)
                    act.wait_ge(*gather_psum(l, n + 1))
                    nc.scalar.activation(hE[:, q, half * 8:half * 8 + 8, :].rearrange("p e s -> p (e s)"),
                                         psum[:, bank, :], ACT.Identity, bias=sh_of(l, 1)[:, q:q + 1],
                                         scale=gain[:, l % 2, 1, q:q + 1]).then_inc(hE_act.sem, 1)

                for n in range(0, GATHERED_FIRST, 2):
                    modulate_gathered(n, 4 + (n + 2) % 4)

                def read_turned():
                    for b, bank in enumerate(TURN_BANKS):
                        act.wait_ge(*combT_psum(l, b + 1))
                        for k in range(2):
                            ins = nc.scalar.activation(combT_weighted[:, 2 * b + k, :],
                                                       psum[:, bank, k * S:(k + 1) * S], ACT.Identity,
                                                       accum_out=slot_weight[:, 2 * b + k:2 * b + k + 1])
                        ins.then_inc(weights_read.sem, 1)
                    act.wait_ge(*weights_read(l, 4))

                def copy_high(i):
                    for half in range(2):
                        act.wait_ge(*y_masked_ready(l, 2 * i + half + 1))
                        if i:
                            act.wait_ge(*added_psum(l, i))
                        at = slice(half * BANK, (half + 1) * BANK)
                        nc.scalar.activation(y_high[:, at], y_masked[:, at], ACT.Identity).then_inc(y_high_ready.sem, 1)

                for i in range(STEPS + 1):
                    if i < STEPS:
                        act.wait_ge(*gu_psum(l, 2 * i + 2))
                        nc.scalar.activation(e_tanh[:, i % 2, :], psum[:, 4 + i % 2, 0:F], ACT.Tanh, scale=0.5) \
                            .then_inc(tanh_ready.sem, 1)
                    if i == 0:
                        read_turned()
                    elif i < 4:
                        modulate_gathered(GATHERED_FIRST + 2 * i - 2, 6)
                    if i >= 1:
                        act.wait_ge(*aT_psum(l, i))
                        nc.scalar.activation(aT.rearrange("p c s -> p (c s)"), psum[:, 6, 0:FC * P], ACT.Identity) \
                            .then_inc(aT_ready.sem, 1)
                        if i in (5, 6):
                            act.wait_ge(*first_gathered(l, i - 4))
                            for m in range(C // 2):
                                q = (i - 5) * C // 2 + m
                                ins = nc.scalar.activation(hE[:, q, 0:2, :].rearrange("p e s -> p (e s)"),
                                                           psum[:, 7, m * P:(m + 1) * P], ACT.Identity,
                                                           bias=sh_of(l, 1)[:, q:q + 1],
                                                           scale=gain[:, l % 2, 1, q:q + 1])
                            ins.then_inc(first_tokens.sem, 1)
                        elif i == 7:
                            act.wait_ge(*first_turned(l))
                            nc.scalar.activation(combT_weighted_x, psum[:, 7, 0:S], ACT.Identity,
                                                 accum_out=slot_weight[:, PAIRS:]).then_inc(first_weights.sem, 1)
                            act.wait_ge(*first_weights(l))
                        copy_high(i - 1)

                act.wait_ge(*extras_ready(l))
                listed = act.value_load(n_extras[0:1, 0:1], min_val=0, max_val=EXTRAS)
                before = act.value_load(passes_before[0:1, 0:1], min_val=0, max_val=L * ITERS)
                with act.If(listed > 2):
                    with act.Fori(0, ITERS) as j:
                        with act.If(listed > 2 * j + 2):
                            act.wait_ge(x_gathered.sem, j + before + 1)
                            for q in range(0, C, 2):
                                ins = nc.scalar.activation(hE[:, q, 0:2, :].rearrange("p e s -> p (e s)"),
                                                           psum[:, 4 + q % 2, (q // 2) * P:(q // 2 + 1) * P],
                                                           ACT.Identity, bias=sh_of(l, 1)[:, q:q + 1],
                                                           scale=gain[:, l % 2, 1, q:q + 1])
                            ins.then_inc(x_tokens_act.sem, 1)
                            act.wait_ge(x_turned.sem, j + before + 1)
                            nc.scalar.activation(combT_weighted_x, psum[:, 6, 0:S], ACT.Identity,
                                                 accum_out=slot_weight[:, PAIRS:]).then_inc(x_weights.sem, 1)
                            act.wait_ge(x_gu.sem, j + before + 1)
                            nc.scalar.activation(e_tanh[:, 0, :], psum[:, 7, 0:F], ACT.Tanh, scale=0.5) \
                                .then_inc(x_tanh.sem, 1)
                            act.wait_ge(x_aT_psum.sem, j + before + 1)
                            nc.scalar.activation(aT.rearrange("p c s -> p (c s)"), psum[:, 6, 0:FC * P],
                                                 ACT.Identity).then_inc(x_aT.sem, 1)
                            act.wait_ge(x_y_masked.sem, j + before + 1)
                            nc.scalar.activation(y_high[:, :], y_masked, ACT.Identity).then_inc(x_y_high.sem, 1)

        @block.vector
        def _(ve):
            step = [0]

            def link(ins):
                step[0] += 1
                ins.then_inc(dve.sem, 1)
                ve.wait_ge(dve.sem, step[0])

            for i in range(HALF):
                nc.vector.memset(freq[:, i:i + 1], float(np.float32(ROPE_THETA ** (-i / HALF))))
            nc.vector.memset(passes_f[:, :], 0.0)
            link(nc.vector.memset(lower[:, :, :], 0.0))
            for i in range(1, GRP):
                ins = nc.vector.memset(lower[:, i, 0:i], 1.0)
            link(ins)
            ve.wait_ge(*consts(0, 7))
            nc.vector.tensor_copy(slot_id[:, :], ids_i)
            link(nc.vector.tensor_copy(count_up[:, :], count_i))

            ve.wait_ge(*c_tanh(0))
            link(nc.vector.scalar_tensor_tensor(out=c_tmp[:, 1, :], in0=c_tmp[:, 0, :], scalar=1.0,
                                                in1=psum[:, 5, 0:C], op0=ALU.add, op1=ALU.mult))
            nc.vector.tensor_scalar(c_act[:, :, :], c_tmp[:, 1, :].unsqueeze(2).broadcast_to([P, C, 32]), 0.5, None,
                                    ALU.mult).then_inc(c_ready.sem, 1)

            ve.wait_ge(params_loaded.sem, 16 * (5 + T))
            link(nc.vector.tensor_copy(pos_f[:, :], pos_i[:, :]))
            two_pi = 2 * np.pi
            part1 = 6.28125
            part2 = float(round((two_pi - part1) * 2 ** 20)) / 2 ** 20
            part3 = float(np.float32(two_pi - part1 - part2))
            turn = 1.5 * 2.0 ** 23
            for t in range(T):
                for k in range(2):
                    ins = nc.vector.tensor_scalar(angle[:, 0, t, k, :], freq[:, :], pos_f[:, t:t + 1], None, ALU.mult)
            link(ins)
            link(nc.vector.tensor_scalar(angle[:, 1, :, 0, :], angle[:, 0, :, 0, :], 1 / two_pi, 0.25, ALU.mult, ALU.add))
            link(nc.vector.tensor_scalar(angle[:, 1, :, 1, :], angle[:, 0, :, 1, :], 1 / two_pi, None, ALU.mult))
            link(nc.vector.tensor_scalar(angle[:, 2], angle[:, 1], turn, None, ALU.add))
            link(nc.vector.tensor_scalar(angle[:, 1], angle[:, 2], -turn, None, ALU.add))
            for q in (part1, part2, part3):
                link(nc.vector.scalar_tensor_tensor(out=angle[:, 0], in0=angle[:, 1], scalar=-q, in1=angle[:, 0],
                                                    op0=ALU.mult, op1=ALU.add))
            link(nc.vector.tensor_scalar(angle[:, 0, :, 0, :], angle[:, 0, :, 0, :], float(np.pi / 2), None, ALU.add))
            limit = float(np.nextafter(np.float32(np.pi), np.float32(0)))
            nc.vector.tensor_scalar(angle[:, 0], angle[:, 0], limit, -limit, ALU.min, ALU.max) \
                .then_inc(angles_ready.sem, 1)

            def mean_squares(l, n, outs):
                for k, (dst, src, width) in enumerate(outs):
                    ins = nc.vector.tensor_scalar(dst, src, 1.0 / width, EPS, ALU.mult, ALU.add)
                ins.then_inc(ms_ready.sem, 1)
                ve.wait_ge(*rstd_ready(l, n))

            def norm_x(l, which):
                ve.wait_ge(*x_squares(l, which + 1))
                mean_squares(l, 5 if which else 1, [(mean_sq[:, 0:T], sumsq[:, :, 0], D)])
                for t in range(T):
                    nc.vector.tensor_scalar(xn[:, t, :], x_sb[:, t, :], rstd[:, t:t + 1], None, ALU.mult) \
                        .then_inc(xn_ready.sem, 1)

            def add_bias(s, bank):
                ve.wait_ge(*(ada_in_psum(s // 3, s % 3) if s % 3 else ada_products_done(s // 3, 4)))
                ve.wait_ge(bias_loaded[s % 2].sem, 64 * (s // 2 + 1))
                if s:
                    ve.wait_ge(*ada_turned(0, s))
                    if s % 3 == 0:
                        ve.wait_ge(*gate_ready(s // 3 - 1, 2))
                    elif s % 3 == 2:
                        ve.wait_ge(*gate_ready(s // 3, 1))
                nc.vector.tensor_tensor(ada_row[:, :], psum[:, bank, :], ada_bias[:, s % 2, :], ALU.add) \
                    .then_inc(ada_row_ready.sem, 1)

            def gains(s):
                l, k = divmod(s, 3)
                ve.wait_ge(*mod_ready(0, s + 1))
                which = 0 if k == 0 else 1
                nc.vector.scalar_tensor_tensor(out=gain[:, l % 2, which, :], in0=sc_of(l, which), scalar=1.0,
                                               in1=col("g_ffn" if which else "g_mix", l, 0, C),
                                               op0=ALU.add, op1=ALU.mult).then_inc(gain_ready.sem, 1)
                ve.wait_ge(*gain_ready(l, which + 1))

            def modulate_half(l, which):
                for b in range(2, 4):
                    ve.wait_ge(*xnT_ready(l, 4 * which + b + 1))
                    for k in range(2):
                        q = 2 * b + k
                        ins = nc.vector.tensor_scalar(hT[:, q, :], psum[:, 3 + b, k * S:(k + 1) * S],
                                                      gain[:, l % 2, which, q:q + 1], sh_of(l, which)[:, q:q + 1],
                                                      ALU.mult, ALU.add)
                    ins.then_inc(hT_dve.sem, 1)

            norm_x(0, 0)
            ve.wait_ge(*cols_psum(0))
            nc.vector.tensor_copy(cols[:, 0:NROWS], psum[:, 6, 0:NROWS]).then_inc(cols_ready.sem, 1)
            ve.wait_ge(*cols_ready(0))
            add_bias(0, 7)
            gains(0)

            for l in range(L):
                if l:
                    norm_x(l, 0)
                modulate_half(l, 0)

                ve.wait_ge(*lat_squares(l, T))
                mean_squares(l, 2, [(mean_sq[:, 0:T], sumsq[:, :, 0], QR), (mean_sq[:, T:2 * T], sumsq[:, :, 1], KR)])
                for t in range(T):
                    nc.vector.tensor_scalar(lat_n[:, t, 0:QR], psum[:, 2 + t, 0:QR], rstd[:, t:t + 1], None, ALU.mult)
                    nc.vector.tensor_scalar(lat_n[:, t, QR:], psum[:, 2 + t, QR:QR + KR], rstd[:, T + t:T + t + 1],
                                            None, ALU.mult)
                    nc.vector.tensor_copy(qk[:, t, 1, :, ND:],
                                          psum[:, 2 + t, QR + KR:LAT].unsqueeze(1).broadcast_to([P, NH, RD])) \
                        .then_inc(lat_ready.sem, 1)

                nc.vector.memset(u[:, :, 0:1], 0.0)
                nc.vector.memset(u[:, :, S + 1:S + 2], 0.0)
                for j in range(2):
                    ve.wait_ge(*cc_ready(l, j + 1))
                    ve.wait_ge(*unit_psum(l, 2 * j + 2))
                    nc.vector.tensor_tensor(u[:, 2 * j:2 * j + 2, 1:S + 1],
                                            psum[:, 1, :].rearrange("p (c s) -> p c s", c=2),
                                            cc_tmp[:, j, :].rearrange("p (c s) -> p c s", c=2), ALU.mult) \
                        .then_inc(u_ready.sem, 1)
                ve.wait_ge(*u_ready(l, 2))
                for k in range(3):
                    for m in range(NB):
                        w = col("conv", l, k * NB + m)
                        if k == 0:
                            ins = nc.vector.tensor_scalar(yc[:, m, :], u[:, m, 0:S], w, None, ALU.mult)
                        else:
                            ins = nc.vector.scalar_tensor_tensor(out=yc[:, m, :], in0=u[:, m, k:k + S], scalar=w,
                                                                 in1=yc[:, m, :], op0=ALU.mult, op1=ALU.add)
                    link(ins)
                for j in range(2):
                    ve.wait_ge(*unit_psum(l, 5 + j))
                    nc.vector.tensor_tensor(yc[:, 2 * j:2 * j + 2, :], psum[:, j, :].rearrange("p (c s) -> p c s", c=2),
                                            yc[:, 2 * j:2 * j + 2, :], ALU.mult).then_inc(conv_ready.sem, 1)

                for t in range(T):
                    ve.wait_ge(*qk_squares(l, t + 1))
                    link(nc.vector.tensor_reduce(rstd[:, :], sq[:, :, :], AX.X, ALU.add))
                    mean_squares(l, 3 + t, [(mean_sq[:, :], rstd[:, :], DH)])
                    flat = qk[:, t].rearrange("p a h d -> p (a h) d")
                    link(nc.vector.tensor_tensor(flat, flat, rstd[:, :].unsqueeze(2).broadcast_to([P, 2 * NH, DH]),
                                                 ALU.mult))
                    if l == 0 and t == 0:
                        ve.wait_ge(*late_loaded(0, 16 * 4))
                    for a in range(2):
                        ins = nc.vector.tensor_tensor(qk[:, t, a], qk[:, t, a],
                                                      head_gain[:, l, a, :].unsqueeze(1).broadcast_to([P, NH, DH]),
                                                      ALU.mult)
                    link(ins)
                    if l == 0 and t == 0:
                        ve.wait_ge(*rope_ready(0))
                    x1, x2 = flat[:, :, ND:ND + HALF], flat[:, :, ND + HALF:]
                    cos, sin = (cos_sin[:, t, k, :].unsqueeze(1).broadcast_to([P, 2 * NH, HALF]) for k in range(2))
                    tmp = [rot_tmp[:, k] for k in range(4)]
                    for dst, a, b in ((tmp[0], x1, cos), (tmp[1], x2, sin), (tmp[2], x2, cos), (tmp[3], x1, sin)):
                        ins = nc.vector.tensor_tensor(dst, a, b, ALU.mult)
                    link(ins)
                    nc.vector.tensor_tensor(x1, tmp[0], tmp[1], ALU.subtract)
                    nc.vector.tensor_tensor(x2, tmp[2], tmp[3], ALU.add).then_inc(qk_ready.sem, 1)

                def gate_a(j):
                    ve.wait_ge(*ga_tanh(l, j + 1))
                    ve.wait_ge(*ya_ready(l, j + 1))
                    m = merged[:, 2 * j:2 * j + 2, :].rearrange("p c s -> p (c s)")
                    nc.vector.scalar_tensor_tensor(out=m, in0=tanh_a[:, j % 2, :], scalar=1.0, in1=m,
                                                   op0=ALU.add, op1=ALU.mult).then_inc(ga_used.sem, 1)

                def copy_oT(j):
                    ve.wait_ge(*pv_psum(l, 2 * j + 2))
                    nc.vector.tensor_copy(oT[:, j, :], psum[:, 7, 0:S]).then_inc(oT_ready.sem, 1)

                def scale_rows(s, i, parts=range(2)):
                    ve.wait_ge(*loaded(("ada", s, i)))
                    w = slot(("ada", s, i), 2)
                    for k in parts:
                        q = 2 * i + k
                        if q == 0:
                            ins = nc.vector.tensor_scalar(ada_acc, w[:, 0, :], c_act[:, 0, 0:1], None, ALU.mult)
                        else:
                            ins = nc.vector.scalar_tensor_tensor(out=ada_acc, in0=w[:, k, :], scalar=c_act[:, q, 0:1],
                                                                 in1=ada_acc, op0=ALU.mult, op1=ALU.add)
                        if k == 0:
                            link(ins)
                        else:
                            ins.then_inc(ada_scaled.sem, 1)
                            ve.wait_ge(*ada_scaled(s // 3, 4 * (s % 3) - 3 + i))

                gate_a(0)
                for h in range(NH):
                    ve.wait_ge(*scores_psum(l, h + 1))
                    link(nc.vector.tensor_reduce(top[:, h % 2, :], psum[:, 4 + h % 2, :].rearrange("p (t s) -> p t s", t=T),
                                                 AX.X, ALU.max))
                    nc.vector.tensor_scalar(bias_m[:, h % 2, :], top[:, h % 2, :], -SCALE, None, ALU.mult) \
                        .then_inc(bias_ready.sem, 1)
                    ve.wait_ge(*exp_done(l, h + 1))
                    link(nc.vector.reciprocal(denom[:, h % 2, :], denom[:, h % 2, :]))
                    for t in range(T):
                        ins = nc.vector.tensor_scalar(probs[:, h % 2, t, :], probs[:, h % 2, t, :],
                                                      denom[:, h % 2, t:t + 1], None, ALU.mult)
                    ins.then_inc(probs_ready.sem, 1)
                    if h < 3:
                        gate_a(1 + h)
                    if h < 4:
                        if h == 0:
                            ve.wait_ge(*unit_psum(l, 10))
                        scale_rows(3 * l + 1, h)
                    elif h < 6:
                        if h == 4:
                            add_bias(3 * l + 1, 3)
                        scale_rows(3 * l + 2, h - 4)
                    if h >= 2 and h % 2 == 0:
                        copy_oT(h // 2 - 1)
                copy_oT(NH // 2 - 1)

                for j in range(4):
                    ve.wait_ge(*unit_psum(l, 19 + j))
                    ve.wait_ge(*gb_tanh(l, j + 1))
                    nc.vector.scalar_tensor_tensor(out=cc_tmp[:, j % 2, :],
                                                   in0=tanh_b[:, 2 * j:2 * j + 2, :].rearrange("p c s -> p (c s)"),
                                                   scalar=1.0, in1=psum[:, j % 2, :], op0=ALU.add, op1=ALU.mult) \
                        .then_inc(yb_gated.sem, 1)
                    ve.wait_ge(*yb_gated(l, j + 1))
                    m = merged[:, 2 * j:2 * j + 2, :].rearrange("p c s -> p (c s)")
                    nc.vector.scalar_tensor_tensor(out=m, in0=cc_tmp[:, j % 2, :], scalar=0.5, in1=m,
                                                   op0=ALU.mult, op1=ALU.add).then_inc(merged_ready.sem, 1)
                    if j < 2:
                        scale_rows(3 * l + 2, 2, [j])
                scale_rows(3 * l + 2, 3)

                def add_gated(half):
                    ve.wait_ge(*gate_ready(l, 1))
                    for n, t in enumerate(WO_ORDER[half]):
                        ve.wait_ge(*mix_psum(l, half * T + n + 1))
                        tmp = cc_tmp[:, t % 2, :]
                        xs = x_sb[:, t, half * BANK:(half + 1) * BANK]
                        link(nc.vector.tensor_tensor(tmp, psum[:, 2 * t + half, :],
                                                     gate_rows[:, 0, half * BANK:(half + 1) * BANK], ALU.mult))
                        ins = nc.vector.tensor_tensor(xs, xs, tmp, ALU.add)
                        if half:
                            ins.then_inc(mix_added.sem, 1)
                    if not half:
                        link(ins)

                add_gated(0)
                add_bias(3 * l + 2, 4)
                add_gated(1)

                norm_x(l, 1)
                gains(3 * l + 2)
                if l + 1 < L:
                    add_bias(3 * l + 3, 7)
                modulate_half(l, 1)

                if l + 1 < L:
                    gains(3 * l + 3)
                nc.vector.tensor_scalar(x_masked.bitcast(I32), xn.bitcast(I32), HIGH_BITS, None, ALU.bitwise_and) \
                    .then_inc(masked_ready.sem, 1)
                ve.wait_ge(*masked_ready(l))
                nc.vector.tensor_tensor(x_low[:, :, :], xn, x_masked, ALU.subtract).then_inc(low_ready.sem, 1)
                ve.wait_ge(*gate_ready(l, 2))
                ve.wait_ge(sdown_loaded.sem, 16 * (l + 1))
                nc.vector.tensor_tensor(sdown_sb[:, :, :], sdown_sb[:, :, :],
                                        gate_rows[:, 1, :].unsqueeze(1).broadcast_to([P, FC, D]), ALU.mult) \
                    .then_inc(sdown_gated.sem, 1)
                ve.wait_ge(*router_exp(l))
                R = lambda k: r_small[:, k, :]
                link(nc.vector.tensor_scalar(R(1), R(0), 1.0, None, ALU.add))
                link(nc.vector.reciprocal(R(2), R(1)))
                link(nc.vector.tensor_tensor(R(3).rearrange("p (t e) -> p t e", t=T),
                                             R(2).rearrange("p (t e) -> p t e", t=T),
                                             b_router_sb[:, :].unsqueeze(1).broadcast_to([P, T, E]), ALU.add))

                def first_ranks(values, groups, n, rank):
                    full = [P, groups, n, n]
                    v = values.rearrange("p (g i) -> p g i", i=n)
                    vi, vj = v.unsqueeze(3).broadcast_to(full), v.unsqueeze(2).broadcast_to(full)
                    low = lower[:, :, :].unsqueeze(1).broadcast_to(full)
                    a, b, d = (pairwise[:, k, 0:groups] for k in range(3))
                    nc.vector.tensor_tensor(a, vj, vi, ALU.is_gt)
                    link(nc.vector.tensor_tensor(b, vj, vi, ALU.is_equal))
                    link(nc.vector.tensor_tensor(d, b, low, ALU.mult))
                    link(nc.vector.tensor_tensor(b, a, d, ALU.add))
                    link(nc.vector.tensor_reduce(rank.rearrange("p (g i) -> p g i", i=n), b, AX.X, ALU.add))

                first_ranks(R(3), T * GRP, EPG, R(4))
                link(nc.vector.tensor_scalar(R(5), R(4), 2.0, None, ALU.is_lt))
                link(nc.vector.tensor_tensor(R(6), R(5), R(3), ALU.mult))
                sums = R(7)[:, 0:T * GRP]
                link(nc.vector.tensor_reduce(sums, R(6).rearrange("p (g i) -> p g i", i=EPG), AX.X, ALU.add))
                g_rank, g_sel = R(8)[:, 0:T * GRP], R(9)[:, 0:T * GRP]
                first_ranks(sums, T, GRP, g_rank)
                link(nc.vector.tensor_scalar(g_sel, g_rank, 1.0, None, ALU.is_lt))
                sel = R(10)
                link(nc.vector.tensor_tensor(sel.rearrange("p (g i) -> p g i", i=EPG),
                                             R(5).rearrange("p (g i) -> p g i", i=EPG),
                                             g_sel.unsqueeze(2).broadcast_to([P, T * GRP, EPG]), ALU.mult))
                nc.vector.tensor_copy(sel_b[:, :, :].rearrange("p t e -> p (t e)"), sel).then_inc(chosen.sem, 1)
                link(nc.vector.tensor_tensor(R(6), sel, R(2), ALU.mult))
                link(nc.vector.tensor_reduce(R(7)[:, 0:T], R(6).rearrange("p (t e) -> p t e", t=T), AX.X, ALU.add))
                link(nc.vector.reciprocal(R(7)[:, 0:T], R(7)[:, 0:T]))
                link(nc.vector.tensor_tensor(combine[:, :, :], R(6).rearrange("p (t e) -> p t e", t=T),
                                             R(7)[:, 0:T].unsqueeze(2).broadcast_to([P, T, E]), ALU.mult))

                ve.wait_ge(*rank_psum(l))
                link(nc.vector.scalar_tensor_tensor(out=slot_of[:, :, :], in0=sel.rearrange("p (t e) -> p t e", t=T),
                                                    scalar=float(-2 * S),
                                                    in1=psum[:, 7, 0:T * E].rearrange("p (t e) -> p t e", t=T),
                                                    op0=ALU.mult, op1=ALU.add))
                nc.vector.tensor_copy(lengths[:, :], psum[:, 7, T * E:(T + 1) * E]).then_inc(ranks_read.sem, 1)
                for t in range(T):
                    ins = nc.vector.tensor_tensor(onehot[:, t], slot_id[:, :].unsqueeze(1).broadcast_to([P, E, SLOTS]),
                                                  slot_of[:, t, :].unsqueeze(2).broadcast_to([P, E, SLOTS]),
                                                  ALU.is_equal)
                ins.then_inc(onehot_ready.sem, 1)
                ve.wait_ge(*s_tanh_ready(l))
                ve.wait_ge(*s_up_psum(l))
                flat_act = s_act.rearrange("p c s -> p (c s)")
                link(nc.vector.scalar_tensor_tensor(out=flat_act, in0=s_tanh.rearrange("p c s -> p (c s)"), scalar=1.0,
                                                    in1=psum[:, 4, :], op0=ALU.add, op1=ALU.mult))
                nc.vector.scalar_tensor_tensor(out=flat_act, in0=flat_act, scalar=0.5, in1=psum[:, 5, :],
                                               op0=ALU.mult, op1=ALU.mult).then_inc(s_act_ready.sem, 1)
                ve.wait_ge(*onehot_ready(l))
                for t in range(T):
                    ins = nc.vector.tensor_tensor(weighted[:, t], onehot[:, t].bitcast(F32),
                                                  combine[:, t, :].unsqueeze(2).broadcast_to([P, E, SLOTS]), ALU.mult)
                ins.then_inc(weighted_ready.sem, 1)

                def modulate_gathered(n, bank):
                    half, q = divmod(n, C)
                    ve.wait_ge(*gather_psum(l, n + 1))
                    nc.vector.tensor_scalar(hE[:, q, half * 8:half * 8 + 8, :].rearrange("p e s -> p (e s)"),
                                            psum[:, bank, :], gain[:, l % 2, 1, q:q + 1],
                                            sh_of(l, 1)[:, q:q + 1], ALU.mult, ALU.add).then_inc(hE_dve.sem, 1)

                for n in range(1, GATHERED_FIRST, 2):
                    modulate_gathered(n, 4 + (n + 2) % 4)

                def list_extras():
                    f3 = flags.rearrange("p (e g) -> p e g", e=E)
                    link(nc.vector.tensor_scalar(lengths[:, :], lengths[:, :], 1.0 / SLOTS, None, ALU.mult))
                    for k in range(2):
                        nc.vector.memset(run_sums[k][:, 0:LEAD], 0.0)
                    link(nc.vector.tensor_tensor(f3, lengths[:, :].unsqueeze(2).broadcast_to([P, E, GROUPS - 1]),
                                                 count_up[:, 1:GROUPS].unsqueeze(1).broadcast_to([P, E, GROUPS - 1]),
                                                 ALU.is_gt))
                    link(nc.vector.tensor_copy(run_sums[0][:, LEAD:], flags))
                    a, b, shift = run_sums[0], run_sums[1], 1
                    while shift < NF:
                        link(nc.vector.tensor_tensor(b[:, LEAD:], a[:, LEAD:], a[:, LEAD - shift:LEAD - shift + NF],
                                                     ALU.add))
                        a, b, shift = b, a, 2 * shift
                    full = [P, EXTRAS, E, GROUPS - 1]
                    m = match.rearrange("p k e g -> p k (e g)")
                    link(nc.vector.tensor_tensor(m, a[:, LEAD:].unsqueeze(1).broadcast_to([P, EXTRAS, NF]),
                                                 count_up[:, 1:EXTRAS + 1].unsqueeze(2).broadcast_to([P, EXTRAS, NF]),
                                                 ALU.is_equal))
                    link(nc.vector.tensor_tensor(m, m, flags.unsqueeze(1).broadcast_to([P, EXTRAS, NF]), ALU.mult))
                    nc.vector.tensor_reduce(is_expert, match, AX.X, ALU.add)
                    link(nc.vector.tensor_reduce(is_group, match.rearrange("p k e g -> p k g e"), AX.X, ALU.add))
                    nc.vector.tensor_tensor(is_group, is_group,
                                            count_up[:, 1:GROUPS].unsqueeze(1).broadcast_to([P, EXTRAS, GROUPS - 1]),
                                            ALU.mult)
                    link(nc.vector.tensor_tensor(scratch_e, is_expert,
                                                 count_up[:, 0:E].unsqueeze(1).broadcast_to([P, EXTRAS, E]), ALU.mult))
                    nc.vector.tensor_reduce(group_of, is_group, AX.X, ALU.add)
                    link(nc.vector.tensor_reduce(expert_f, scratch_e, AX.X, ALU.add))
                    nc.vector.tensor_copy(extra_expert[:, :], expert_f)
                    for src, dst in ((slot_of, slot_x), (combine, combine_x)):
                        for t in range(T):
                            link(nc.vector.tensor_tensor(scratch_e, is_expert,
                                                         src[:, t, :].unsqueeze(1).broadcast_to([P, EXTRAS, E]),
                                                         ALU.mult))
                            link(nc.vector.tensor_reduce(dst[:, t, :], scratch_e, AX.X, ALU.add))
                    link(nc.vector.tensor_scalar(group_of, group_of, float(-SLOTS), None, ALU.mult))
                    link(nc.vector.tensor_tensor(slot_x[:, :, :], slot_x[:, :, :],
                                                 group_of.unsqueeze(1).broadcast_to([P, T, EXTRAS]), ALU.add))
                    n_listed = a[:, LEAD + NF - 1:LEAD + NF]
                    nc.vector.tensor_copy(passes_before[:, :], passes_f[:, 0:1])
                    link(nc.vector.tensor_scalar(passes_f[:, 2:], count_up[:, 2:EXTRAS:2], n_listed, None, ALU.is_lt))
                    link(nc.vector.tensor_reduce(passes_f[:, 1:2], passes_f[:, 2:], AX.X, ALU.add))
                    link(nc.vector.tensor_tensor(passes_f[:, 0:1], passes_f[:, 0:1], passes_f[:, 1:2], ALU.add))
                    nc.vector.tensor_copy(n_extras[:, :], n_listed) \
                        .then_inc(extras_ready.sem, 1)

                for i in range(STEPS + 1):
                    if i == 4:
                        list_extras()
                        for t in range(T):
                            for k in range(2):
                                ins = nc.vector.tensor_scalar(onehot_x[:, t, k, :], slot_id[:, :],
                                                              slot_x[:, t, k:k + 1], None, ALU.is_equal)
                        ins.then_inc(first_onehot.sem, 1)
                        ve.wait_ge(*first_onehot(l))
                        for t in range(T):
                            for k in range(2):
                                ins = nc.vector.tensor_scalar(weighted_x[:, t, k, :], onehot_x[:, t, k, :].bitcast(F32),
                                                              combine_x[:, t, k:k + 1], None, ALU.mult)
                        ins.then_inc(first_weighted.sem, 1)
                    if i == 8:
                        ve.wait_ge(*first_weights(l))
                        nc.vector.tensor_scalar(combT[:, 0, :], combT_weighted_x, 0.0, None, ALU.is_gt) \
                            .then_inc(first_combT.sem, 1)
                    if i < STEPS:
                        ve.wait_ge(*tanh_ready(l, i + 1))
                        a = e_act[:, i % 2, :]
                        link(nc.vector.scalar_tensor_tensor(out=a, in0=e_tanh[:, i % 2, :], scalar=1.0,
                                                            in1=psum[:, 4 + i % 2, 0:F], op0=ALU.add, op1=ALU.mult))
                        nc.vector.scalar_tensor_tensor(out=a, in0=a, scalar=0.5, in1=psum[:, 4 + i % 2, F:2 * F],
                                                       op0=ALU.mult, op1=ALU.mult).then_inc(act_ready.sem, 1)
                    if i == 0:
                        for b in range(4):
                            ve.wait_ge(*weights_read(l, b + 1))
                            nc.vector.tensor_scalar(combT[:, 2 * b:2 * b + 2, :], combT_weighted[:, 2 * b:2 * b + 2, :],
                                                    0.0, None, ALU.is_gt).then_inc(combT_ready.sem, 1)
                    if 1 <= i < 4:
                        modulate_gathered(GATHERED_FIRST + 2 * i - 1, 7)
                    if i >= 1:
                        if i == 1:
                            ve.wait_ge(*combT_ready(l, 4))
                            ve.wait_ge(*gate_ready(l, 2))
                        for half in range(2):
                            n = 2 * i - 1 + half
                            at = slice(half * BANK, (half + 1) * BANK)
                            ve.wait_ge(*down_psum(l, n))
                            nc.vector.scalar_tensor_tensor(out=y[:, at], in0=psum[:, 7 - half, :],
                                                           scalar=slot_weight[:, i - 1:i], in1=gate_rows[:, 1, at],
                                                           op0=ALU.mult, op1=ALU.mult).then_inc(y_read.sem, 1)
                            ve.wait_ge(*y_read(l, n))
                            if i >= 2:
                                ve.wait_ge(*y_high_ready(l, n - 2))
                            nc.vector.tensor_scalar(y_masked[:, at].bitcast(I32), y[:, at].bitcast(I32), HIGH_BITS,
                                                    None, ALU.bitwise_and).then_inc(y_masked_ready.sem, 1)
                            ve.wait_ge(*y_masked_ready(l, n))
                            if i >= 2:
                                ve.wait_ge(*added_psum(l, i - 1))
                            nc.vector.tensor_tensor(y_low[:, at], y[:, at], y_masked[:, at], ALU.subtract) \
                                .then_inc(y_low_ready.sem, 1)

                ve.wait_ge(*extras_ready(l))
                listed = ve.value_load(n_extras[0:1, 0:1], min_val=0, max_val=EXTRAS)
                before = ve.value_load(passes_before[0:1, 0:1], min_val=0, max_val=L * ITERS)
                with ve.If(listed > 2):
                    with ve.Fori(0, ITERS) as j:
                        with ve.If(listed > 2 * j + 2):
                            for t in range(T):
                                for k in range(2):
                                    ins = nc.vector.tensor_scalar(onehot_x[:, t, k, :], slot_id[:, :],
                                                                  slot_x[:, t, bass.ds(2 * j + (k + 2), 1)], None, ALU.is_equal)
                            ins.then_inc(x_onehot.sem, 1)
                            ve.wait_ge(x_onehot.sem, j + before + 1)
                            for t in range(T):
                                for k in range(2):
                                    ins = nc.vector.tensor_scalar(weighted_x[:, t, k, :], onehot_x[:, t, k, :].bitcast(F32),
                                                                  combine_x[:, t, bass.ds(2 * j + (k + 2), 1)], None, ALU.mult)
                            ins.then_inc(x_weighted.sem, 1)
                            ve.wait_ge(x_gathered.sem, j + before + 1)
                            for q in range(1, C, 2):
                                ins = nc.vector.tensor_scalar(hE[:, q, 0:2, :].rearrange("p e s -> p (e s)"),
                                                              psum[:, 4 + q % 2, (q // 2) * P:(q // 2 + 1) * P],
                                                              gain[:, l % 2, 1, q:q + 1], sh_of(l, 1)[:, q:q + 1],
                                                              ALU.mult, ALU.add)
                            ins.then_inc(x_tokens_dve.sem, 1)
                            ve.wait_ge(x_weights.sem, j + before + 1)
                            nc.vector.tensor_scalar(combT[:, 0, :], combT_weighted_x, 0.0, None, ALU.is_gt) \
                                .then_inc(x_combT.sem, 1)
                            ve.wait_ge(x_tanh.sem, j + before + 1)
                            nc.vector.scalar_tensor_tensor(out=e_act[:, 0, :], in0=e_tanh[:, 0, :], scalar=1.0,
                                                           in1=psum[:, 7, 0:F], op0=ALU.add, op1=ALU.mult) \
                                .then_inc(x_act1.sem, 1)
                            ve.wait_ge(x_act1.sem, j + before + 1)
                            nc.vector.scalar_tensor_tensor(out=e_act[:, 0, :], in0=e_act[:, 0, :], scalar=0.5,
                                                           in1=psum[:, 7, F:2 * F], op0=ALU.mult, op1=ALU.mult) \
                                .then_inc(x_act.sem, 1)
                            ve.wait_ge(x_down.sem, j + before + 1)
                            ve.wait_ge(x_weights.sem, j + before + 1)
                            for half in range(2):
                                at = slice(half * BANK, (half + 1) * BANK)
                                ins = nc.vector.scalar_tensor_tensor(out=y[:, at], in0=psum[:, 4 + half, :],
                                                                     scalar=slot_weight[:, PAIRS:],
                                                                     in1=gate_rows[:, 1, at], op0=ALU.mult, op1=ALU.mult)
                            ins.then_inc(x_y.sem, 1)
                            ve.wait_ge(x_y.sem, j + before + 1)
                            nc.vector.tensor_scalar(y_masked.bitcast(I32), y.bitcast(I32), HIGH_BITS, None,
                                                    ALU.bitwise_and).then_inc(x_y_masked.sem, 1)
                            ve.wait_ge(x_y_masked.sem, j + before + 1)
                            nc.vector.tensor_tensor(y_low[:, :], y, y_masked, ALU.subtract).then_inc(x_y_low.sem, 1)

                ve.wait_ge(*moe_psum(l))
                for t in range(T):
                    ins = nc.vector.tensor_tensor(x_sb[:, t, :], x_sb[:, t, :],
                                                  psum[:, 2 * t:2 * t + 2, :].rearrange("p b n -> p (b n)"), ALU.add)
                    ins.then_inc(moe_added.sem, 1)

        @block.tensor
        def _(pe):
            def turn(dst, src):
                return nc.tensor.transpose(dst, src, ident[0:src.shape[0], 0:src.shape[0]])

            def ada_products(s, bank):
                for i in range(4):
                    pe.wait_ge(*loaded(("ada", s, i)))
                    w = slot(("ada", s, i), 2)
                    for k in range(2):
                        q = 2 * i + k
                        for j in range(4):
                            ins = nc.tensor.matmul(psum[32 * j:32 * j + 32, bank, :], c_act[:, q, :],
                                                   w[:, k, j * BANK:(j + 1) * BANK], start=q == 0, stop=q == C - 1)
                    ins.then_inc(ada_products_done.sem, 1)

            def ada_reduce(s, bank):
                pe.wait_ge(*ada_scaled(s // 3, 4 * (s % 3)))
                for j in range(4):
                    ins = nc.tensor.matmul(psum[32 * j:32 * j + 32, bank, :], ones_f[:, :],
                                           ada_acc[:, j * BANK:(j + 1) * BANK], start=True, stop=True)
                ins.then_inc(ada_in_psum.sem, 1)

            def ada_turn(s, bank):
                pe.wait_ge(*ada_row_ready(0, s + 1))
                for b in range(4):
                    ins = turn(psum[:, bank, b * P:(b + 1) * P], ada_row[:, b * P:(b + 1) * P])
                ins.then_inc(ada_turned.sem, 1)

            def turn_x(l, which):
                for t in range(T):
                    pe.wait_ge(*xn_ready(l, which * T + t + 1))
                    for b in range(4):
                        for k in range(2):
                            q = 2 * b + k
                            ins = turn(psum[:, 3 + b, k * S + t * P:k * S + (t + 1) * P], xn[:, t, q * P:(q + 1) * P])
                        if t == T - 1:
                            ins.then_inc(xnT_ready.sem, 1)

            HT_ORDER = (0, 1, 4, 5, 2, 3, 6, 7)

            def hT_wait(l, which, n):
                if n % 2 == 0:
                    pe.wait_ge(*(hT_act if n % 4 == 0 else hT_dve)(l, 2 * which + n // 4 + 1))

            def unit(l, n, w, src, k, a, blocks=range(2)):
                b = n % 2
                if n >= 2:
                    pe.wait_ge(*bank_emptied(l, n))
                for m in blocks:
                    for q in range(k):
                        ins = nc.tensor.matmul(psum[:, b, m * S:(m + 1) * S], w[:, q, a + m * P:a + (m + 1) * P],
                                               src[:, q, :], start=q == 0, stop=q == k - 1)
                if m == 1:
                    ins.then_inc(unit_psum.sem, 1)

            def bank_emptied(l, n):
                p = n - 2
                if p in (0, 2):
                    return cc_ready(l, p // 2 + 1)
                if p in (1, 3):
                    return u_ready(l, p // 2 + 1)
                if p in (4, 5):
                    return conv_ready(l, p - 3)
                if p < 10:
                    return ya_ready(l, p - 5)
                if p < 14:
                    return ga_tanh(l, p - 9)
                if p < 18:
                    return gb_tanh(l, p - 13)
                return yb_gated(l, p - 17)

            pe.wait_ge(*consts(0, 7))
            pe.wait_ge(c_loaded.sem, 16)
            turn(psum[:, 5, 0:C], c_rows).then_inc(c_psum.sem, 1)
            pe.wait_ge(*c_ready(0))
            ada_products(0, 7)
            pe.wait_ge(params_loaded.sem, 16 * (5 + T))
            turn(psum[:, 6, 0:NROWS], rows[0:NROWS, :]).then_inc(cols_psum.sem, 1)
            ada_turn(0, 7)

            for l in range(L):
                turn_x(l, 0)

                pe.wait_ge(*loaded(("lat", l)))
                w = slot(("lat", l), C)
                for t in range(T):
                    for n, q in enumerate(HT_ORDER):
                        if t == 0:
                            hT_wait(l, 0, n)
                        ins = nc.tensor.matmul(psum[:, 2 + t, 0:LAT], hT[:, q, t * P:(t + 1) * P], w[:, q, 0:LAT],
                                               start=n == 0, stop=n == C - 1)
                    ins.then_inc(lat_psum.sem, 1)

                def conv_unit(n, key, a):
                    pe.wait_ge(*loaded((key, l)))
                    unit(l, n, slot((key, l), C), hT, C, a)

                conv_unit(0, "cc", 0)
                conv_unit(1, "cx", 0)
                for t in range(T):
                    pe.wait_ge(*lat_ready(l, t + 1))
                    for b in range(QB + 1):
                        ins = turn(psum[:, 4 + t, b * P:(b + 1) * P], lat_n[:, t, b * P:(b + 1) * P])
                    ins.then_inc(latT_psum.sem, 1)
                conv_unit(2, "cc", S)
                conv_unit(3, "cx", S)

                def up_q(t, bank):
                    for a, n in ((0, BANK), (BANK, NH * DH - BANK)):
                        for q in range(QB):
                            ins = nc.tensor.matmul(psum[:, bank + a // BANK, 0:n], latT[:, q, t * P:(t + 1) * P],
                                                   uq_sb[:, q, a:a + n], start=q == 0, stop=q == QB - 1)
                    ins.then_inc(up_psum.sem, 1)

                def up_kv(t, bank):
                    for a in range(2):
                        ins = nc.tensor.matmul(psum[:, bank + a, :], latT[:, QB, t * P:(t + 1) * P],
                                               ukv_sb[:, a * BANK:(a + 1) * BANK], start=True, stop=True)
                    ins.then_inc(up_psum.sem, 1)

                pe.wait_ge(*latT_ready(l, T))
                pe.wait_ge(latw_loaded.sem, 32 * (l + 1))
                up_q(0, 2)
                up_kv(0, 4)
                up_q(1, 6)
                conv_unit(4, "cb", 0)
                pe.wait_ge(*qkv_copied(l, 1))
                up_kv(1, 2)
                conv_unit(5, "cb", S)

                pe.wait_ge(*loaded(("conv", l)))
                pe.wait_ge(*conv_ready(l, 2))
                for j in range(4):
                    unit(l, 6 + j, slot(("conv", l), NB), yc, NB, j * S)

                def gate_unit(n, blocks=range(2)):
                    key = ("ga%d" if n < 14 else "gb%d") % ((n - 10) % 4 // 2)
                    pe.wait_ge(*loaded((key, l)))
                    unit(l, n, slot((key, l), C), hT, C, (n % 2) * S, blocks)

                def turn_qk(h):
                    if h:
                        pe.wait_ge(*qkT_ready(l, h))
                    for a in range(2):
                        for t in range(T):
                            ins = turn(psum[0:DH, 2, a * S + t * P:a * S + (t + 1) * P], qk[:, t, a, h, :])
                    ins.then_inc(qkT_psum.sem, 1)

                def turn_probs(h):
                    pe.wait_ge(*probs_ready(l, h + 1))
                    if h:
                        pe.wait_ge(*pT_ready(l, h))
                    for k in range(T):
                        for t in range(T):
                            ins = turn(psum[:, 6, k * S + t * P:k * S + (t + 1) * P],
                                       probs[:, h % 2, t, k * P:(k + 1) * P])
                    ins.then_inc(pT_psum.sem, 1)

                def apply_probs(h):
                    pe.wait_ge(*pT_ready(l, h + 1))
                    if h >= 2 and h % 2 == 0:
                        pe.wait_ge(*oT_ready(l, h // 2))
                    a = (h % 2) * VD
                    for k in range(T):
                        ins = nc.tensor.matmul(psum[a:a + VD, 7, 0:S], v_sb[:, k, h, :], probsT[:, h % 2, k, :],
                                               start=k == 0, stop=k == T - 1)
                    ins.then_inc(pv_psum.sem, 1)

                gate_unit(10)
                pe.wait_ge(*qk_ready(l, T))
                pe.wait_ge(*qkv_copied(l, 4))
                turn_qk(0)
                for h in range(NH):
                    if h + 1 < NH:
                        turn_qk(h + 1)
                    pe.wait_ge(*qkT_ready(l, h + 1))
                    if h >= 2:
                        pe.wait_ge(*exp_done(l, h - 1))
                    for t in range(T):
                        ins = nc.tensor.matmul(psum[:, 4 + h % 2, t * S:(t + 1) * S],
                                               qkT[0:DH, h % 2, 0, t * P:(t + 1) * P], qkT[0:DH, h % 2, 1, :],
                                               start=True, stop=True)
                    ins.then_inc(scores_psum.sem, 1)
                    if h < 6:
                        gate_unit(11 + h)
                    else:
                        gate_unit(17, [h - 6])
                    if h == 4:
                        ada_reduce(3 * l + 1, 3)
                    elif h == 5:
                        ada_turn(3 * l + 1, 3)
                    turn_probs(h)
                    if h:
                        apply_probs(h - 1)
                apply_probs(NH - 1)

                pe.wait_ge(*oT_ready(l, NH // 2))
                pe.wait_ge(*loaded(("attn", l)))
                for j in range(4):
                    unit(l, 18 + j, slot(("attn", l), NB), oT, NB, j * S)

                pe.wait_ge(*mod_ready(0, 3 * l + 2))
                for half in range(2):
                    if half:
                        ada_reduce(3 * l + 2, 4)
                    pe.wait_ge(*loaded((f"wo{half}", l)))
                    w = slot((f"wo{half}", l), C)
                    for n, t in enumerate(WO_ORDER[half]):
                        for q in range(C):
                            if half == 0 and n == 0 and q % 2 == 0:
                                pe.wait_ge(*merged_ready(l, q // 2 + 1))
                            ins = nc.tensor.matmul(psum[:, 2 * t + half, :], merged[:, q, t * P:(t + 1) * P], w[:, q, :],
                                                   start=q == 0, stop=q == C - 1)
                        ins.then_inc(mix_psum.sem, 1)
                        if half and n == 0:
                            ada_turn(3 * l + 2, 4)

                if l + 1 < L:
                    ada_products(3 * l + 3, 7)
                pe.wait_ge(*mod_ready(0, 3 * l + 3))
                turn_x(l, 1)
                if l + 1 < L:
                    ada_turn(3 * l + 3, 7)
                if l == 0:
                    pe.wait_ge(*late_loaded(0, 16 * 4))
                for n, q in enumerate(HT_ORDER):
                    hT_wait(l, 1, n)
                    ins = nc.tensor.matmul(psum[0:E, 0, 0:S], router_sb[:, q, :], hT[:, q, :], start=n == 0,
                                           stop=n == C - 1)
                ins.then_inc(router_psum.sem, 1)
                pe.wait_ge(*loaded(("shared", l)))
                w = slot(("shared", l), C)

                def shared_block(m, bank, sig=None):
                    for q in range(C):
                        ins = nc.tensor.matmul(psum[:, bank, (m % FC) * S:(m % FC + 1) * S], w[:, q, m * P:(m + 1) * P],
                                               hT[:, q, :], start=q == 0, stop=q == C - 1)
                    if sig:
                        ins.then_inc(sig.sem, 1)

                shared_block(0, 4)
                pe.wait_ge(*router_copied(l))
                for t in range(T):
                    ins = turn(psum[:, 6, t * E:(t + 1) * E], router_out[0:E, t * P:(t + 1) * P])
                ins.then_inc(routerT_psum.sem, 1)
                shared_block(1, 4, s_gate_psum)
                shared_block(2, 5)
                pe.wait_ge(*chosen(l))
                if l + 1 < L:
                    pe.wait_ge(*mod_ready(0, 3 * l + 4))
                nc.tensor.matmul(psum[:, 7, 0:E], tri[:, :], sel_b[:, 0, :], start=True, stop=True)
                nc.tensor.matmul(psum[:, 7, E:2 * E], ones[:, :], sel_b[:, 0, :], start=True, stop=False)
                nc.tensor.matmul(psum[:, 7, E:2 * E], tri[:, :], sel_b[:, 1, :], start=False, stop=True)
                nc.tensor.matmul(psum[:, 7, 2 * E:3 * E], ones[:, :], sel_b[:, 0, :], start=True, stop=False)
                nc.tensor.matmul(psum[:, 7, 2 * E:3 * E], ones[:, :], sel_b[:, 1, :], start=False, stop=True) \
                    .then_inc(rank_psum.sem, 1)
                shared_block(3, 5, s_up_psum)

                pe.wait_ge(*onehot_ready(l))
                pe.wait_ge(*ranks_read(l))
                pe.wait_ge(*high_ready(l))
                pe.wait_ge(*low_ready(l))
                def gather(n, bank):
                    half, q = divmod(n, C)
                    for t in range(T):
                        for part_x in (x_high, x_low):
                            ins = nc.tensor.matmul(psum[:, bank, :], part_x[:, t, q * P:(q + 1) * P],
                                                   onehot[:, t, half * 8:half * 8 + 8, :]
                                                   .rearrange("p e s -> p (e s)"),
                                                   start=t == 0 and part_x is x_high,
                                                   stop=t == T - 1 and part_x is x_low)
                    ins.then_inc(gather_psum.sem, 1)

                for n in range(GATHERED_FIRST):
                    if n == C // 2:
                        pe.wait_ge(*high_ready(l, 2))
                    if n == 2:
                        pe.wait_ge(*s_act_ready(l))
                    if n >= 4:
                        pe.wait_ge(*(hE_act if n % 2 == 0 else hE_dve)(l, (n - 4) // 2 + 1))
                    gather(n, 4 + (n + 2) % 4)

                def shared_down():
                    pe.wait_ge(*s_act_ready(l))
                    pe.wait_ge(*sdown_gated(l))
                    for t in range(T):
                        for half in range(2):
                            for q in range(FC):
                                ins = nc.tensor.matmul(psum[:, 2 * t + half, :], s_act[:, q, t * P:(t + 1) * P],
                                                       sdown_sb[:, q, half * BANK:(half + 1) * BANK],
                                                       start=q == 0, stop=False)
                    ins.then_inc(s_down_psum.sem, 1)

                def turn_weighted():
                    pe.wait_ge(*weighted_ready(l))
                    for b, bank in enumerate(TURN_BANKS):
                        if b == 3:
                            pe.wait_ge(*weights_read(l, 2))
                        for k in range(2):
                            for t in range(T):
                                j = 2 * b + k
                                ins = turn(psum[:, bank, k * S + t * P:k * S + (t + 1) * P],
                                           weighted[:, t, 2 * j:2 * j + 2, :].rearrange("p e s -> p (e s)"))
                        ins.then_inc(combT_psum.sem, 1)


                def gate_up(i):
                    if i == 4:
                        pe.wait_ge(*hE_act(l, C))
                        pe.wait_ge(*hE_dve(l, C))
                    if i >= 2:
                        pe.wait_ge(*act_ready(l, i - 1))
                    elif i == 0:
                        pe.wait_ge(*hE_act(l, GATHERED_FIRST // 2))
                        pe.wait_ge(*hE_dve(l, GATHERED_FIRST // 2))
                    else:
                        pe.wait_ge(*weights_read(l, 1))
                    if i == PAIRS:
                        pe.wait_ge(*first_tokens(l, 2))
                    for part_no in range(2):
                        pe.wait_ge(*loaded(("gu", l, i, part_no)))
                        w = ring[:, number["gu", l, i, part_no] % RING, :].rearrange("p (k c n) -> p k c n", k=2, n=BANK)
                        for m in range(C // 2):
                            q = part_no * C // 2 + m
                            for k in range(2):
                                ins = nc.tensor.matmul(psum[k * SLOTS:(k + 1) * SLOTS, 4 + i % 2, :],
                                                       hE[:, q, (2 * i + k) % E, :], w[:, k, m, :], start=q == 0,
                                                       stop=q == C - 1)
                        ins.then_inc(gu_psum.sem, 1)

                def turn_act(i):
                    pe.wait_ge(*act_ready(l, i + 1))
                    if i:
                        pe.wait_ge(*y_read(l, 2 * i))
                    if i < 3:
                        pe.wait_ge(*hE_act(l, GATHERED_FIRST // 2 + i + 1))
                    for q in range(FC):
                        ins = turn(psum[:, 6, q * P:(q + 1) * P], e_act[:, i % 2, q * P:(q + 1) * P])
                    ins.then_inc(aT_psum.sem, 1)

                def down(i):
                    pe.wait_ge(*loaded(("down", l, i)))
                    pe.wait_ge(*aT_ready(l, i + 1))
                    w = slot(("down", l, i), 2 * FC)
                    if i:
                        pe.wait_ge(*y_read(l, 2 * i))
                    if i < 3:
                        pe.wait_ge(*hE_dve(l, GATHERED_FIRST // 2 + i + 1))
                    if i in (4, 5):
                        pe.wait_ge(*first_tokens(l, i - 3))
                    elif i == 6:
                        pe.wait_ge(*first_weights(l))
                    for half in range(2):
                        for q in range(FC):
                            for k in range(2):
                                ins = nc.tensor.matmul(psum[k * SLOTS:(k + 1) * SLOTS, 7 - half, :],
                                                       aT[:, q, k * SLOTS:(k + 1) * SLOTS],
                                                       w[:, k * FC + q, half * BANK:(half + 1) * BANK],
                                                       start=q == 0, stop=q == FC - 1)
                        ins.then_inc(down_psum.sem, 1)

                def add_tokens(i):
                    pe.wait_ge(*combT_ready(l, 4))
                    if i == PAIRS:
                        pe.wait_ge(*first_combT(l))
                    for half in range(2):
                        pe.wait_ge(*y_high_ready(l, 2 * i + half + 1))
                        pe.wait_ge(*y_low_ready(l, 2 * i + half + 1))
                        for t in range(T):
                            for part_y in (y_high, y_low):
                                ins = nc.tensor.matmul(psum[:, 2 * t + half, :],
                                                       combT[:, i % PAIRS, t * P:(t + 1) * P],
                                                       part_y[:, half * BANK:(half + 1) * BANK], start=False,
                                                       stop=i == STEPS - 1 and part_y is y_low)
                    ins.then_inc(added_psum.sem, 1)

                def first_extras(i):
                    pe.wait_ge(*y_read(l, 2 * i - 2))
                    if i < 7:
                        pe.wait_ge(*first_onehot(l))
                        for m in range(C // 2):
                            q = (i - 5) * C // 2 + m
                            for t in range(T):
                                for part_x in (x_high, x_low):
                                    ins = nc.tensor.matmul(psum[:, 7, m * P:(m + 1) * P],
                                                           part_x[:, t, q * P:(q + 1) * P],
                                                           onehot_x[:, t].rearrange("p e s -> p (e s)"),
                                                           start=t == 0 and part_x is x_high,
                                                           stop=t == T - 1 and part_x is x_low)
                        ins.then_inc(first_gathered.sem, 1)
                    else:
                        pe.wait_ge(*first_weighted(l))
                        for t in range(T):
                            ins = turn(psum[:, 7, t * P:(t + 1) * P], weighted_x[:, t].rearrange("p e s -> p (e s)"))
                        ins.then_inc(first_turned.sem, 1)

                for i in range(STEPS + 2):
                    if i < STEPS:
                        gate_up(i)
                    if i == 0:
                        turn_weighted()
                    if 1 <= i < 4:
                        if i == 1:
                            pe.wait_ge(*weights_read(l, 4))
                        else:
                            pe.wait_ge(*y_read(l, 2 * i - 2))
                        gather(GATHERED_FIRST + 2 * i - 2, 6)
                        gather(GATHERED_FIRST + 2 * i - 1, 7)
                    if i == 1:
                        shared_down()
                    if 1 <= i <= STEPS:
                        turn_act(i - 1)
                    if i >= 2:
                        add_tokens(i - 2)
                    if i in (5, 6, 7):
                        first_extras(i)
                    if i == STEPS - 1:
                        pe.wait_ge(*extras_ready(l))
                        listed = pe.value_load(n_extras[0:1, 0:1], min_val=0, max_val=EXTRAS)
                        before = pe.value_load(passes_before[0:1, 0:1], min_val=0, max_val=L * ITERS)
                    if 1 <= i <= STEPS:
                        down(i - 1)

                first = number["down", l, PAIRS] - 2
                with pe.If(listed > 2):
                    with pe.Fori(0, ITERS) as j:
                        with pe.If(listed > 2 * j + 2):
                            pe.wait_ge(x_onehot.sem, j + before + 1)
                            for q in range(C):
                                for t in range(T):
                                    for part_x in (x_high, x_low):
                                        ins = nc.tensor.matmul(psum[:, 4 + q % 2, (q // 2) * P:(q // 2 + 1) * P],
                                                               part_x[:, t, q * P:(q + 1) * P],
                                                               onehot_x[:, t].rearrange("p e s -> p (e s)"),
                                                               start=t == 0 and part_x is x_high,
                                                               stop=t == T - 1 and part_x is x_low)
                            ins.then_inc(x_gathered.sem, 1)
                            pe.wait_ge(x_weighted.sem, j + before + 1)
                            for t in range(T):
                                ins = turn(psum[:, 6, t * P:(t + 1) * P], weighted_x[:, t].rearrange("p e s -> p (e s)"))
                            ins.then_inc(x_turned.sem, 1)
                            pe.wait_ge(x_tokens_act.sem, j + before + 1)
                            pe.wait_ge(x_tokens_dve.sem, j + before + 1)
                            pe.wait_ge(x_loaded_w.sem, j * F_LOADED + before * F_LOADED + F_LOADED)
                            for q in range(C):
                                for k in range(2):
                                    w = ring[:, (first + k) % RING, :].rearrange("p (c n) -> p c n", c=C)
                                    ins = nc.tensor.matmul(psum[k * SLOTS:(k + 1) * SLOTS, 7, :], hE[:, q, k, :],
                                                           w[:, q, :], start=q == 0, stop=q == C - 1)
                            ins.then_inc(x_gu.sem, 1)
                            pe.wait_ge(x_act.sem, j + before + 1)
                            for q in range(FC):
                                ins = turn(psum[:, 6, q * P:(q + 1) * P], e_act[:, 0, q * P:(q + 1) * P])
                            ins.then_inc(x_aT_psum.sem, 1)
                            pe.wait_ge(x_aT.sem, j + before + 1)
                            w = ring[:, (first + 2) % RING, :].rearrange("p (k n) -> p k n", k=2 * FC)
                            for half in range(2):
                                for q in range(FC):
                                    for k in range(2):
                                        ins = nc.tensor.matmul(psum[k * SLOTS:(k + 1) * SLOTS, 4 + half, :],
                                                               aT[:, q, k * SLOTS:(k + 1) * SLOTS],
                                                               w[:, k * FC + q, half * BANK:(half + 1) * BANK],
                                                               start=q == 0, stop=q == FC - 1)
                            ins.then_inc(x_down.sem, 1)
                            pe.wait_ge(x_combT.sem, j + before + 1)
                            pe.wait_ge(x_y_high.sem, j + before + 1)
                            pe.wait_ge(x_y_low.sem, j + before + 1)
                            for t in range(T):
                                for half in range(2):
                                    for part_y in (y_high, y_low):
                                        ins = nc.tensor.matmul(psum[:, 2 * t + half, :], combT[:, 0, t * P:(t + 1) * P],
                                                               part_y[:, half * BANK:(half + 1) * BANK], start=False,
                                                               stop=True, skip_group_check=True)
                            ins.then_inc(x_free.sem, 1)
                turn(psum[:, 4, 0:P], ident[:, :]).then_inc(moe_psum.sem, 1)


_INS = ["x", "c", "positions", "w_ada", "b_ada", "g_mix", "g_ffn", "w_in", "conv_w", "g_q_a", "w_uq", "g_kv_a",
        "w_ukv", "g_qn", "g_kn", "w_conv_out", "w_attn_out", "w_o", "w_router", "b_router", "w_e_gate", "w_e_up",
        "w_e_down", "w_s_gate", "w_s_up", "w_s_down"]


def kernel(**inputs):
    import concourse.bacc as bacc
    from concourse.bass_utils import run_bass_kernel_spmd

    nc = bacc.Bacc("TRN2", target_bir_lowering=False, num_devices=1)
    arrays, args = {}, []
    for name in _INS:
        a = np.ascontiguousarray(inputs[name])
        arrays[f"in_{name}"] = a
        args.append(nc.dram_tensor(f"in_{name}", a.shape, mybir.dt.from_np(a.dtype), kind="ExternalInput").ap())
    shape = arrays["in_x"].shape
    args.append(nc.dram_tensor("out_0", shape, F32, kind="ExternalOutput").ap())
    trunk(nc, *args)
    r = run_bass_kernel_spmd(nc, [arrays], core_ids=[0])
    return r.results[0]["out_0"]
```
